# Optimizing a Trainium2 kernel written in Bass

```python
import math
import jax, jax.numpy as jnp
from jax import lax
import numpy as np

D_MODEL = 1024
BATCH = 1
SEQ = 256
DEPTH = 1

RWKV_HEADS = 8
RWKV_HEAD_DIM = 64
RWKV_WIDTH = RWKV_HEADS * RWKV_HEAD_DIM
DECAY_LORA = 64
ICLR_LORA = 64
GN_EPS = 64e-5
ATT_HEADS = 8
ATT_HEAD_DIM = 64
ATT_WIDTH = ATT_HEADS * ATT_HEAD_DIM
KV_LATENT = 128
IDX_HEADS = 8
IDX_HEAD_DIM = 64
TOPK_MAX = 256
Q_BLOCK = 128
NUM_BUCKETS = 32
MAX_DISTANCE = 128
NORM_EPS = 1e-6
COL_SIZES = (RWKV_WIDTH, RWKV_WIDTH, RWKV_WIDTH, DECAY_LORA, ICLR_LORA, RWKV_WIDTH,
             ATT_WIDTH, KV_LATENT, ATT_WIDTH, IDX_HEADS * IDX_HEAD_DIM, IDX_HEAD_DIM, IDX_HEADS,
             D_MODEL, D_MODEL)
N_SHIFT = 3 * RWKV_WIDTH + DECAY_LORA + ICLR_LORA
N_IN = sum(COL_SIZES)


def rms_norm(x, g):
    xf = x.astype(jnp.float32)
    y = xf * lax.rsqrt(jnp.mean(xf * xf, axis=-1, keepdims=True) + NORM_EPS)
    return (y * g.astype(jnp.float32)).astype(x.dtype)

def token_shift(u):
    return jnp.pad(u, ((0, 0), (1, 0), (0, 0)))[:, :-1]

def t5_bucket(dist):
    max_exact = NUM_BUCKETS // 2
    is_small = dist < max_exact
    d = jnp.maximum(dist, 1).astype(jnp.float32)
    large = max_exact + (jnp.log(d / max_exact) / math.log(MAX_DISTANCE / max_exact)
                         * (NUM_BUCKETS - max_exact)).astype(jnp.int32)
    large = jnp.minimum(large, NUM_BUCKETS - 1)
    return jnp.where(is_small, dist, large)

def rwkv7_scan(r, w, k, v, a_vec, b_vec):
    B, S, H, N = r.shape

    def step(state, inp):
        r_t, w_t, k_t, v_t, a_t, b_t = inp
        sa = jnp.einsum('bhvk,bhk->bhv', state, a_t)
        state = (state * w_t[:, :, None, :] + sa[..., None] * b_t[:, :, None, :]
                 + v_t[..., None] * k_t[:, :, None, :])
        y_t = jnp.einsum('bhvk,bhk->bhv', state, r_t)
        return state, y_t

    xs = tuple(jnp.moveaxis(t, 1, 0) for t in (r, w, k, v, a_vec, b_vec))
    s0 = jnp.zeros((B, H, N, N), jnp.float32)
    _, y = lax.scan(step, s0, xs)
    return jnp.moveaxis(y, 0, 1)

def rwkv7_branch(pr, pk, pv, pwd, pad_, w0, w2, a0, a2, k_k, k_a, r_k, lnx_g, lnx_b):
    B, S, _ = pr.shape
    f32 = jnp.float32
    heads = lambda t: t.astype(f32).reshape(B, S, RWKV_HEADS, RWKV_HEAD_DIM)
    w_log = -jax.nn.softplus(-(w0 + jnp.tanh(pwd) @ w2).astype(f32)) - 0.5
    decay = jnp.exp(-jnp.exp(w_log))
    a = jax.nn.sigmoid((a0 + pad_ @ a2).astype(f32))
    kk = heads(pk * k_k)
    kk = kk / jnp.maximum(jnp.sqrt(jnp.sum(kk * kk, axis=-1, keepdims=True)), 1e-12)
    k = pk.astype(f32) * (1.0 + (a - 1.0) * k_a)
    r_h, k_h, v_h, a_h, w_h = heads(pr), heads(k), heads(pv), heads(a), heads(decay)
    y = rwkv7_scan(r_h, w_h, k_h, v_h, -kk, kk * a_h)
    mu = jnp.mean(y, axis=-1, keepdims=True)
    var = jnp.mean(jnp.square(y - mu), axis=-1, keepdims=True)
    yn = ((y - mu) * lax.rsqrt(var + GN_EPS)).reshape(B, S, RWKV_WIDTH) * lnx_g + lnx_b
    bonus = jnp.sum(r_h * k_h * r_k.astype(f32), axis=-1, keepdims=True) * v_h
    out = yn + bonus.reshape(B, S, RWKV_WIDTH)
    return out.astype(pr.dtype)

def dsa_branch(q, ckv, qi, ki, wi, kv_norm_g, w_uk, w_uv, rel_bias):
    B, S, _ = q.shape
    topk = min(TOPK_MAX, S // 4)
    nb = S // Q_BLOCK
    q = q.reshape(B, S, ATT_HEADS, ATT_HEAD_DIM)
    lat = rms_norm(ckv, kv_norm_g)
    q_abs = jnp.einsum('bshd,chd->bshc', q, w_uk) * (ATT_HEAD_DIM ** -0.5)
    qi = qi.reshape(B, S, IDX_HEADS, IDX_HEAD_DIM)
    key_pos = jnp.arange(S, dtype=jnp.int32)
    qpos = key_pos.reshape(nb, Q_BLOCK)
    b_idx = jnp.arange(B)[:, None, None]

    def blocks(t):
        return jnp.moveaxis(t.reshape((B, nb, Q_BLOCK) + t.shape[2:]), 1, 0)

    def one_block(args):
        qa_b, qi_b, wi_b, pos_b = args
        s_idx = jax.nn.relu(jnp.einsum('bqhd,bsd->bqhs', qi_b, ki))
        score = jnp.einsum('bqh,bqhs->bqs', wi_b, s_idx).astype(jnp.float32)
        causal = key_pos[None, :] <= pos_b[:, None]
        score = jnp.where(causal[None], score, -jnp.inf)
        _, sel = lax.top_k(score, topk)
        lat_sel = lat[b_idx, sel]
        dist = pos_b[None, :, None] - sel
        valid = dist >= 0
        bias = rel_bias[t5_bucket(jnp.maximum(dist, 0))]
        logits = (jnp.einsum('bqhc,bqkc->bqhk', qa_b, lat_sel).astype(jnp.float32)
                  + jnp.moveaxis(bias, -1, 2).astype(jnp.float32))
        logits = jnp.where(valid[:, :, None, :], logits, -jnp.inf)
        p = jax.nn.softmax(logits, axis=-1)
        return jnp.einsum('bqhk,bqkc->bqhc', p.astype(lat_sel.dtype), lat_sel)

    o_lat = lax.map(one_block, (blocks(q_abs), blocks(qi), blocks(wi), qpos))
    o_lat = jnp.moveaxis(o_lat, 0, 1).reshape(B, S, ATT_HEADS, KV_LATENT)
    o = jnp.einsum('bshc,chd->bshd', o_lat, w_uv)
    return o.reshape(B, S, ATT_WIDTH)

def first_inputs(seed: int = 0) -> dict:
    key = jax.random.key(seed)
    ks = jax.random.split(key, 24)
    f32 = jnp.float32

    def nrm(k, shape, s):
        return jax.random.normal(k, shape, f32) * s

    return {
        "x": nrm(ks[0], (BATCH, SEQ, D_MODEL), 1.0),
        "c": nrm(ks[1], (BATCH, D_MODEL), 1.0),
        "ada_w": nrm(ks[2], (DEPTH, D_MODEL, 3 * D_MODEL), 0.5 * D_MODEL ** -0.5),
        "ada_b": nrm(ks[3], (DEPTH, 3 * D_MODEL), 0.02),
        "norm_g": 1.0 + nrm(ks[4], (DEPTH, D_MODEL), 0.05),
        "w_in": nrm(ks[5], (DEPTH, D_MODEL, N_IN), D_MODEL ** -0.5),
        "shift_mu": jax.random.uniform(ks[6], (DEPTH, N_SHIFT), f32),
        "w0": jax.random.uniform(ks[7], (DEPTH, RWKV_WIDTH), f32, -6.0, -1.0),
        "w2": nrm(ks[8], (DEPTH, DECAY_LORA, RWKV_WIDTH), 0.1),
        "a0": nrm(ks[9], (DEPTH, RWKV_WIDTH), 0.5),
        "a2": nrm(ks[10], (DEPTH, ICLR_LORA, RWKV_WIDTH), 0.1),
        "k_k": 0.85 + nrm(ks[11], (DEPTH, RWKV_WIDTH), 0.05),
        "k_a": 1.0 + nrm(ks[12], (DEPTH, RWKV_WIDTH), 0.05),
        "r_k": nrm(ks[13], (DEPTH, RWKV_HEADS, RWKV_HEAD_DIM), 0.1),
        "lnx_g": 1.0 + nrm(ks[14], (DEPTH, RWKV_WIDTH), 0.05),
        "lnx_b": nrm(ks[15], (DEPTH, RWKV_WIDTH), 0.02),
        "kv_norm_g": 1.0 + nrm(ks[16], (DEPTH, KV_LATENT), 0.05),
        "w_uk": nrm(ks[17], (DEPTH, KV_LATENT, ATT_HEADS, ATT_HEAD_DIM), KV_LATENT ** -0.5),
        "w_uv": nrm(ks[18], (DEPTH, KV_LATENT, ATT_HEADS, ATT_HEAD_DIM), KV_LATENT ** -0.5),
        "w_pa": nrm(ks[19], (DEPTH, RWKV_WIDTH, D_MODEL), RWKV_WIDTH ** -0.5),
        "w_pb": nrm(ks[20], (DEPTH, ATT_WIDTH, D_MODEL), ATT_WIDTH ** -0.5),
        "w_o": nrm(ks[21], (DEPTH, D_MODEL, D_MODEL), D_MODEL ** -0.5),
        "rel_bias": nrm(ks[22], (NUM_BUCKETS, ATT_HEADS), 0.5),
        "final_g": 1.0 + nrm(ks[23], (D_MODEL,), 0.05),
    }

def first_block(x, c, ada_w, ada_b, norm_g, w_in, shift_mu, w0, w2, a0, a2, k_k, k_a, r_k,
              lnx_g, lnx_b, kv_norm_g, w_uk, w_uv, w_pa, w_pb, w_o, rel_bias, final_g):
    split_at = np.cumsum(np.array(COL_SIZES))[:-1].tolist()
    c_act = jax.nn.silu(c)
    for l in range(DEPTH):
        mod = c_act @ ada_w[l] + ada_b[l]
        shift, scale, gate = jnp.split(mod, 3, axis=-1)
        h = rms_norm(x, norm_g[l]) * (1.0 + scale[:, None, :]) + shift[:, None, :]
        p = h @ w_in[l]
        ps = p[..., :N_SHIFT]
        ps = ps + (token_shift(ps) - ps) * shift_mu[l]
        p = jnp.concatenate([ps, p[..., N_SHIFT:]], axis=-1)
        (pr, pk, pv, pwd, pad_, z_a, q, ckv, z_b, qi, ki, wi, g_a, g_b) = jnp.split(p, split_at, axis=-1)
        y_a = rwkv7_branch(pr, pk, pv, pwd, pad_, w0[l], w2[l], a0[l], a2[l], k_k[l], k_a[l],
                           r_k[l], lnx_g[l], lnx_b[l])
        y_b = dsa_branch(q, ckv, qi, ki, wi, kv_norm_g[l], w_uk[l], w_uv[l], rel_bias)
        br_a = (y_a * jax.nn.silu(z_a)) @ w_pa[l]
        br_b = (y_b * jax.nn.silu(z_b)) @ w_pb[l]
        merged = jax.nn.sigmoid(g_a) * br_a + jax.nn.sigmoid(g_b) * br_b
        x = x + gate[:, None, :] * (merged @ w_o[l])
    return rms_norm(x, final_g)


CHUNK = 64
HG_HEADS = 8
HG_DK = 128
HG_DV = D_MODEL // HG_HEADS
HG_KW = HG_HEADS * HG_DK
HG_VW = HG_HEADS * HG_DV
FOX_HEADS = 8
FOX_DH = 128
FOX_W = FOX_HEADS * FOX_DH
MEM_LEN = 256
MEM_HEADS = 4
MEM_DH = D_MODEL // MEM_HEADS
D_FF = 2816
N_BRANCH = 2
EPS = 1e-6
IN_SPLITS = [HG_KW, HG_KW, HG_VW, HG_VW, FOX_W, FOX_W, FOX_W, FOX_HEADS, N_BRANCH * D_MODEL]
IN_COLS = sum(IN_SPLITS)
IN_OFFSETS = list(np.cumsum(IN_SPLITS)[:-1])


def rmsnorm(x, g):
    x32 = x.astype(jnp.float32)
    y = x32 * lax.rsqrt(jnp.mean(x32 * x32, axis=-1, keepdims=True) + EPS)
    return (y * g.astype(jnp.float32)).astype(x.dtype)

def swiglu(h, w_in, w_down):
    gate, up = jnp.split(h @ w_in, 2, axis=-1)
    return (jax.nn.silu(gate) * up) @ w_down

def hgrn2_chunkwise(q, f_logit, inp, lb):
    B, S = q.shape[0], q.shape[1]
    n = S // CHUNK
    f = lb + (1.0 - lb) * jax.nn.sigmoid(f_logit.astype(jnp.float32))
    logf = jnp.log(f)
    k = 1.0 - f
    q = jax.nn.silu(q.astype(jnp.float32))
    inp = inp.astype(jnp.float32)

    def to_chunks(t):
        return t.reshape(B, n, CHUNK, t.shape[2], t.shape[3]).transpose(1, 0, 3, 2, 4)

    qc, kc, ic = to_chunks(q), to_chunks(k), to_chunks(inp)
    bc = jnp.cumsum(to_chunks(logf), axis=3)
    mask = jnp.tril(jnp.ones((CHUNK, CHUNK), dtype=bool))[:, :, None]

    def step(state, xs):
        qt, kt, it, bt = xs
        diff = bt[:, :, :, None, :] - bt[:, :, None, :, :]
        decay = jnp.exp(jnp.where(mask, diff, -jnp.inf))
        a = jnp.einsum('bhtd,bhsd,bhtsd->bhts', qt, kt, decay)
        o_intra = jnp.einsum('bhts,bhsv->bhtv', a, it)
        o_inter = jnp.einsum('bhtd,bhdv->bhtv', qt * jnp.exp(bt), state)
        b_last = bt[:, :, -1:, :]
        new_state = jnp.exp(b_last[:, :, 0, :])[..., None] * state + jnp.einsum(
            'bhsd,bhsv->bhdv', kt * jnp.exp(b_last - bt), it)
        return new_state, o_intra + o_inter

    s0 = jnp.zeros((B, q.shape[2], HG_DK, HG_DV), jnp.float32)
    _, o = lax.scan(step, s0, (qc, kc, ic, bc))
    return o.transpose(1, 0, 3, 2, 4).reshape(B, S, HG_VW)

def fox_attention(q, k, v, f_logit):
    B, S, H, dh = q.shape
    n_blk = S // Q_BLOCK
    scale = 1.0 / math.sqrt(dh)
    c = jnp.cumsum(jax.nn.log_sigmoid(f_logit.astype(jnp.float32)), axis=1).transpose(0, 2, 1)
    k32 = k.astype(jnp.float32)
    v32 = v.astype(jnp.float32)
    qb = q.astype(jnp.float32).reshape(B, n_blk, Q_BLOCK, H, dh).transpose(1, 0, 3, 2, 4)
    cb = c.reshape(B, H, n_blk, Q_BLOCK).transpose(2, 0, 1, 3)
    kpos = jnp.arange(S)

    def block(args):
        qi, ci, blk = args
        s = jnp.einsum('bhqd,bkhd->bhqk', qi, k32) * scale
        s = s + ci[..., None] - c[:, :, None, :]
        qpos = blk * Q_BLOCK + jnp.arange(Q_BLOCK)
        s = jnp.where(kpos[None, :] <= qpos[:, None], s, -jnp.inf)
        p = jax.nn.softmax(s, axis=-1)
        return jnp.einsum('bhqk,bkhd->bqhd', p, v32)

    o = lax.map(block, (qb, cb, jnp.arange(n_blk)))
    return o.transpose(1, 0, 2, 3, 4).reshape(B, S, H * dh)

def mem_cross_attention(h, mem_n, w_mq, w_mkv, w_mo):
    B, S, _ = h.shape
    q = (h @ w_mq).reshape(B, S, MEM_HEADS, MEM_DH).astype(jnp.float32)
    k, v = jnp.split(mem_n @ w_mkv, 2, axis=-1)
    k = k.reshape(B, MEM_LEN, MEM_HEADS, MEM_DH).astype(jnp.float32)
    v = v.reshape(B, MEM_LEN, MEM_HEADS, MEM_DH).astype(jnp.float32)
    s = jnp.einsum('bqhd,bkhd->bhqk', q, k) * (1.0 / math.sqrt(MEM_DH))
    p = jax.nn.softmax(s, axis=-1)
    o = jnp.einsum('bhqk,bkhd->bqhd', p, v).reshape(B, S, D_MODEL).astype(h.dtype)
    return o @ w_mo

def second_inputs(seed: int = 0) -> dict:
    key = jax.random.key(seed)
    ks = iter(jax.random.split(key, 40))
    f32 = jnp.float32

    def w(shape, fan_in):
        return jax.random.normal(next(ks), shape, f32) * (fan_in ** -0.5)

    def gain(shape):
        return 1.0 + 0.05 * jax.random.normal(next(ks), shape, f32)

    L, D = DEPTH, D_MODEL
    return {
        "x": jax.random.normal(next(ks), (BATCH, SEQ, D), f32),
        "mem": jax.random.normal(next(ks), (BATCH, MEM_LEN, D), f32),
        "ffn1_pre_g": gain((L, D)),
        "ffn1_w_in": w((L, D, 2 * D_FF), D),
        "ffn1_w_down": w((L, D_FF, D), D_FF),
        "ffn1_post_g": gain((L, D)),
        "mix_pre_g": gain((L, D)),
        "w_in": w((L, D, IN_COLS), D),
        "hg_lb_logits": 0.5 * jax.random.normal(next(ks), (L + 1, HG_HEADS, HG_DK), f32),
        "hg_norm_g": gain((L, HG_VW)),
        "fox_f_bias": 1.0 + 0.5 * jax.random.normal(next(ks), (L, FOX_HEADS), f32),
        "w_branch_a": w((L, HG_VW, D), HG_VW),
        "w_branch_b": w((L, FOX_W, D), FOX_W),
        "b_gate": 0.02 * jax.random.normal(next(ks), (L, N_BRANCH * D), f32),
        "w_out": w((L, D, D), D),
        "mix_post_g": gain((L, D)),
        "mem_pre_g": gain((L, D)),
        "mem_kv_g": gain((L, D)),
        "w_mq": w((L, D, D), D),
        "w_mkv": w((L, D, 2 * D), D),
        "w_mo": w((L, D, D), D),
        "mem_post_g": gain((L, D)),
        "ffn2_pre_g": gain((L, D)),
        "ffn2_w_in": w((L, D, 2 * D_FF), D),
        "ffn2_w_down": w((L, D_FF, D), D_FF),
        "ffn2_post_g": gain((L, D)),
    }

def second_block(x, mem, ffn1_pre_g, ffn1_w_in, ffn1_w_down, ffn1_post_g,
              mix_pre_g, w_in, hg_lb_logits, hg_norm_g, fox_f_bias,
              w_branch_a, w_branch_b, b_gate, w_out, mix_post_g,
              mem_pre_g, mem_kv_g, w_mq, w_mkv, w_mo, mem_post_g,
              ffn2_pre_g, ffn2_w_in, ffn2_w_down, ffn2_post_g):
    B, S, D = x.shape
    lb_all = jnp.cumsum(jax.nn.softmax(hg_lb_logits.astype(jnp.float32), axis=0), axis=0)
    for l in range(DEPTH):
        h = rmsnorm(x, ffn1_pre_g[l])
        x = x + 0.5 * rmsnorm(swiglu(h, ffn1_w_in[l], ffn1_w_down[l]), ffn1_post_g[l])

        h = rmsnorm(x, mix_pre_g[l])
        q_a, f_a, i_a, g_a, q_b, k_b, v_b, f_b, gates = jnp.split(h @ w_in[l], IN_OFFSETS, axis=-1)

        o_a = hgrn2_chunkwise(q_a.reshape(B, S, HG_HEADS, HG_DK),
                              f_a.reshape(B, S, HG_HEADS, HG_DK),
                              i_a.reshape(B, S, HG_HEADS, HG_DV), lb_all[l])
        o_a = rmsnorm(o_a.astype(x.dtype), hg_norm_g[l]) * jax.nn.silu(g_a)
        y_a = o_a @ w_branch_a[l]

        o_b = fox_attention(q_b.reshape(B, S, FOX_HEADS, FOX_DH),
                            k_b.reshape(B, S, FOX_HEADS, FOX_DH),
                            v_b.reshape(B, S, FOX_HEADS, FOX_DH),
                            f_b + fox_f_bias[l])
        y_b = o_b.astype(x.dtype) @ w_branch_b[l]

        gate = jax.nn.sigmoid((gates + b_gate[l]).astype(jnp.float32)).reshape(B, S, N_BRANCH, D)
        y = (gate[:, :, 0] * y_a.astype(jnp.float32) + gate[:, :, 1] * y_b.astype(jnp.float32)).astype(x.dtype)
        x = x + rmsnorm(y @ w_out[l], mix_post_g[l])

        h = rmsnorm(x, mem_pre_g[l])
        mem_n = rmsnorm(mem, mem_kv_g[l])
        x = x + rmsnorm(mem_cross_attention(h, mem_n, w_mq[l], w_mkv[l], w_mo[l]), mem_post_g[l])

        h = rmsnorm(x, ffn2_pre_g[l])
        x = x + 0.5 * rmsnorm(swiglu(h, ffn2_w_in[l], ffn2_w_down[l]), ffn2_post_g[l])
    return x


def setup_inputs(seed=0):
    out = dict(first_inputs(seed))
    for name, value in second_inputs(seed + 1).items():
        if name != "x":
            out[name + "_2"] = value
    return out


def reference(
    x, c, ada_w, ada_b, norm_g, w_in, shift_mu, w0, w2, a0, a2, k_k, k_a, r_k, lnx_g, lnx_b,
    kv_norm_g, w_uk, w_uv, w_pa, w_pb, w_o, rel_bias, final_g, mem_2, ffn1_pre_g_2, ffn1_w_in_2,
    ffn1_w_down_2, ffn1_post_g_2, mix_pre_g_2, w_in_2, hg_lb_logits_2, hg_norm_g_2,
    fox_f_bias_2, w_branch_a_2, w_branch_b_2, b_gate_2, w_out_2, mix_post_g_2, mem_pre_g_2,
    mem_kv_g_2, w_mq_2, w_mkv_2, w_mo_2, mem_post_g_2, ffn2_pre_g_2, ffn2_w_in_2, ffn2_w_down_2,
    ffn2_post_g_2,
):
    x = first_block(
        x, c, ada_w, ada_b, norm_g, w_in, shift_mu, w0, w2, a0, a2, k_k, k_a, r_k, lnx_g, lnx_b,
        kv_norm_g, w_uk, w_uv, w_pa, w_pb, w_o, rel_bias, final_g,
    )
    return second_block(
        x, mem_2, ffn1_pre_g_2, ffn1_w_in_2, ffn1_w_down_2, ffn1_post_g_2, mix_pre_g_2, w_in_2,
        hg_lb_logits_2, hg_norm_g_2, fox_f_bias_2, w_branch_a_2, w_branch_b_2, b_gate_2,
        w_out_2, mix_post_g_2, mem_pre_g_2, mem_kv_g_2, w_mq_2, w_mkv_2, w_mo_2, mem_post_g_2,
        ffn2_pre_g_2, ffn2_w_in_2, ffn2_w_down_2, ffn2_post_g_2,
    )


_drawn_inputs = setup_inputs


def setup_inputs(seed=0):
    import zlib

    import numpy as np

    out = dict(_drawn_inputs(seed))
    spreads = {}
    factors = {'ada_b': 3.415,
     'norm_g': 3.047,
     'w2': 6.171,
     'k_k': 37.719,
     'k_a': 4.816,
     'lnx_g': 21.274,
     'lnx_b': 46.533,
     'kv_norm_g': 8.0,
     'rel_bias': 4.063,
     'b_gate_2': 8.0,
     'ffn2_pre_g_2': 3.097,
     'ffn2_post_g_2': 4.234}
    for name, (base, spread) in spreads.items():
        noise = np.random.default_rng([zlib.crc32(name.encode()), seed]).standard_normal(out[name].shape)
        drawn = base * np.exp(spread * noise) if base else spread * noise
        out[name] = __import__('jax').numpy.asarray(drawn.astype(out[name].dtype))
    for name, factor in factors.items():
        out[name] = (out[name] * factor).astype(out[name].dtype)
    return out
```

```python
import math
from contextlib import ExitStack

import numpy as np

import concourse.bass as bass
from concourse import mybir

F32 = mybir.dt.float32
F32R = mybir.dt.float32r
U32 = mybir.dt.uint32
ALU = mybir.AluOpType
ACT = mybir.ActivationFunctionType
AX = mybir.AxisListType
P = 128
NRAW, NHL = 3, 3
NEG = -1.0e30
GONE = -3.0e38

VEC = {}
for _n, _w in [("c", 8), ("norm_g", 8), ("ada_b", 24), ("shift_mu", 13), ("w0", 4), ("a0", 4), ("k_k", 4),
               ("k_a", 4), ("r_k", 4), ("lnx_g", 4), ("lnx_b", 4), ("ffn1_pre_g_2", 8), ("mix_pre_g_2", 8),
               ("hg_lb_logits_2", 16), ("hg_norm_g_2", 8), ("b_gate_2", 16), ("mem_pre_g_2", 8),
               ("mem_kv_g_2", 8), ("ffn2_pre_g_2", 8), ("fox_f_bias_2", 1)]:
    VEC[_n] = (sum(w for _, w in VEC.values()), _w)
NVEC = sum(w for _, w in VEC.values())

CON = {}
for _n, _w in [("ident", 128), ("flip", 128), ("strict", 128), ("incl", 128), ("zero", 128), ("causal", 128),
               ("ones64", 128), ("off", 7 * 128), ("reset", 256), ("one", 256), ("eps", 4), ("hot", 384)]:
    CON[_n] = (sum(w for _, w in CON.values()), _w)
NCON = sum(w for _, w in CON.values())


def constants():
    c = np.zeros((P, NCON), np.float32)

    def put(name, a):
        o, w = CON[name]
        c[:a.shape[0], o:o + w] = a
    s, t = np.arange(P)[:, None], np.arange(P)[None, :]
    put("ident", s == t)
    put("flip", s + t == P - 1)
    put("strict", s < t)
    put("incl", s <= t)
    put("causal", np.where(t > s, NEG, 0.0))
    put("ones64", s // 64 == t // 64)
    put("off", np.concatenate([(s // (2 << l) == t // (2 << l)) & ((s >> l) % 2 == 0) & ((t >> l) % 2 == 1)
                               for l in range(7)], axis=1))
    put("reset", np.broadcast_to(np.arange(256) % P != 0, (P, 256)))
    put("one", np.ones((P, 256)))
    put("eps", np.broadcast_to(np.array([1e-6, 64e-5, 0.0, 0.0]), (P, 4)))
    dist = np.arange(256)
    d = np.maximum(dist, 1).astype(np.float32)
    large = 16 + (np.log(d / np.float32(16)) / np.float32(math.log(8)) * np.float32(16)).astype(np.int32)
    bucket = np.where(dist < 16, dist, np.minimum(large, 31))
    hot = np.zeros((32, 384), np.float32)
    hot[bucket, 255 - dist] = 1.0
    put("hot", hot)
    return c


class Engine:

    def __init__(self, sem, serial):
        self.sem, self.serial, self.n, self.ops, self.seen = sem, serial, 0, [], {}

    def __call__(self, fn, *waits, inc=True):
        if self.serial and self.n:
            waits += (self.last(),)
        self.wait(*waits)
        if inc:
            self.n += 1
        self.ops.append((fn, self.sem if inc else None))
        return (self.sem, self.n)

    def wait(self, *waits):
        for w in waits:
            for sem, v in (w if isinstance(w, list) else [w]):
                if v > self.seen.get(sem.name, 0):
                    self.seen[sem.name] = v
                    self.ops.append((None, (sem, v)))

    def last(self):
        return (self.sem, self.n)

    def play(self, eng):
        for fn, s in self.ops:
            if fn is None:
                eng.wait_ge(*s)
            elif s is None:
                fn(eng)
            elif isinstance(s, tuple):
                fn(eng).then_inc(*s)
            else:
                fn(eng).then_inc(s, 1)


class Loader:

    def __init__(self):
        self.q, self.count = Engine(None, False), {}

    def __call__(self, out, in_, sem, *waits):
        self.q.wait(*waits)
        self.q.ops.append((lambda e: e.dma_start(out, in_), (sem, 16)))
        self.count[sem.name] = self.count.get(sem.name, 0) + 16
        return (sem, self.count[sem.name])


def program(nc, I, consts, vecs, out):
    ctx = ExitStack()
    with ctx:
        def sem(name):
            return ctx.enter_context(nc.semaphore(name))

        class Scope:
            def __init__(self):
                self.es = ExitStack()

            def __call__(self, name, shape, dt=F32):
                return self.es.enter_context(nc.sbuf_tensor(name, shape, dt))

            def close(self):
                self.es.close()

        glob = Scope()
        V, A, G, T = (Engine(sem(n), s) for n, s in
                      [("s_vec", True), ("s_act", True), ("s_pool", True), ("s_pe", False)])
        load = Loader()
        s_const = sem("s_const")
        s_row = sem("s_row")
        s_raw = [sem(f"s_raw{i}") for i in range(NRAW)]
        s_misc = sem("s_misc")
        s_out = sem("s_out")

        con = glob("con", [P, NCON])
        vec = glob("vec", [P, NVEC])
        raw = [glob(f"raw{i}", [P, 2048]) for i in range(NRAW)]
        whi = [glob(f"whi{i}", [P, 2048], F32R) for i in range(NHL)]
        wlo = [glob(f"wlo{i}", [P, 2048], F32R) for i in range(NHL)]
        x = glob("x", [P, 2, 1024])
        hT = [glob("hThi", [P, 8, 256], F32R), glob("hTlo", [P, 8, 256], F32R)]
        row = glob("row", [P, 1024])
        st = glob("st", [P, 16])
        PS = [ctx.enter_context(nc.psum_tensor(f"ps{i}", [P, 512], F32)) for i in range(8)]
        free = [[] for _ in range(8)]
        turn = {"main": 0, "side": 0}
        BANKS = {"main": [0, 1, 2, 3], "side": [4, 5, 6, 7]}

        def bank(kind):
            b = BANKS[kind][turn[kind] % 4]
            turn[kind] += 1
            return b

        def C(name, i=0, w=None, rows=P):
            o, n = CON[name]
            return con[0:rows, o + i:o + (i + w if w else n)]

        def vcol(name, j=0, w=1):
            o = VEC[name][0] + j
            return vec[:, o:o + w]

        ident = C("ident")

        def fence():
            return [e.last() for e in (V, A, G, T)]

        def enter():
            f = fence()
            for e in (V, A, G):
                e.wait(f)
            return f

        def tt(E, o, a, b, op, *w):
            return E(lambda e: e.tensor_tensor(o, a, b, op), *w)

        def ts(E, o, a, s1, s2, op0, op1, *w):
            if op1 is None:
                return E(lambda e: e.tensor_scalar(o, a, s1, None, op0), *w)
            return E(lambda e: e.tensor_scalar(o, a, s1, s2, op0, op1), *w)

        def stt(o, a, s, b, op0, op1, *w):
            return V(lambda e: e.scalar_tensor_tensor(out=o, in0=a, scalar=s, in1=b, op0=op0, op1=op1), *w)

        def act(o, a, f, *w, **kw):
            return A(lambda e: e.activation(o, a, f, **kw), *w)

        def cp(E, o, a, *w):
            if E is A:
                return act(o, a, ACT.Copy, *w)
            return E(lambda e: e.tensor_copy(o, a), *w)

        def mm(o, l, r, start, stop, *w, inc=False, skip=False):
            return T(lambda e: e.matmul(o, l, r, start=start, stop=stop, skip_group_check=skip), *w, inc=inc)

        def mm3(o, l, r, start, stop, *w, inc=False):
            mm(o, l[0], r[0], start, False, *w)
            mm(o, l[0], r[1], False, False)
            return mm(o, l[1], r[0], False, stop, inc=inc)

        def tr(o, a, *w, inc=False):
            return T(lambda e: e.transpose(o, a, ident), *w, inc=inc)

        def split(hi, lo, a, *w):
            t = cp(A, hi, a, *w)
            return tt(V, lo, a, hi, ALU.subtract, t)

        tasks = []

        def slab(parts, fn, shape):
            tasks.append(("slab", parts, fn, shape))

        def do(fn):
            tasks.append(("do", fn))

        def steps(gen, k=None):
            def go():
                for n, _ in enumerate(gen):
                    if k is not None and n + 1 == k:
                        return
            tasks.append(("do", go))

        def fmslab(w, c0, n, fn):
            slab([(None, w[:, c0:c0 + n].rearrange("(k p) n -> p k n", p=P))], fn, (8, n))

        def tmslabs(w, cols, fn):
            for kh in range(2):
                parts, o = [], 0
                for c0, n in cols:
                    parts.append(((o, n), w[kh * 512:(kh + 1) * 512, c0:c0 + n].rearrange("(k p) n -> p k n", p=P)))
                    o += n
                slab(parts, lambda hi, lo, kh=kh: fn(kh, hi, lo), (4, o))

        def run_tasks():
            slabs = [t for t in tasks if t[0] == "slab"]
            dma_tok, lo_tok, hi_tok, pe_tok = [None] * len(slabs), [None] * len(slabs), [None] * len(slabs), [None] * len(slabs)

            def view(buf, shape):
                k, n = shape
                return buf[:, 0:k * n].rearrange("p (k n) -> p k n", k=k)

            def fetch(i):
                _, parts, _, shape = slabs[i]
                w = [lo_tok[i - NRAW], hi_tok[i - NRAW]] if i >= NRAW else []
                dst = view(raw[i % NRAW], shape)
                for sel, src in parts:
                    d = dst if sel is None else dst[:, :, sel[0]:sel[0] + sel[1]]
                    dma_tok[i] = load(d, src, s_raw[i % NRAW], *w)

            def cut(i):
                n = slabs[i][3][0] * slabs[i][3][1]
                r, h, l = raw[i % NRAW], whi[i % NHL], wlo[i % NHL]
                w = [pe_tok[i - NHL]] if i >= NHL else []
                hi_tok[i] = cp(A, h[:, 0:n], r[:, 0:n], dma_tok[i], *w)
                lo_tok[i] = tt(G, l[:, 0:n], r[:, 0:n], h[:, 0:n], ALU.subtract, hi_tok[i])

            fetched = done = 0
            i = 0
            for t in tasks:
                if t[0] == "do":
                    t[1]()
                    continue
                while done < min(i + 2, len(slabs)):
                    while fetched < min(done + NRAW, len(slabs)):
                        fetch(fetched)
                        fetched += 1
                    cut(done)
                    done += 1
                T.wait(hi_tok[i], lo_tok[i])
                sh = t[3]
                t[2](view(whi[i % NHL], sh), view(wlo[i % NHL], sh))
                pe_tok[i] = T.last()
                i += 1

        def rms_rows(src, n, col, junk, *w, eps=0):
            for t in range(2):
                act(junk, src[:, t, :], ACT.Square, *w, accum_out=st[:, col + t:col + t + 1])
            r = st[:, col:col + 2]
            a = act(r, r, ACT.Sqrt, scale=1.0 / n, bias=C("eps", eps, 1))
            return V(lambda e: e.reciprocal(r, r), a)

        def to_fm(src, dst, kind, nf, scale, bias, *w):
            tmp = src[2]
            for f0 in range(0, nf, 2):
                b = bank(kind)
                for f in (f0, f0 + 1):
                    for t in range(2):
                        k = tr(PS[b][:, (f - f0) * 256 + t * 128:(f - f0) * 256 + t * 128 + 128],
                               src[0][:, t, f * 128:f * 128 + 128], free[b], *w, inc=True)
                j = (f0 // 2) % 2
                for f in (f0, f0 + 1):
                    o = tmp[:, j, f - f0, :]
                    i = PS[b][:, (f - f0) * 256:(f - f0) * 256 + 256]
                    if bias is None:
                        v = ts(V, o, i, scale(f), None, ALU.mult, None, k, src[1][j])
                    else:
                        v = ts(V, o, i, scale(f), bias(f), ALU.mult, ALU.add, k, src[1][j])
                free[b] = [v]
                h = cp(A, dst[0][:, f0:f0 + 2, :], tmp[:, j], v)
                src[1][j] = [tt(V, dst[1][:, f0:f0 + 2, :], tmp[:, j], dst[0][:, f0:f0 + 2, :], ALU.subtract, h)]
            return src[1][0] + src[1][1]

        def norm_fm(S, src, g, wait, bias=None, scale=None, kind="main"):
            xn = S("xn" + g, [P, 2, 1024])
            tmp = S("tmp" + g, [P, 2, 2, 256])
            v = rms_rows(src, 1024, 0, xn[:, 0, :], wait)
            for t in range(2):
                v = ts(V, xn[:, t, :], src[:, t, :], st[:, t:t + 1], None, ALU.mult, None)
            T.wait(to_fm((xn, [[], []], tmp), hT, kind, 8, scale or (lambda f: vcol(g, f)), bias, v))

        def load_row(name, *w):
            return load(row[:, :], I[name].rearrange("a n -> (a n)").rearrange("(a n) -> a n", a=1)
                        .broadcast_to([P, 1024]) if len(I[name].shape) == 2 else
                        I[name].rearrange("(a n) -> a n", a=1).broadcast_to([P, 1024]), s_row, *w)

        row_free = [[]]

        def add_rms(S, y, name, half):
            r = load_row(name, *row_free[0])
            junk = S("junk" + name, [P, 1024])
            v = rms_rows(y, 1024, 2, junk[:, :], V.last())
            if half:
                v = ts(V, st[:, 2:4], st[:, 2:4], 0.5, None, ALU.mult, None)
            for t in range(2):
                stt(y[:, t, :], y[:, t, :], st[:, 2 + t:3 + t], row[:, :], ALU.mult, ALU.mult, r)
                v = tt(V, x[:, t, :], x[:, t, :], y[:, t, :], ALU.add)
            row_free[0] = [v]
            return v

        tm_banks = {}

        def tm_out(key, lhs, kt0, nk, last, hi, lo, evac, kind="main"):
            if kt0 == 0:
                tm_banks[key] = [bank(kind), bank(kind)]
            bs = tm_banks[key]
            n = hi.shape[2]
            for t in range(2):
                for k in range(nk):
                    l = [z[:, kt0 + k, t * 128:t * 128 + 128] for z in lhs]
                    end = last and k == nk - 1
                    m = mm3(PS[bs[t]][:, 0:n], l, (hi[:, k, :], lo[:, k, :]), kt0 + k == 0, end,
                            *(free[bs[t]] if kt0 + k == 0 else []), inc=(k == nk - 1))
                if last:
                    free[bs[t]] = [evac(t, PS[bs[t]][:, 0:n], m)]

        def fm_tiles(hi, lo, cols, rhs, evac, nk=8, kind="main"):
            for j0 in range(0, len(cols), 2):
                b = bank(kind)
                part = cols[j0:j0 + 2]
                for j, c0 in enumerate(part):
                    for k in range(nk):
                        m = mm3(PS[b][:, j * 256:j * 256 + 256], (hi[:, k, c0:c0 + 128], lo[:, k, c0:c0 + 128]),
                                (rhs[0][:, k, :], rhs[1][:, k, :]), k == 0, k == nk - 1, free[b], inc=(k == nk - 1))
                free[b] = [evac(j0, PS[b][:, 0:256 * len(part)].rearrange("p (j t) -> p j t", t=256), m)]

        def attention(S, tag, heads, logits, mask, vt, nkt, outp, pt=None):
            z = [S(f"z{t}{tag}", [P, 4, 128 * nkt[t]]) for t in range(2)]
            if pt is None:
                pt = S(f"pt{tag}", [P, 4, 2, 256])
            red = S(f"red{tag}", [P, 2, 3, 4])
            pt_free = []
            for g in range(0, len(heads), 4):
                for t in range(2):
                    n = 128 * nkt[t]
                    for h0 in range(0, 4, 2):
                        b = bank("side")
                        T.wait(free[b])
                        for j in range(2):
                            k = logits(heads[g + h0 + j], t, PS[b][:, j * n:(j + 1) * n])
                        i = PS[b][:, 0:2 * n].rearrange("p (j k) -> p j k", j=2)
                        m = mask(t)
                        if m is None:
                            v = cp(V, z[t][:, h0:h0 + 2, :], i, k, pt_free)
                        else:
                            v = tt(V, z[t][:, h0:h0 + 2, :], i, m.unsqueeze(1).broadcast_to([P, 2, n]), ALU.add, k, pt_free)
                        free[b] = [v]
                        yield
                    mx, sm, rc = (red[:, t, q, :] for q in range(3))
                    zt = z[t]
                    v = V(lambda e, mx=mx, zt=zt: e.tensor_reduce(mx, zt[:, :, :], AX.X, ALU.max, negate=True))
                    for h in range(4):
                        a = act(zt[:, h, :], zt[:, h, :], ACT.Exp, v, bias=red[:, t, 0, h:h + 1],
                                accum_out=red[:, t, 1, h:h + 1])
                    V(lambda e, rc=rc, sm=sm: e.reciprocal(rc, sm), a)
                    v = tt(V, zt[:, :, :], zt[:, :, :], rc.unsqueeze(2).broadcast_to([P, 4, n]), ALU.mult)
                    yield
                    for h0 in range(0, 4, 4 // nkt[t]):
                        b = bank("side")
                        nh = 4 // nkt[t]
                        for j in range(nh):
                            for k in range(nkt[t]):
                                m = tr(PS[b][:, (j * nkt[t] + k) * 128:(j * nkt[t] + k) * 128 + 128],
                                       zt[:, h0 + j, k * 128:k * 128 + 128], v, free[b], inc=True)
                        o = pt[:, h0:h0 + nh, 0:nkt[t], t * 128:t * 128 + 128]
                        i = PS[b][:, :].rearrange("p (j k q) -> p j k q", j=nh, k=nkt[t])
                        c = cp(V, o, i, m, pt_free)
                        free[b] = [c]
                    yield
                for j in range(4):
                    h = heads[g + j]
                    b = bank("side")
                    if nkt[0] == 2:
                        mm(PS[b][:, 0:256], vt(h, 0), pt[:, j, 0, :], True, False, c, free[b])
                        m = mm(PS[b][:, 0:256], vt(h, 1), pt[:, j, 1, :], False, True, inc=True)
                    else:
                        mm(PS[b][:, 0:256], vt(h, 0), pt[:, j, 0, :], True, False, c, free[b])
                        m = mm(PS[b][:, 128:256], vt(h, 1), pt[:, j, 1, 128:256], False, True, inc=True)
                    free[b] = [outp(h, PS[b][:, 0:256], m)]
                    yield
                pt_free = [m]

        t_con = [load(con[:, :], consts, s_const), load(vec[:, :], vecs, s_const),
                 load(x[:, :, :], I["x"].rearrange("a (t p) d -> p (a t) d", p=P), s_const)][-1]
        for e in (V, A, G, T):
            e.wait(t_con)

        B1 = Scope()
        za = B1("za", [P, 4, 256])
        zb = B1("zb", [P, 4, 256])
        qq = B1("qq", [P, 8, 256])
        qT, qiT = qq[:, 0:4, :], qq[:, 4:8, :]
        kiT = B1("kiT", [P, 256])
        lat = B1("lat", [P, 2, 128])
        latT = B1("latT", [P, 256])
        wi = B1("wi", [P, 2, 8])
        gab = B1("gab", [P, 16, 256])
        gate = B1("gate", [P, 8])
        w2a2 = B1("w2a2", [P, 512])
        wukT = B1("wukT", [P, 4, 128])
        wuv = B1("wuv", [P, 512])
        kvg = B1("kvg", [P, 128])
        relb = B1("relb", [32, 8])
        biasv = B1("biasv", [8, 384])
        t_small = [load(w2a2[0:64, :], I["w2"].rearrange("a r n -> (a r) n"), s_misc),
                   load(w2a2[64:128, :], I["a2"].rearrange("a r n -> (a r) n"), s_misc),
                   load(wukT[:, :, :], I["w_uk"], s_misc),
                   load(wuv[:, :], I["w_uv"].rearrange("a c h d -> (a c) (h d)"), s_misc),
                   load(kvg[:, :], I["kv_norm_g"].broadcast_to([P, 128]), s_misc),
                   load(relb[:, :], I["rel_bias"], s_misc)][-1]

        M1 = Scope()
        cs = M1("cs", [P, 8])
        cHL = M1("cHL", [P, 8, 2], F32R)
        mod = M1("mod", [P, 24])
        hsc = M1("hsc", [P, 8])
        S = M1
        a = act(cs[:, :], vcol("c", 0, 8), ACT.Sigmoid)
        v = tt(V, cs[:, :], cs[:, :], vcol("c", 0, 8), ALU.mult, a)
        t_c = [split(cHL[:, :, 0], cHL[:, :, 1], cs[:, :], v)]
        bmod = 7
        ada = I["ada_w"].rearrange("a r n -> (a r) n")

        def ada_cols(j, hi, lo):
            T.wait(t_c)
            if j == 8:
                T.wait(free[bmod])
            for f in range(2):
                o = PS[bmod][:, (2 * j + f) * 2:(2 * j + f) * 2 + 2]
                for k in range(8):
                    mm(o, hi[:, k, f * 128:f * 128 + 128], cHL[:, k, :], k == 0, False)
                    m = mm(o, lo[:, k, f * 128:f * 128 + 128], cHL[:, k, :], False, k == 7, inc=True)
            if j == 7:
                v = V(lambda e: e.tensor_reduce(mod[:, 0:16], PS[bmod][:, 0:32].rearrange("p (f a) -> p f a", a=2),
                                                AX.X, ALU.add), m)
                tt(V, mod[:, 0:16], mod[:, 0:16], vcol("ada_b", 0, 16), ALU.add)
                stt(hsc[:, :], mod[:, 8:16], 1.0, vcol("norm_g", 0, 8), ALU.add, ALU.mult)
                free[bmod] = [v]
            if j == 11:
                v = V(lambda e: e.tensor_reduce(mod[:, 16:24], PS[bmod][:, 32:48].rearrange("p (f a) -> p f a", a=2),
                                                AX.X, ALU.add), m)
                free[bmod] = [v]
                tt(V, gate[:, :], mod[:, 16:24], vcol("ada_b", 16, 8), ALU.add)

        for j in range(8):
            fmslab(ada, 256 * j, 256, lambda hi, lo, j=j: ada_cols(j, hi, lo))

        def first_norm():
            norm_fm(M1, x, "norm_g", t_con, bias=lambda f: mod[:, f:f + 1], scale=lambda f: hsc[:, f:f + 1])
        do(first_norm)

        for j in range(8, 12):
            fmslab(ada, 256 * j, 256, lambda hi, lo, j=j: ada_cols(j, hi, lo))

        w_in = I["w_in"].rearrange("a r n -> (a r) n")
        RW = [None]
        SC = [None]
        R = {}

        def open_rwkv():
            M1.close()
            f = enter()
            RW[0] = Scope()
            SC[0] = Scope()
            for n in ("AR",):
                R[n] = RW[0](n, [P, 4, 2, 2, 128])
            for n in ("bt", "kt", "bonus"):
                R[n] = RW[0](n, [P, 4, 256])
            R["VT"] = RW[0]("VT", [P, 2, 512])
            R["Y"] = gab[:, 12:16, :].rearrange("p f t -> p (f t)").rearrange("p (c h v) -> p c h v", c=2, v=64)
            R["esc"] = RW[0]("esc", [P, 4])
            R["rkv"] = SC[0]("rkv", [P, 13, 256])
            for n in ("c", "lw", "a", "kkn"):
                R[n] = SC[0](n, [P, 4, 256])
            R["mid"] = SC[0]("mid", [P, 8])
            R["u"] = R["AR"][:, 0:2, :, :, :].rearrange("p a b c d -> p (a b c d)").rearrange("p (z j t) -> p z j t", z=2, j=2)
            R["d"] = R["AR"][:, 2:4, :, :, :].rearrange("p a b c d -> p (a b c d)").rearrange("p (z j t) -> p z j t", z=2, j=2)
        do(open_rwkv)

        def shifted(t0):
            def evac(j0, p, m):
                n = p.shape[1]
                z = ((t0 + j0) // 2) % 2
                u, d = R["u"][:, z, 0:n, :], R["d"][:, z, 0:n, :]
                a = cp(A, u, p, m, V.last())
                tt(V, d[:, :, 1:256], u[:, :, 0:255], u[:, :, 1:256], ALU.subtract, a)
                v = ts(V, d[:, :, 0:1], u[:, :, 0:1], -1.0, None, ALU.mult, None)
                for j in range(n):
                    f = t0 + j0 + j
                    v = stt(R["rkv"][:, f, :], d[:, j, :], vcol("shift_mu", f), u[:, j, :], ALU.mult, ALU.add)
                return a
            return evac

        for j in range(6):
            fmslab(w_in, 256 * j, 256, lambda hi, lo, j=j: fm_tiles(hi, lo, [0, 128], hT, shifted(2 * j)))
        fmslab(w_in, 1536, 128, lambda hi, lo: fm_tiles(hi, lo, [0], hT, shifted(12)))

        def rwkv():
            r, k, v_, wa = R["rkv"][:, 0:4, :], R["rkv"][:, 4:8, :], R["rkv"][:, 8:12, :], R["rkv"][:, 12, :]
            AR, bt, kt, c, lw, a, kkn = (R[n] for n in ("AR", "bt", "kt", "c", "lw", "a", "kkn"))
            sq = kt
            t = act(wa[0:64, :], wa[0:64, :], ACT.Tanh, V.last())
            for dst, p0, cb in ((lw, 0, "w0"), (a, 64, "a0")):
                for f in range(0, 4, 2):
                    b = bank("side")
                    for j in range(2):
                        m = mm(PS[b][:, j * 256:j * 256 + 256], w2a2[p0:p0 + 64, (f + j) * 128:(f + j) * 128 + 128],
                               wa[p0:p0 + 64, :], True, True, t, t_small, free[b], inc=True)
                    for j in range(2):
                        q = act(dst[:, f + j, :], PS[b][:, j * 256:j * 256 + 256], ACT.Sigmoid, m, bias=vcol(cb, f + j))
                    free[b] = [q]
            yield
            for f in range(4):
                s = act(sq[:, f, :], k[:, f, :], ACT.Square, scale=vcol("k_k", f))
            for f in range(4):
                ts(V, kkn[:, f, :], k[:, f, :], vcol("k_k", f), None, ALU.mult, None)
            ts(V, lw[:, :, :], lw[:, :, :], -math.exp(-0.5), None, ALU.mult, None, q)
            for f in range(4):
                V(lambda e, f=f: e.tensor_tensor_scan(c[:, f, :], C("reset"), lw[:, f, :], 0.0, ALU.mult, ALU.add))
            for f in range(0, 4, 2):
                b = bank("side")
                for j in range(2):
                    m = mm(PS[b][:, j * 256:j * 256 + 256], C("ones64"), sq[:, f + j, :], True, True, s, free[b], inc=True)
                q = act(bt[:, f:f + 2, :], PS[b][:, :].rearrange("p (j t) -> p j t", j=2), ACT.Sqrt, m)
                free[b] = [q]
            yield
            ts(V, bt[:, :, :], bt[:, :, :], 1e-12, None, ALU.max, None, q)
            V(lambda e: e.reciprocal(bt[:, :, :], bt[:, :, :]))
            tt(V, kkn[:, :, :], kkn[:, :, :], bt[:, :, :], ALU.mult)
            for f in range(4):
                ts(V, bt[:, f, :], a[:, f, :], -1.0, vcol("k_a", f), ALU.add, ALU.mult)
            stt(k, bt[:, :, :], 1.0, k, ALU.add, ALU.mult)
            yield
            for f in range(4):
                v = stt(sq[:, f, :], r[:, f, :], vcol("r_k", f), k[:, f, :], ALU.mult, ALU.mult, T.last())
            for f in range(0, 4, 2):
                b = bank("side")
                for j in range(2):
                    m = mm(PS[b][:, j * 256:j * 256 + 256], C("ones64"), sq[:, f + j, :], True, True, v, free[b], inc=True)
                free[b] = [tt(V, R["bonus"][:, f:f + 2, :], PS[b][:, :].rearrange("p (j t) -> p j t", j=2),
                              v_[:, f:f + 2, :], ALU.mult, m)]
            for t in range(2):
                b = bank("side")
                for f in range(4):
                    m2 = tr(PS[b][:, f * 128:f * 128 + 128], v_[:, f, t * 128:t * 128 + 128], free[b], inc=True)
                free[b] = [cp(A, R["VT"][:, t, :], PS[b][:, :], m2)]
            yield
            cv = c[:, :, :].rearrange("p f (c t) -> p (f c) t", c=2)
            cp(V, R["mid"][:, :], cv[:, :, 63])
            tt(V, cv, cv, R["mid"][:, :].unsqueeze(2).broadcast_to([P, 8, 128]), ALU.subtract)
            v = tt(V, lw[:, :, :], c[:, :, :], lw[:, :, :], ALU.subtract)
            mid = R["mid"][:, :].rearrange("p (f c) -> p f c", c=2)
            v = tt(V, R["esc"][:, :], c[:, :, 127], mid[:, :, 1], ALU.add)
            ARv = AR[:, :, :, :, :].rearrange("p f c a t -> p (f c) a t")
            act(R["esc"][:, :], R["esc"][:, :], ACT.Exp, v)
            a0 = act(ARv[:, :, 0, :], lw[:, :, :].rearrange("p f (c t) -> p (f c) t", c=2), ACT.Exp)
            a1 = act(ARv[:, :, 1, :], cv, ACT.Exp)
            a2 = act(kt[:, :, :], c[:, :, :], ACT.Exp, m, scale=-1.0)
            tt(V, bt[:, :, :], kkn[:, :, :], a[:, :, :], ALU.mult)
            stt(ARv[:, :, 0, :], ARv[:, :, 0, :], -1.0, kkn[:, :, :].rearrange("p f (c t) -> p (f c) t", c=2),
                ALU.mult, ALU.mult, a0)
            tt(V, ARv[:, :, 1, :], ARv[:, :, 1, :], r.rearrange("p f (c t) -> p (f c) t", c=2), ALU.mult, a1)
            tt(V, bt[:, :, :], bt[:, :, :], kt[:, :, :], ALU.mult, a2)
            v = tt(V, kt[:, :, :], kt[:, :, :], k, ALU.mult)
            yield
            SC[0].close()
            enter()
            SC[0] = Scope()
            NM = 8
            TB = SC[0]("TB", [P, NM, 2, 128])
            TK = SC[0]("TK", [P, NM, 2, 128])
            W = SC[0]("W", [P, NM, 128])
            WT = SC[0]("WT", [P, NM, 128])
            X1 = gab[:, 8:12, :].rearrange("p f t -> p (f t)").rearrange("p (n t) -> p n t", t=128)
            OF = gab[:, 4:8, :].rearrange("p f t -> p (f t)").rearrange("p (n t) -> p n t", t=128)
            XU = SC[0]("XU", [P, 2, 4, 64])
            S0 = SC[0]("S0", [P, 2, 64])
            btT = SC[0]("btT", [P, 2, 2, 128])
            G(lambda e: e.memset(TB[:, :, :, :], 0.0))
            zt = G(lambda e: e.memset(TK[:, :, :, :], 0.0))
            tri = con[:, CON["strict"][0]:CON["strict"][0] + 256].bitcast(U32)
            VT, Y = R["VT"], R["Y"]
            for g in range(2):
                war = T.last()
                for src, dst in ((bt, TB), (kt, TK)):
                    for i in range(4):
                        h = 4 * g + i
                        p0, f = (h % 2) * 64, h // 2
                        b = bank("side")
                        for c_ in range(2):
                            m = mm(PS[b][:, c_ * 256:c_ * 256 + 256], src[p0:p0 + 64, f, c_ * 128:c_ * 128 + 128],
                                   AR[p0:p0 + 64, f, c_, :, :].rearrange("p a t -> p (a t)"), True, True, v, free[b], inc=True)
                        o = dst[:, 2 * i:2 * i + 2, :, :].rearrange("p c a t -> p c (a t)")
                        q = V(lambda e, o=o, b=b: e.copy_predicated(
                            o, tri.unsqueeze(1).broadcast_to([P, 2, 256]), PS[b][:, :].rearrange("p (c n) -> p c n", c=2)),
                            m, zt, war)
                        free[b] = [q]
                    yield
                off = lambda l: C("off", 128 * l, 128).unsqueeze(1).broadcast_to([P, NM, 128])
                idb = ident.unsqueeze(1).broadcast_to([P, NM, 128])
                TT = TB[:, :, 0, :]
                o_tok = tt(V, OF[:, :, :], TT, off(0), ALU.mult, T.last())
                wt_tok = tt(V, WT[:, :, :], OF[:, :, :], idb, ALU.add)
                w_tok = None
                for q4 in range(2):
                    b = bank("side")
                    for j in range(4):
                        m = mm(PS[b][:, j * 128:j * 128 + 128], OF[:, 4 * q4 + j, :], ident, True, True, o_tok, free[b], inc=True)
                    w_tok = tt(V, W[:, 4 * q4:4 * q4 + 4, :], PS[b][:, :].rearrange("p (j t) -> p j t", j=4),
                               ident.unsqueeze(1).broadcast_to([P, 4, 128]), ALU.add, m)
                    free[b] = [w_tok]
                yield
                for l in range(1, 7):
                    o_tok = tt(V, OF[:, :, :], TT, off(l), ALU.mult, m)
                    xs = []
                    for q4 in range(2):
                        b = bank("side")
                        for j in range(4):
                            n = 4 * q4 + j
                            m = mm(PS[b][:, j * 128:j * 128 + 128], OF[:, n, :], W[:, n, :], True, True, o_tok, w_tok, free[b], inc=True)
                        q = cp(A, X1[:, 4 * q4:4 * q4 + 4, :], PS[b][:, :].rearrange("p (j t) -> p j t", j=4), m)
                        free[b] = [q]
                        xs.append(q)
                    yield
                    for q4 in range(2):
                        if l < 6:
                            b = bank("side")
                            for j in range(4):
                                n = 4 * q4 + j
                                m = mm(PS[b][:, j * 128:j * 128 + 128], WT[:, n, :], X1[:, n, :], True, True, xs[q4], wt_tok, free[b], inc=True)
                            ws = W[:, 4 * q4:4 * q4 + 4, :]
                            w_tok = tt(V, ws, ws, PS[b][:, :].rearrange("p (j t) -> p j t", j=4), ALU.add, m)
                            free[b] = [w_tok]
                        b = bank("side")
                        for j in range(4):
                            n = 4 * q4 + j
                            m = mm(PS[b][:, j * 128:j * 128 + 128], X1[:, n, :], WT[:, n, :], True, True, xs[q4], wt_tok, free[b], inc=True)
                        ws = WT[:, 4 * q4:4 * q4 + 4, :]
                        wt_new = tt(V, ws, ws, PS[b][:, :].rearrange("p (j t) -> p j t", j=4), ALU.add, m)
                        free[b] = [wt_new]
                    wt_tok = wt_new
                    yield
                b = bank("side")
                for j in range(2):
                    for s_, src in enumerate((bt, kt)):
                        m = tr(PS[b][:, (2 * s_ + j) * 128:(2 * s_ + j) * 128 + 128], src[:, 2 * g + j, 0:128], free[b], inc=True)
                bt_tok = cp(A, btT[:, :, :, :].rearrange("p s j k -> p (s j k)"), PS[b][:, :], m)
                free[b] = [bt_tok]
                s_tok = []
                for c_ in range(2):
                    bb = [bank("side"), bank("side")]
                    for i in range(4):
                        h = 4 * g + i
                        p0, f = (h % 2) * 64, h // 2
                        b = bb[i % 2]
                        o = PS[b][:, (i // 2) * 64:(i // 2) * 64 + 64]
                        m = mm(o, TK[:, 2 * i + c_, 0, :], VT[:, c_, h * 64:h * 64 + 64], True, c_ == 0, free[b], V.last(), A.last(), inc=True)
                        if c_ == 1:
                            m = mm(o, AR[p0:p0 + 64, f, 1, 0, :], S0[p0:p0 + 64, f - 2 * g, :], False, True, s_tok, inc=True)
                    for z, b in enumerate(bb):
                        q = cp(V, XU[:, 0, z:4:2, :], PS[b][:, 0:128].rearrange("p (i v) -> p i v", i=2), m)
                        free[b] = [q]
                    yield
                    b = bank("side")
                    for i in range(4):
                        m = mm(PS[b][:, i * 64:i * 64 + 64], WT[:, 2 * i + c_, :], XU[:, 0, i, :], True, True, q, wt_tok, free[b], inc=True)
                    q = cp(V, XU[:, 1, :, :], PS[b][:, 0:256].rearrange("p (i v) -> p i v", i=4), m)
                    free[b] = [q]
                    yield
                    bb = [bank("side"), bank("side")]
                    for i in range(4):
                        h = 4 * g + i
                        p0, f = (h % 2) * 64, h // 2
                        b = bb[i % 2]
                        o = PS[b][:, (i // 2) * 64:(i // 2) * 64 + 64]
                        mm(o, TB[:, 2 * i + c_, 1, :], XU[:, 1, i, :], True, False, q, free[b])
                        m = mm(o, TK[:, 2 * i + c_, 1, :], VT[:, c_, h * 64:h * 64 + 64], False, c_ == 0, inc=True)
                        if c_ == 1:
                            m = mm(o, AR[p0:p0 + 64, f, 1, 1, :], S0[p0:p0 + 64, f - 2 * g, :], False, True, inc=True)
                    for z, b in enumerate(bb):
                        y_tok = cp(A, Y[:, c_, 4 * g + z:4 * g + 4:2, :], PS[b][:, 0:128].rearrange("p (i v) -> p i v", i=2), m)
                        free[b] = [y_tok]
                    if c_ == 0:
                        b = bank("side")
                        for j in range(2):
                            o = PS[b][:, j * 128:j * 128 + 128]
                            mm(o, btT[:, 0, j, :], XU[:, 1, 2 * j:2 * j + 2, :].rearrange("p i v -> p (i v)"), True, False, bt_tok, free[b])
                            m = mm(o, btT[:, 1, j, :], VT[:, 0, (4 * g + 2 * j) * 64:(4 * g + 2 * j + 2) * 64], False, True, inc=True)
                        for j in range(2):
                            for p0 in (0, 64):
                                q = ts(V, S0[p0:p0 + 64, j, :], PS[b][p0:p0 + 64, j * 128 + p0:j * 128 + p0 + 64],
                                       R["esc"][p0:p0 + 64, 2 * g + j:2 * g + j + 1], None, ALU.mult, None, m)
                        free[b] = [q]
                        s_tok = [q]
                    yield
            yv = Y[:, :, :, :].rearrange("p c h v -> p (c h) v")
            mu = SC[0]("mu", [P, 2, 16])
            ysq = W[:, :, :].rearrange("p n t -> p (n t)").rearrange("p (g v) -> p g v", v=64)
            V(lambda e: e.tensor_reduce(mu[:, 0, :], yv, AX.X, ALU.add), y_tok)
            ts(V, mu[:, 0, :], mu[:, 0, :], 1.0 / 64, None, ALU.mult, None)
            v = tt(V, yv, yv, mu[:, 0, :].unsqueeze(2).broadcast_to([P, 16, 64]), ALU.subtract)
            q = act(ysq, yv, ACT.Square, v, T.last())
            v = V(lambda e: e.tensor_reduce(mu[:, 1, :], ysq, AX.X, ALU.add), q)
            q = act(mu[:, 1, :], mu[:, 1, :], ACT.Sqrt, v, scale=1.0 / 64, bias=C("eps", 1, 1))
            V(lambda e: e.reciprocal(mu[:, 1, :], mu[:, 1, :]), q)
            v = tt(V, yv, yv, mu[:, 1, :].unsqueeze(2).broadcast_to([P, 16, 64]), ALU.mult)
            yield
            yT = R["bonus"]
            tmp = WT[:, :, :].rearrange("p n t -> p (n t)").rearrange("p (f t) -> p f t", t=256)
            for f in range(0, 4, 2):
                b = bank("side")
                for j in range(2):
                    for t in range(2):
                        m = tr(PS[b][:, j * 256 + t * 128:j * 256 + t * 128 + 128],
                               Y[:, t, 2 * (f + j):2 * (f + j) + 2, :].rearrange("p h v -> p (h v)"), v, free[b], inc=True)
                for j in range(2):
                    q = act(tmp[:, f + j, :], PS[b][:, j * 256:j * 256 + 256], ACT.Identity, m,
                            scale=vcol("lnx_g", f + j), bias=vcol("lnx_b", f + j))
                free[b] = [q]
            v = tt(V, yT[:, :, :], yT[:, :, :], tmp, ALU.add, q)
            R["yT"] = v
            yield

        def silu_fm(dst, t0):
            def evac(j0, p, m):
                a = act(dst[:, t0 + j0:t0 + j0 + 2, :], p, ACT.Sigmoid, m)
                return tt(V, dst[:, t0 + j0:t0 + j0 + 2, :], dst[:, t0 + j0:t0 + j0 + 2, :], p, ALU.mult, a)
            return evac

        def copy_fm(dst, t0):
            return lambda j0, p, m: cp(V, dst[:, t0 + j0:t0 + j0 + p.shape[1], :], p, m)

        def sig_fm(dst, t0, bias=None):
            def evac(j0, p, m):
                if bias is None:
                    return act(dst[:, t0 + j0:t0 + j0 + 2, :], p, ACT.Sigmoid, m)
                for j in range(2):
                    a = act(dst[:, t0 + j0 + j, :], p[:, j, :], ACT.Sigmoid, m, bias=vcol(bias, t0 + j0 + j))
                return a
            return evac

        def ki_cols(hi, lo):
            def evac(j0, p, m):
                cp(V, kiT[64:128, :], p[64:128, 0, :], m)
                return cp(V, kiT[0:64, :], p[0:64, 1, :])
            fm_tiles(hi, lo, [0, 64], hT, evac)
            b = bank("main")
            for t in range(2):
                for k in range(8):
                    m = mm3(PS[b][:, t * 8:t * 8 + 8], [z[:, k, t * 128:t * 128 + 128] for z in hT],
                            (hi[:, k, 128:136], lo[:, k, 128:136]), k == 0, k == 7, free[b], inc=(k == 7))
            free[b] = [cp(V, wi[:, :, :], PS[b][:, 0:16].rearrange("p (t h) -> p t h", t=2), m)]

        def ckv_cols(hi, lo):
            b = bank("main")
            for t in range(2):
                for k in range(8):
                    m = mm3(PS[b][:, t * 128:t * 128 + 128], [z[:, k, t * 128:t * 128 + 128] for z in hT],
                            (hi[:, k, :], lo[:, k, :]), k == 0, k == 7, free[b], inc=(k == 7))
            free[b] = [cp(V, lat[:, :, :], PS[b][:, 0:256].rearrange("p (t c) -> p t c", t=2), m)]

        DS = [None]

        def dsa():
            RW_done = R["yT"]
            DS[0] = Scope()
            S = DS[0]
            qabs = S("qabs", [P, 8, 256])
            hk = [S("hk0", [P, 8, 128]), S("hk1", [P, 8, 256])]
            sc = [S("sc0", [P, 128]), S("sc1", [P, 256])]
            wk = [S("wk0", [P, 128]), S("wk1", [P, 256])]
            rl = S("rl", [P, 2, 2, 256])
            top = S("top", [P, 8])
            olT = S("olT", [P, 2, 256])
            b = bank("side")
            m = mm(PS[b][0:8, 0:384], relb[:, :], C("hot", rows=32), True, True, t_small, free[b], inc=True)
            q = cp(V, biasv[:, :], PS[b][0:8, 0:384], m)
            free[b] = [q]
            t_b = load(bias_dram, biasv[:, :], s_misc, q)
            for t in range(2):
                n = 128 * (t + 1)
                t_hk = load(hk[t][:, :, :], bass.AP(bias_dram.tensor, 128 * (1 - t), [[1, 128], [384, 8], [1, n]]),
                            s_misc, t_b)
            v = rms_rows(lat, 128, 4, rl[:, 0, 0, 0:128], V.last())
            for t in range(2):
                v = stt(lat[:, t, :], lat[:, t, :], st[:, 4 + t:5 + t], kvg[:, :], ALU.mult, ALU.mult, t_small)
            b = bank("side")
            for t in range(2):
                m = tr(PS[b][:, t * 128:t * 128 + 128], lat[:, t, :], v, free[b], inc=True)
            free[b] = [cp(V, latT[:, :], PS[b][:, 0:256], m)]
            yield
            for h in (0, 1, 4, 5):
                b = bank("side")
                for j in range(2):
                    p0 = (h % 2) * 64
                    m = mm(PS[b][:, j * 256:j * 256 + 256], wukT[p0:p0 + 64, h // 2 + j, :], qT[p0:p0 + 64, h // 2 + j, :],
                           True, True, V.last(), free[b], inc=True)
                free[b] = [act(qabs[:, h:h + 3:2, :], PS[b][:, :].rearrange("p (j t) -> p j t", j=2), ACT.Copy, m, scale=0.125)]
            yield
            rl_free = [[], []]
            for t in range(2):
                n = 128 * (t + 1)
                for h in (0, 1, 4, 5):
                    b = bank("side")
                    z = h % 2
                    for j in range(2):
                        p0 = z * 64
                        m = mm(PS[b][:, j * n:j * n + n], qiT[p0:p0 + 64, h // 2 + j, t * 128:t * 128 + 128],
                               kiT[p0:p0 + 64, 0:n], True, True, free[b], inc=True)
                    r = rl[:, z, :, 0:n]
                    a = act(r, PS[b][:, 0:2 * n].rearrange("p (j k) -> p j k", j=2), ACT.Relu, m, rl_free[z])
                    free[b] = [a]
                    for j in range(2):
                        if h + j == 0:
                            v = ts(V, sc[t][:, :], r[:, 0, :], wi[:, t, 0:1], None, ALU.mult, None, a)
                        else:
                            v = stt(sc[t][:, :], r[:, j, :], wi[:, t, h + 2 * j:h + 2 * j + 1], sc[t][:, :], ALU.mult, ALU.add, a)
                    rl_free[z] = [v]
                    yield
                s, w = sc[t], wk[t]
                tt(V, s[:, n - 128:n], s[:, n - 128:n], C("causal"), ALU.add)
                for i in range(8):
                    src = s if i == 0 else w
                    V(lambda e, src=src: e.max(top[:, :], src[:, :]))
                    V(lambda e, src=src, w=w: e.match_replace(w[:, :], top[:, :], src[:, :], GONE))
                    if i % 4 == 3:
                        yield
                ts(V, w[:, :], w[:, :], -2.0e38, NEG, ALU.is_ge, ALU.mult)
                tt(V, w[:, n - 128:n], w[:, n - 128:n], C("causal"), ALU.add)
            yb = R["yb"]

            def logits(h, t, o):
                n = 128 * (t + 1)
                mm(o, qabs[:, h, t * 128:t * 128 + 128], latT[:, 0:n], True, False, V.last(), A.last(), t_hk)
                return mm(o, C("flip"), hk[t][:, h, :], False, True, inc=True)

            ob = {}
            ol_free = [[], []]

            def outp(h, p, m):
                a = cp(A, olT[:, h % 2, :], p, m, ol_free[h % 2])
                if h % 2 == 0:
                    ob[0] = bank("side")
                b = ob[0]
                p0 = (h % 2) * 64
                k = mm(PS[b][p0:p0 + 64, 0:256], wuv[:, h * 64:h * 64 + 64], olT[:, h % 2, :], True, True, a, free[b], inc=True)
                ol_free[h % 2] = [k]
                if h % 2 == 1:
                    free[b] = [tt(V, yb[:, h // 2, :], PS[b][:, 0:256], zb[:, h // 2, :], ALU.mult, k)]
                return a
            yield from attention(S, "d", list(range(8)), logits, lambda t: wk[t][:, :],
                                 lambda h, kt_: lat[:, kt_, :], (1, 2), outp,
                                 qq[:, :, :].rearrange("p (j k) t -> p j k t", k=2))

        g_rw = rwkv()
        g_ds = dsa()

        def weave(gen, k):
            tasks.append(("do", lambda: [next(gen, None) for _ in range(k)]))

        def col(c0, fn, n=256):
            fmslab(w_in, c0, n, fn)
        weave(g_rw, 1)
        col(2688, ckv_cols, 128)
        weave(g_rw, 2)
        col(2176, lambda hi, lo: fm_tiles(hi, lo, [0, 128], hT, copy_fm(qT, 0)))
        weave(g_rw, 2)
        col(2432, lambda hi, lo: fm_tiles(hi, lo, [0, 128], hT, copy_fm(qT, 2)))
        weave(g_rw, 2)
        col(3328, lambda hi, lo: fm_tiles(hi, lo, [0, 128], hT, copy_fm(qiT, 0)))
        weave(g_rw, 3)
        col(3584, lambda hi, lo: fm_tiles(hi, lo, [0, 128], hT, copy_fm(qiT, 2)))
        weave(g_rw, 3)
        col(3776, ki_cols, 192)
        weave(g_rw, 3)
        for j in range(2):
            col(1664 + 256 * j, lambda hi, lo, j=j: fm_tiles(hi, lo, [0, 128], hT, silu_fm(za, 2 * j)))
            weave(g_rw, 3)
        for j in range(2):
            col(2816 + 256 * j, lambda hi, lo, j=j: fm_tiles(hi, lo, [0, 128], hT, silu_fm(zb, 2 * j)))
            weave(g_rw, 3)
        for j in range(2):
            col(3912 + 256 * j, lambda hi, lo, j=j: fm_tiles(hi, lo, [0, 128], hT, sig_fm(gab, 2 * j)))
            weave(g_rw, 5)
        steps(g_rw)
        YA = {}

        def finish_a():
            SC[0].close()
            v = tt(V, R["bonus"][:, :, :], R["bonus"][:, :, :], za[:, :, :], ALU.mult, R["yT"])
            v = cp(V, za[:, :, :], R["bonus"][:, :, :])
            RW[0].close()
            enter()
            Y_ = Scope()
            YA["scope"] = Y_
            YA["a"] = [Y_("yahi", [P, 4, 256], F32R), Y_("yalo", [P, 4, 256], F32R)]
            YA["b"] = [Y_("ybhi", [P, 4, 256], F32R), Y_("yblo", [P, 4, 256], F32R)]
            split(YA["a"][0][:, :, :], YA["a"][1][:, :, :], za[:, :, :])
            R["yb"] = za
        do(finish_a)
        for j in range(2, 8):
            col(3912 + 256 * j, lambda hi, lo, j=j: fm_tiles(hi, lo, [0, 128], hT, sig_fm(gab, 2 * j)))
            weave(g_ds, 5)

        def pa_slabs(w, key, evac):
            wv = w.rearrange("a r n -> (a r) n")
            for n in range(2):
                slab([(None, wv[:, n * 512:n * 512 + 512].rearrange("(k p) n -> p k n", p=P))],
                     lambda hi, lo, n=n: (T.wait([V.last(), A.last()]) if n == 0 else None,
                                          fm_tiles(hi, lo, [0, 128, 256, 384], YA[key], evac(4 * n), nk=4)), (4, 512))

        def br_a(t0):
            return lambda j0, p, m: tt(V, gab[:, t0 + j0:t0 + j0 + 2, :], gab[:, t0 + j0:t0 + j0 + 2, :], p, ALU.mult, m)
        pa_slabs(I["w_pa"], "a", br_a)
        steps(g_ds)

        def finish_b():
            DS[0].close()
            split(YA["b"][0][:, :, :], YA["b"][1][:, :, :], za[:, :, :], V.last())
        do(finish_b)

        def br_b(t0):
            def evac(j0, p, m):
                f = t0 + j0
                o = gab[:, 8 + f:10 + f, :]
                k = tt(V, o, o, p, ALU.mult, m)
                tt(V, o, o, gab[:, f:f + 2, :], ALU.add)
                split(hT[0][:, f:f + 2, :], hT[1][:, f:f + 2, :], o, V.last(), T.last())
                return k
            return evac
        pa_slabs(I["w_pb"], "b", br_b)
        w_o = I["w_o"].rearrange("a r n -> (a r) n")
        def wo_evac(t0):
            def evac(j0, p, m):
                z = (t0 // 2) % 2
                for j in range(2):
                    v = ts(V, YA["m"][:, z, j, :], p[:, j, :], gate[:, t0 + j:t0 + j + 1], None, ALU.mult, None, m,
                           YA.get(z, []))
                b = bank("side")
                for j in range(2):
                    for t in range(2):
                        m = tr(PS[b][:, t * 256 + j * 128:t * 256 + j * 128 + 128], YA["m"][:, z, j, t * 128:t * 128 + 128],
                               v, free[b], inc=True)
                YA[z] = [m]
                o = x[:, :, t0 * 128:t0 * 128 + 256]
                free[b] = [tt(V, o, o, PS[b][:, :].rearrange("p (t n) -> p t n", t=2), ALU.add, m)]
                return v
            return evac

        def wo_cols(j, hi, lo):
            if j == 0:
                T.wait([V.last(), A.last()])
                YA["m"] = za[:, :, :].rearrange("p (z j) t -> p z j t", z=2)
            fm_tiles(hi, lo, [0, 128], hT, wo_evac(2 * j))
        for j in range(4):
            fmslab(w_o, 256 * j, 256, lambda hi, lo, j=j: wo_cols(j, hi, lo))

        def after_block1():
            r = load_row("final_g", *row_free[0])
            YA["scope"].close()
            v = rms_rows(x, 1024, 0, gab[:, 0:4, :].rearrange("p f t -> p (f t)"), V.last())
            for t in range(2):
                v = stt(x[:, t, :], x[:, t, :], st[:, t:t + 1], row[:, :], ALU.mult, ALU.mult, r)
            row_free[0] = [v]
            B1.close()
            enter()
        do(after_block1)

        def ffn(tag, w_in_, w_down, pre, post):
            wv = w_in_.rearrange("a r n -> (a r) n")
            wd = w_down.rearrange("a r n -> (a r) n")
            L = {}

            def start():
                S = L["S"] = Scope()
                L["aT"] = [S("aThi" + tag, [P, 22, 256], F32R), S("aTlo" + tag, [P, 22, 256], F32R)]
                L["sg"] = S("sg" + tag, [P, 2, 256])
                L["ac"] = S("ac" + tag, [P, 2, 2, 256])
                L["y"] = S("y" + tag, [P, 2, 1024])
                L["pend"] = None
                N = Scope()
                norm_fm(N, x, pre, V.last())
                N.close()
                T.wait(fence())
                for e in (V, A, G):
                    e.wait(fence())
            do(start)

            def turn_over():
                if L["pend"] is None:
                    return
                u, v = L["pend"]
                z = u % 2
                b = bank("side")
                for j in range(2):
                    for t in range(2):
                        m = tr(PS[b][:, j * 256 + t * 128:j * 256 + t * 128 + 128], L["ac"][:, z, t, j * 128:j * 128 + 128],
                               v, free[b], inc=True)
                L["acfree"] = [m]
                p = PS[b][:, :].rearrange("p (j t) -> p j t", j=2)
                hi, lo = (q[:, 2 * u:2 * u + 2, :] for q in L["aT"])
                a = cp(A, hi, p, m)
                free[b] = [tt(V, lo, p, hi, ALU.subtract, a)]
                L["pend"] = None

            for u in range(11):
                def evac(t, p, m, u=u):
                    a = act(L["sg"][:, t, :], p[:, 0:256], ACT.Silu, m)
                    v = tt(V, L["ac"][:, u % 2, t, :], L["sg"][:, t, :], p[:, 256:512], ALU.mult, a, L.get("acfree", []))
                    if t == 1:
                        L["pend2"] = (u, v)
                    return v

                def unit(kh, hi, lo, u=u, ev=evac):
                    tm_out(f"f{tag}{u}", hT, kh * 4, 4, kh == 1, hi, lo, ev)
                    if kh == 0:
                        turn_over()
                    else:
                        L["pend"] = L["pend2"]
                tmslabs(wv, [(256 * u, 256), (2816 + 256 * u, 256)], unit)

            def down(i, hi, lo):
                if i == 0:
                    turn_over()
                    L["bk"] = [bank("main") for _ in range(4)]
                    T.wait([V.last(), A.last()])
                for t in range(2):
                    for n in range(2):
                        b = L["bk"][2 * t + n]
                        for k in range(2):
                            kk = 2 * i + k
                            m = mm3(PS[b][:, :], [z[:, kk, t * 128:t * 128 + 128] for z in L["aT"]],
                                    (hi[:, k, n * 512:n * 512 + 512], lo[:, k, n * 512:n * 512 + 512]), kk == 0, kk == 21,
                                    free[b] if kk == 0 else [], inc=(k == 1))
                        if i == 10:
                            free[b] = [cp(V, L["y"][:, t, n * 512:n * 512 + 512], PS[b][:, :], m)]
            for i in range(11):
                slab([(None, wd[256 * i:256 * i + 256, :].rearrange("(k p) n -> p k n", p=P))],
                     lambda hi, lo, i=i: down(i, hi, lo), (2, 1024))

            def end():
                add_rms(L["S"], L["y"], post, True)
                L["S"].close()
                enter()
            do(end)

        ffn("1", I["ffn1_w_in_2"], I["ffn1_w_down_2"], "ffn1_pre_g_2", "ffn1_post_g_2")

        w2 = I["w_in_2"].rearrange("a r n -> (a r) n")
        Z = {}

        def mix_start():
            S = Z["S"] = Scope()
            H = Z["H"] = Scope()
            for n in ("qb", "kb"):
                Z[n] = S(n, [P, 8, 256])
            Z["vb"] = S("vb", [P, 2, 1024])
            Z["ga"] = S("ga", [P, 8, 256])
            Z["lf"] = S("lf", [8, 4, 256])
            Z["sel"] = S("sel", [8, 8, 128])
            Z["lb"] = S("lb", [P, 2, 8])
            for n in ("b", "q", "k", "E"):
                Z[n] = H("h" + n, [P, 8, 256])
            Z["i"] = H("hi_", [P, 2, 1024])
            N = Scope()
            norm_fm(N, x, "mix_pre_g_2", V.last())
            N.close()
            T.wait(fence())
            for e in (V, A, G):
                e.wait(fence())
            lb = Z["lb"]
            v = tt(V, lb[:, 0, :], vcol("hg_lb_logits_2", 0, 8), vcol("hg_lb_logits_2", 8, 8), ALU.subtract)
            a = act(lb[:, 0, :], lb[:, 0, :], ACT.Sigmoid, v)
            ts(V, lb[:, 1, :], lb[:, 0, :], -1.0, 1.0, ALU.mult, ALU.add, a)
            cp(V, Z["sel"][:, :, :], con[0:8, CON["ident"][0]:CON["ident"][0] + 8].unsqueeze(2).broadcast_to([8, 8, 128]))
        do(mix_start)

        def f_evac(t0):
            def evac(j0, p, m):
                a = act(Z["k"][:, t0:t0 + 2, :], p, ACT.Sigmoid, m)
                for j in range(2):
                    f = t0 + j
                    v = ts(V, Z["E"][:, f, :], Z["k"][:, f, :], Z["lb"][:, 1, f:f + 1], Z["lb"][:, 0, f:f + 1],
                           ALU.mult, ALU.add, a)
                ts(V, Z["k"][:, t0:t0 + 2, :], Z["E"][:, t0:t0 + 2, :], -1.0, 1.0, ALU.mult, ALU.add)
                return a
            return evac
        for j in range(4):
            fmslab(w2, 1024 + 256 * j, 256, lambda hi, lo, j=j: fm_tiles(hi, lo, [0, 128], hT, f_evac(2 * j)))
        for j in range(4):
            fmslab(w2, 256 * j, 256, lambda hi, lo, j=j: fm_tiles(hi, lo, [0, 128], hT, (lambda t0: lambda j0, p, m: silu_fm(Z["q"], t0)(j0, p, m))(2 * j)))

        def tm_copy(key, dst):
            for n in range(2):
                def evac(t, p, m, n=n):
                    return cp(V, dst()[:, t, n * 512:n * 512 + 512], p, m)
                yield n, evac

        for n, ev in tm_copy("i", lambda: Z["i"]):
            tmslabs(w2, [(2048 + 512 * n, 512)], lambda kh, hi, lo, n=n, ev=ev: tm_out(f"i{n}", hT, kh * 4, 4, kh == 1, hi, lo, ev))

        def hgrn():
            b_, q_, k_, E = Z["b"], Z["q"], Z["k"], Z["E"]
            H = Z["H"]
            AD = H("AD", [P, 8, 2, 128])
            AX_ = H("AXc", [P, 8, 128])
            a = act(E[:, :, :], E[:, :, :], ACT.Ln, V.last())
            for f in range(8):
                v = V(lambda e, f=f: e.tensor_tensor_scan(b_[:, f, :], C("reset"), E[:, f, :], 0.0, ALU.mult, ALU.add), a)
            zt = G(lambda e: e.memset(AD[:, :, :, :], 0.0))
            yield
            bv = b_[:, :, :].rearrange("p f t -> p (f t)")
            qv = q_[:, :, :].rearrange("p f t -> p (f t)")
            kv = k_[:, :, :].rearrange("p f t -> p (f t)")
            ev = E[:, :, :].rearrange("p f t -> p (f t)")

            def masked(l, lhs, rhs, tok):
                mask = (ident if l is None else C("off", 128 * l, 128)).bitcast(U32)
                for f in range(0, 8, 2):
                    b = bank("side")
                    for j in range(2):
                        for t in range(2):
                            s = slice(t * 128, t * 128 + 128)
                            m = mm(PS[b][:, (2 * j + t) * 128:(2 * j + t) * 128 + 128], lhs[:, f + j, s], rhs[:, f + j, s],
                                   True, True, tok, free[b], inc=True)
                    o = AD[:, f:f + 2, :, :].rearrange("p j t n -> p (j t) n")
                    c = V(lambda e, o=o, b=b: e.copy_predicated(o, mask.unsqueeze(1).broadcast_to([P, 4, 128]),
                                                                PS[b][:, :].rearrange("p (j n) -> p j n", j=4)), m, zt)
                    free[b] = [c]
                    if f == 2:
                        yield m
                yield m

            for m in masked(None, k_, q_, V.last()):
                yield
            for l in range(8):
                B = 1 << l
                w = T.last()
                if l < 7:
                    pv = bv.rearrange("p (n z) -> p n z", z=2 * B)
                    pe = ev.rearrange("p (n z) -> p n z", z=2 * B)
                    n = 1024 // B
                    ref = pv[:, :, B - 1:B].broadcast_to([P, n, B])
                    tt(V, pe[:, :, 0:B], ref, pv[:, :, 0:B], ALU.subtract, w)
                    v = tt(V, pe[:, :, B:2 * B], pv[:, :, B:2 * B], ref, ALU.subtract)
                    a = act(ev, ev, ACT.Exp, v)
                else:
                    v = tt(V, E[:, :, 0:128], b_[:, :, 127:128].broadcast_to([P, 8, 128]), b_[:, :, 0:128], ALU.subtract, w)
                    pe = E[:, :, :].rearrange("p f (n z) -> p (f n) z", z=256)
                    act(E[:, :, 128:256], b_[:, :, 128:256], ACT.Exp, w)
                    a = act(E[:, :, 0:128], E[:, :, 0:128], ACT.Exp, v)
                    n = 8
                pk = kv.rearrange("p (n z) -> p n z", z=2 * B)
                pq = qv.rearrange("p (n z) -> p n z", z=2 * B)
                tt(V, pe[:, :, 0:B], pe[:, :, 0:B], pk[:, :, 0:B], ALU.mult, a)
                v = tt(V, pe[:, :, B:2 * B], pe[:, :, B:2 * B], pq[:, :, B:2 * B], ALU.mult)
                yield
                if l < 7:
                    for m in masked(l, E, E, v):
                        yield
                else:
                    for f in range(0, 8, 4):
                        b = bank("side")
                        for j in range(4):
                            m = mm(PS[b][:, j * 128:j * 128 + 128], E[:, f + j, 0:128], E[:, f + j, 128:256], True, True,
                                   v, free[b], inc=True)
                        c = cp(V, AX_[:, f:f + 4, :], PS[b][:, :].rearrange("p (j n) -> p j n", j=4), m)
                        free[b] = [c]
                    yield
            o_ = b_[:, :, :].rearrange("p f t -> p (f t)").rearrange("p (t n) -> p t n", t=2)
            i_ = Z["i"]
            for t in range(2):
                for f in range(0, 8, 4):
                    b = bank("side")
                    for j in range(4):
                        h = f + j
                        o = PS[b][:, j * 128:j * 128 + 128]
                        m = mm(o, AD[:, h, t, :], i_[:, t, h * 128:h * 128 + 128], True, t == 0, c, free[b], inc=True)
                        if t == 1:
                            m = mm(o, AX_[:, h, :], i_[:, 0, h * 128:h * 128 + 128], False, True, inc=True)
                    v = cp(V, o_[:, t, f * 128:f * 128 + 512], PS[b][:, :], m)
                    free[b] = [v]
                yield
            junk = E[:, 0:4, :].rearrange("p f t -> p (f t)")
            rms_rows(o_, 1024, 6, junk, v, T.last())
            for t in range(2):
                v = ts(V, o_[:, t, :], o_[:, t, :], st[:, 6 + t:7 + t], None, ALU.mult, None)
            yield
            for f in range(0, 8, 2):
                b = bank("side")
                for j in range(2):
                    for t in range(2):
                        m = tr(PS[b][:, j * 256 + t * 128:j * 256 + t * 128 + 128], o_[:, t, (f + j) * 128:(f + j) * 128 + 128],
                               v, free[b], inc=True)
                for j in range(2):
                    k = stt(Z["ga"][:, f + j, :], PS[b][:, j * 256:j * 256 + 256], vcol("hg_norm_g_2", f + j),
                            Z["ga"][:, f + j, :], ALU.mult, ALU.mult, m)
                free[b] = [k]
            yield

        g_h = hgrn()
        for j in range(4):
            fmslab(w2, 3072 + 256 * j, 256, lambda hi, lo, j=j: fm_tiles(hi, lo, [0, 128], hT, silu_fm(Z["ga"], 2 * j)))
            weave(g_h, 2)

        def scaled(t0):
            return lambda j0, p, m: act(Z["qb"][:, t0:t0 + 2, :], p, ACT.Copy, m, scale=1.0 / math.sqrt(128))
        for j in range(4):
            fmslab(w2, 4096 + 256 * j, 256, lambda hi, lo, j=j: fm_tiles(hi, lo, [0, 128], hT, scaled(2 * j)))
            weave(g_h, 3)
        for j in range(4):
            fmslab(w2, 5120 + 256 * j, 256, lambda hi, lo, j=j: fm_tiles(hi, lo, [0, 128], hT, copy_fm(Z["kb"], 2 * j)))
            weave(g_h, 3)
        for n, ev in tm_copy("v", lambda: Z["vb"]):
            tmslabs(w2, [(6144 + 512 * n, 512)], lambda kh, hi, lo, n=n, ev=ev: tm_out(f"v{n}", hT, kh * 4, 4, kh == 1, hi, lo, ev))
            weave(g_h, 3)

        def fb_cols(hi, lo):
            def evac(j0, p, m):
                lf = Z["lf"]
                xx, t1, nc_ = lf[:, 0, :], lf[:, 1, :], lf[:, 2, :]
                k = act(xx, p[0:8, 0, :], ACT.Identity, m, bias=vec[0:8, VEC["fox_f_bias_2"][0]:VEC["fox_f_bias_2"][0] + 1])
                act(t1, xx, ACT.Abs)
                act(t1, t1, ACT.Exp, scale=-1.0)
                a = act(t1, t1, ACT.Ln, bias=C("one", 0, 1, rows=8))
                stt(xx, xx, 0.0, t1, ALU.min, ALU.subtract, a)
                V(lambda e: e.tensor_tensor_scan(nc_, C("one", rows=8), xx, 0.0, ALU.mult, ALU.add))
                ts(V, lf[:, 3, :], nc_, -1.0, None, ALU.mult, None)
                return k
            fm_tiles(hi, lo, [0], hT, evac)
        fmslab(w2, 7168, 128, fb_cols)
        steps(g_h)

        def end_hgrn():
            Z["H"].close()
            enter()
            F = Z["F"] = Scope()
            Z["gt"] = F("gt", [P, 16, 256])
            Z["oa"] = [F("oahi", [P, 8, 256], F32R), F("oalo", [P, 8, 256], F32R)]
            split(Z["oa"][0][:, :, :], Z["oa"][1][:, :, :], Z["ga"][:, :, :], V.last())
            Z["A"] = Scope()
        do(end_hgrn)

        def fox():
            def logits(h, t, o):
                n = 128 * (t + 1)
                mm(o, Z["qb"][:, h, t * 128:t * 128 + 128], Z["kb"][:, h, 0:n], True, False, V.last(), A.last())
                return mm(o, Z["sel"][:, h, :], Z["lf"][:, 3, 0:n], False, True, inc=True)

            def mask(t):
                return C("causal") if t == 0 else con[:, CON["zero"][0]:CON["zero"][0] + 256]

            def outp(h, p, m):
                return cp(V, Z["ga"][:, h, :], p, m)
            yield from attention(Z["A"], "f", list(range(8)), logits, mask,
                                 lambda h, kt_: Z["vb"][:, kt_, h * 128:h * 128 + 128], (1, 2), outp)
        g_f = fox()

        def sig_gate(t0):
            return lambda j0, p, m: sig_fm(Z["gt"], t0, "b_gate_2")(j0, p, m)
        for j in range(8):
            fmslab(w2, 7176 + 256 * j, 256, lambda hi, lo, j=j: fm_tiles(hi, lo, [0, 128], hT, sig_gate(2 * j)))
            weave(g_f, 2)
        wba = I["w_branch_a_2"].rearrange("a r n -> (a r) n")
        wbb = I["w_branch_b_2"].rearrange("a r n -> (a r) n")

        def br2a(t0):
            def evac(j0, p, m):
                o = Z["gt"][:, t0:t0 + 2, :]
                return tt(V, o, o, p, ALU.mult, m)
            return evac
        for j in range(4):
            fmslab(wba, 256 * j, 256, lambda hi, lo, j=j: (T.wait([A.last(), V.last()]) if j == 0 else None,
                                                           fm_tiles(hi, lo, [0, 128], Z["oa"], br2a(2 * j))))
            weave(g_f, 3)
        steps(g_f)

        def split_b():
            split(Z["oa"][0][:, :, :], Z["oa"][1][:, :, :], Z["ga"][:, :, :], V.last(), T.last())
        do(split_b)

        def br2b(t0):
            def evac(j0, p, m):
                o = Z["gt"][:, 8 + t0:10 + t0, :]
                k = tt(V, o, o, p, ALU.mult, m)
                tt(V, o, o, Z["gt"][:, t0:t0 + 2, :], ALU.add)
                split(hT[0][:, t0:t0 + 2, :], hT[1][:, t0:t0 + 2, :], o, V.last())
                return k
            return evac
        for j in range(4):
            fmslab(wbb, 256 * j, 256, lambda hi, lo, j=j: (T.wait([A.last(), V.last()]) if j == 0 else None,
                                                           fm_tiles(hi, lo, [0, 128], Z["oa"], br2b(2 * j))))
        wout = I["w_out_2"].rearrange("a r n -> (a r) n")

        def yv():
            return Z["ga"][:, :, :].rearrange("p f t -> p (f t)").rearrange("p (t n) -> p t n", t=2)
        for n, ev in tm_copy("wout", yv):
            tmslabs(wout, [(512 * n, 512)], lambda kh, hi, lo, n=n, ev=ev: (
                T.wait([A.last(), V.last()]) if (n, kh) == (0, 0) else None,
                tm_out(f"wout{n}", hT, kh * 4, 4, kh == 1, hi, lo, ev)))

        def mix_end():
            add_rms(Z["A"], yv(), "mix_post_g_2", False)
            Z["A"].close()
            Z["F"].close()
            Z["S"].close()
            enter()
        do(mix_end)

        Q = {}
        wkv = I["w_mkv_2"].rearrange("a r n -> (a r) n")
        wmq = I["w_mq_2"].rearrange("a r n -> (a r) n")
        wmo = I["w_mo_2"].rearrange("a r n -> (a r) n")

        def mem_start():
            S = Q["S"] = Scope()
            Q["k"] = S("mk", [P, 8, 256])
            Q["v"] = S("mv", [P, 2, 1024])
            Q["q"] = S("mq", [P, 8, 256])
            Q["o"] = S("mo", [P, 8, 256])
            Q["oh"] = [S("mohi", [P, 8, 256], F32R), S("molo", [P, 8, 256], F32R)]
            mem = Q["o"][:, :, :].rearrange("p f t -> p (f t)").rearrange("p (t n) -> p t n", t=2)
            t_m = load(mem, I["mem_2"].rearrange("a (t p) d -> p (a t) d", p=P), s_misc, fence())
            N = Scope()
            norm_fm(N, mem, "mem_kv_g_2", t_m)
            N.close()
            for e in (V, A, G, T):
                e.wait(fence())
        do(mem_start)
        for j in range(4):
            fmslab(wkv, 256 * j, 256, lambda hi, lo, j=j: fm_tiles(hi, lo, [0, 128], hT, copy_fm(Q["k"], 2 * j)))
        for n, ev in tm_copy("mv", lambda: Q["v"]):
            tmslabs(wkv, [(1024 + 512 * n, 512)], lambda kh, hi, lo, n=n, ev=ev: tm_out(f"mv{n}", hT, kh * 4, 4, kh == 1, hi, lo, ev))

        def mem_q():
            enter()
            N = Scope()
            norm_fm(N, x, "mem_pre_g_2", V.last())
            N.close()
            for e in (V, A, G, T):
                e.wait(fence())
        do(mem_q)
        for j in range(4):
            fmslab(wmq, 256 * j, 256, lambda hi, lo, j=j: fm_tiles(hi, lo, [0, 128], hT, (
                lambda j0, p, m, j=j: act(Q["q"][:, 2 * j:2 * j + 2, :], p, ACT.Copy, m, scale=1.0 / 16))))

        def mem_attention():
            S = Q["S"]
            z = [S(f"mz{t}", [P, 4, 256]) for t in range(2)]
            pt = S("mpt", [P, 4, 2, 256])
            red = S("mred", [P, 2, 3, 4])
            t0 = [V.last(), A.last()]
            for t in range(2):
                for h0 in (0, 2):
                    b = bank("side")
                    for j in range(2):
                        h = h0 + j
                        for d in range(2):
                            m = mm(PS[b][:, j * 256:j * 256 + 256], Q["q"][:, 2 * h + d, t * 128:t * 128 + 128],
                                   Q["k"][:, 2 * h + d, :], d == 0, d == 1, t0, free[b], inc=(d == 1))
                    free[b] = [cp(V, z[t][:, h0:h0 + 2, :], PS[b][:, :].rearrange("p (j k) -> p j k", j=2), m)]
                mx, sm, rc = (red[:, t, q, :] for q in range(3))
                zt = z[t]
                v = V(lambda e, mx=mx, zt=zt: e.tensor_reduce(mx, zt[:, :, :], AX.X, ALU.max, negate=True))
                for h in range(4):
                    a = act(zt[:, h, :], zt[:, h, :], ACT.Exp, v, bias=red[:, t, 0, h:h + 1], accum_out=red[:, t, 1, h:h + 1])
                V(lambda e, rc=rc, sm=sm: e.reciprocal(rc, sm), a)
                v = tt(V, zt[:, :, :], zt[:, :, :], rc.unsqueeze(2).broadcast_to([P, 4, 256]), ALU.mult)
                for h0 in (0, 2):
                    b = bank("side")
                    for j in range(2):
                        for k in range(2):
                            m = tr(PS[b][:, (2 * j + k) * 128:(2 * j + k) * 128 + 128], zt[:, h0 + j, k * 128:k * 128 + 128],
                                   v, free[b], inc=True)
                    c = cp(V, pt[:, h0:h0 + 2, :, t * 128:t * 128 + 128],
                           PS[b][:, :].rearrange("p (j k q) -> p j k q", j=2, k=2), m)
                    free[b] = [c]
            for f in range(0, 8, 2):
                b = bank("side")
                for j in range(2):
                    for k in range(2):
                        m = mm(PS[b][:, j * 256:j * 256 + 256], Q["v"][:, k, (f + j) * 128:(f + j) * 128 + 128],
                               pt[:, (f + j) // 2, k, :], k == 0, k == 1, c, free[b], inc=(k == 1))
                free[b] = [cp(V, Q["o"][:, f:f + 2, :], PS[b][:, :].rearrange("p (j t) -> p j t", j=2), m)]
            split(Q["oh"][0][:, :, :], Q["oh"][1][:, :, :], Q["o"][:, :, :], V.last())
            T.wait([V.last(), A.last()])
        do(mem_attention)

        def my():
            return Q["o"][:, :, :].rearrange("p f t -> p (f t)").rearrange("p (t n) -> p t n", t=2)
        for n, ev in tm_copy("wmo", my):
            tmslabs(wmo, [(512 * n, 512)], lambda kh, hi, lo, n=n, ev=ev: tm_out(f"wmo{n}", Q["oh"], kh * 4, 4, kh == 1, hi, lo, ev))

        def mem_end():
            add_rms(Q["S"], my(), "mem_post_g_2", False)
            Q["S"].close()
            enter()
        do(mem_end)

        ffn("2", I["ffn2_w_in_2"], I["ffn2_w_down_2"], "ffn2_pre_g_2", "ffn2_post_g_2")

        bias_dram = nc.dram_tensor("bias_scratch", (8, 384), F32, kind="Internal").ap()
        run_tasks()
        t_out = load(out.rearrange("a (t p) d -> p (a t) d", p=P), x[:, :, :], s_out, V.last())
        load.q.wait(t_out, (s_misc, load.count[s_misc.name]))

        block = ctx.enter_context(nc.Block())

        @block.sync
        def _(e):
            load.q.play(e)

        @block.vector
        def _(e):
            V.play(e)

        @block.scalar
        def _(e):
            A.play(e)

        @block.gpsimd
        def _(e):
            G.play(e)

        @block.tensor
        def _(e):
            T.play(e)


DIRECT = ["x", "ada_w", "ada_b", "w_in", "w2", "a2", "kv_norm_g", "w_uk", "w_uv", "w_pa", "w_pb", "w_o", "rel_bias",
          "final_g", "mem_2", "ffn1_w_in_2", "ffn1_w_down_2", "ffn1_post_g_2", "w_in_2", "w_branch_a_2",
          "w_branch_b_2", "w_out_2", "mix_post_g_2", "w_mq_2", "w_mkv_2", "w_mo_2", "mem_post_g_2",
          "ffn2_w_in_2", "ffn2_w_down_2", "ffn2_post_g_2"]


def kernel(**inputs):
    import concourse.bacc as bacc
    from concourse.bass_utils import run_bass_kernel_spmd

    arrays = {}
    for name in DIRECT:
        a = np.asarray(inputs[name])
        if name == "w_uk":
            a = a.reshape(128, 4, 128).transpose(2, 1, 0)
        arrays[name] = np.ascontiguousarray(a)
    vecs = np.zeros((P, NVEC), np.float32)
    for name, (o, w) in VEC.items():
        a = np.asarray(inputs[name]).reshape(-1)
        if name == "fox_f_bias_2":
            vecs[0:8, o] = a
        elif name == "shift_mu" or a.size == 128 * w:
            vecs[:, o:o + w] = a.reshape(w, 128).T
    arrays["vecs"] = vecs
    arrays["consts"] = constants()
    nc = bacc.Bacc("TRN2", target_bir_lowering=False, num_devices=1)
    aps = {n: nc.dram_tensor(f"in_{n}", a.shape, mybir.dt.from_np(a.dtype), kind="ExternalInput").ap()
           for n, a in arrays.items()}
    out = nc.dram_tensor("out_0", (1, 256, 1024), F32, kind="ExternalOutput").ap()
    program(nc, {n: aps[n] for n in DIRECT}, aps["consts"], aps["vecs"], out)
    r = run_bass_kernel_spmd(nc, [{f"in_{n}": a for n, a in arrays.items()}], core_ids=[0])
    return r.results[0]["out_0"]
```

```python
import math
from contextlib import ExitStack

import numpy as np

import concourse.bass as bass
from concourse import mybir

F32 = mybir.dt.float32
F32R = mybir.dt.float32r
U32 = mybir.dt.uint32
ALU = mybir.AluOpType
ACT = mybir.ActivationFunctionType
AX = mybir.AxisListType
P = 128
NRAW, NHL = 3, 3
NEG = -1.0e30
GONE = -3.0e38

VEC = {}
for _n, _w in [("c", 8), ("norm_g", 8), ("ada_b", 24), ("shift_mu", 13), ("w0", 4), ("a0", 4), ("k_k", 4),
               ("k_a", 4), ("r_k", 4), ("lnx_g", 4), ("lnx_b", 4), ("ffn1_pre_g_2", 8), ("mix_pre_g_2", 8),
               ("hg_lb_logits_2", 16), ("hg_norm_g_2", 8), ("b_gate_2", 16), ("mem_pre_g_2", 8),
               ("mem_kv_g_2", 8), ("ffn2_pre_g_2", 8), ("fox_f_bias_2", 1)]:
    VEC[_n] = (sum(w for _, w in VEC.values()), _w)
NVEC = sum(w for _, w in VEC.values())

CON = {}
for _n, _w in [("ident", 128), ("flip", 128), ("strict", 128), ("incl", 128), ("zero", 128), ("causal", 128),
               ("ones64", 128), ("off", 7 * 128), ("reset", 256), ("one", 256), ("eps", 4), ("hot", 384)]:
    CON[_n] = (sum(w for _, w in CON.values()), _w)
NCON = sum(w for _, w in CON.values())


def constants():
    c = np.zeros((P, NCON), np.float32)

    def put(name, a):
        o, w = CON[name]
        c[:a.shape[0], o:o + w] = a
    s, t = np.arange(P)[:, None], np.arange(P)[None, :]
    put("ident", s == t)
    put("flip", s + t == P - 1)
    put("strict", s < t)
    put("incl", s <= t)
    put("causal", np.where(t > s, NEG, 0.0))
    put("ones64", s // 64 == t // 64)
    put("off", np.concatenate([(s // (2 << l) == t // (2 << l)) & ((s >> l) % 2 == 0) & ((t >> l) % 2 == 1)
                               for l in range(7)], axis=1))
    put("reset", np.broadcast_to(np.arange(256) % P != 0, (P, 256)))
    put("one", np.ones((P, 256)))
    put("eps", np.broadcast_to(np.array([1e-6, 64e-5, 4e-6, 0.0]), (P, 4)))
    dist = np.arange(256)
    d = np.maximum(dist, 1).astype(np.float32)
    large = 16 + (np.log(d / np.float32(16)) / np.float32(math.log(8)) * np.float32(16)).astype(np.int32)
    bucket = np.where(dist < 16, dist, np.minimum(large, 31))
    hot = np.zeros((32, 384), np.float32)
    hot[bucket, 255 - dist] = 1.0
    put("hot", hot)
    return c


class Engine:

    def __init__(self, sem, serial):
        self.sem, self.serial, self.n, self.ops, self.seen = sem, serial, 0, [], {}

    def __call__(self, fn, *waits, inc=True):
        if self.serial and self.n:
            waits += (self.last(),)
        self.wait(*waits)
        if inc:
            self.n += 1
        self.ops.append((fn, self.sem if inc else None))
        return (self.sem, self.n)

    def wait(self, *waits):
        for w in waits:
            for sem, v in (w if isinstance(w, list) else [w]):
                if v > self.seen.get(sem.name, 0):
                    self.seen[sem.name] = v
                    self.ops.append((None, (sem, v)))

    def last(self):
        return (self.sem, self.n)

    def play(self, eng):
        for fn, s in self.ops:
            if fn is None:
                eng.wait_ge(*s)
            elif s is None:
                fn(eng)
            elif isinstance(s, tuple):
                fn(eng).then_inc(*s)
            else:
                fn(eng).then_inc(s, 1)


class Loader:

    def __init__(self):
        self.q, self.count = Engine(None, False), {}

    def __call__(self, out, in_, sem, *waits):
        self.q.wait(*waits)
        self.q.ops.append((lambda e: e.dma_start(out, in_), (sem, 16)))
        self.count[sem.name] = self.count.get(sem.name, 0) + 16
        return (sem, self.count[sem.name])


def program(nc, I, consts, vecs, out):
    ctx = ExitStack()
    with ctx:
        def sem(name):
            return ctx.enter_context(nc.semaphore(name))

        class Scope:
            def __init__(self):
                self.es = ExitStack()

            def __call__(self, name, shape, dt=F32):
                return self.es.enter_context(nc.sbuf_tensor(name, shape, dt))

            def close(self):
                self.es.close()

        glob = Scope()
        V, A, G, T = (Engine(sem(n), s) for n, s in
                      [("s_vec", True), ("s_act", True), ("s_pool", True), ("s_pe", False)])
        load = Loader()
        s_const = sem("s_const")
        s_row = sem("s_row")
        s_raw = [sem(f"s_raw{i}") for i in range(NRAW)]
        s_misc = sem("s_misc")
        s_out = sem("s_out")

        con = glob("con", [P, NCON])
        vec = glob("vec", [P, NVEC])
        raw = [glob(f"raw{i}", [P, 2048]) for i in range(NRAW)]
        whi = [glob(f"whi{i}", [P, 2048], F32R) for i in range(NHL)]
        wlo = [glob(f"wlo{i}", [P, 2048], F32R) for i in range(NHL)]
        x = glob("x", [P, 2, 1024])
        hT = [glob("hThi", [P, 8, 256], F32R), glob("hTlo", [P, 8, 256], F32R)]
        row = glob("row", [P, 1024])
        st = glob("st", [P, 16])
        PS = [ctx.enter_context(nc.psum_tensor(f"ps{i}", [P, 512], F32)) for i in range(8)]
        free = [[] for _ in range(8)]
        turn = {"main": 0, "side": 0}
        BANKS = {"main": [0, 1, 2, 3], "side": [4, 5, 6, 7]}

        def bank(kind):
            b = BANKS[kind][turn[kind] % 4]
            turn[kind] += 1
            return b

        def C(name, i=0, w=None, rows=P):
            o, n = CON[name]
            return con[0:rows, o + i:o + (i + w if w else n)]

        def vcol(name, j=0, w=1):
            o = VEC[name][0] + j
            return vec[:, o:o + w]

        ident = C("ident")

        def fence():
            return [e.last() for e in (V, A, G, T)]

        def enter():
            f = fence()
            for e in (V, A, G):
                e.wait(f)
            return f

        def tt(E, o, a, b, op, *w):
            return E(lambda e: e.tensor_tensor(o, a, b, op), *w)

        def ts(E, o, a, s1, s2, op0, op1, *w):
            if op1 is None:
                return E(lambda e: e.tensor_scalar(o, a, s1, None, op0), *w)
            return E(lambda e: e.tensor_scalar(o, a, s1, s2, op0, op1), *w)

        def stt(o, a, s, b, op0, op1, *w):
            return V(lambda e: e.scalar_tensor_tensor(out=o, in0=a, scalar=s, in1=b, op0=op0, op1=op1), *w)

        def act(o, a, f, *w, **kw):
            return A(lambda e: e.activation(o, a, f, **kw), *w)

        def cp(E, o, a, *w):
            if E is A:
                return act(o, a, ACT.Copy, *w)
            return E(lambda e: e.tensor_copy(o, a), *w)

        def mm(o, l, r, start, stop, *w, inc=False, skip=False):
            return T(lambda e: e.matmul(o, l, r, start=start, stop=stop, skip_group_check=skip), *w, inc=inc)

        def mm3(o, l, r, start, stop, *w, inc=False):
            mm(o, l[0], r[0], start, False, *w)
            mm(o, l[0], r[1], False, False)
            return mm(o, l[1], r[0], False, stop, inc=inc)

        def tr(o, a, *w, inc=False):
            return T(lambda e: e.transpose(o, a, ident), *w, inc=inc)

        def split(hi, lo, a, *w):
            t = cp(A, hi, a, *w)
            return tt(V, lo, a, hi, ALU.subtract, t)

        tasks = []

        def slab(parts, fn, shape, plain=False):
            tasks.append(("slab", parts, fn, shape, plain))

        side = [None]

        def beside(gen):
            def go():
                side[0] = gen
            tasks.append(("do", go))

        def finish(gen):
            def go():
                for _ in gen:
                    pass
            tasks.append(("do", go))

        def do(fn):
            tasks.append(("do", fn))

        def fmslab(w, c0, n, fn, plain=False):
            slab([(None, w[:, c0:c0 + n].rearrange("(k p) n -> p k n", p=P))], fn, (8, n), plain)

        def tmslabs(w, cols, fn):
            for kh in range(2):
                parts, o = [], 0
                for c0, n in cols:
                    parts.append(((o, n), w[kh * 512:(kh + 1) * 512, c0:c0 + n].rearrange("(k p) n -> p k n", p=P)))
                    o += n
                slab(parts, lambda hi, lo, kh=kh: fn(kh, hi, lo), (4, o))

        def run_tasks():
            slabs = [t for t in tasks if t[0] == "slab"]
            dma_tok, lo_tok, hi_tok, pe_tok = [None] * len(slabs), [None] * len(slabs), [None] * len(slabs), [None] * len(slabs)

            def view(buf, shape):
                k, n = shape
                return buf[:, 0:k * n].rearrange("p (k n) -> p k n", k=k)

            def release(i):
                if slabs[i][4]:
                    return pe_tok[i] and [pe_tok[i]]
                return lo_tok[i] and [lo_tok[i], hi_tok[i]]

            def fetch(i):
                _, parts, _, shape, _ = slabs[i]
                w = release(i - NRAW) if i >= NRAW else []
                dst = view(raw[i % NRAW], shape)
                for sel, src in parts:
                    d = dst if sel is None else dst[:, :, sel[0]:sel[0] + sel[1]]
                    dma_tok[i] = load(d, src, s_raw[i % NRAW], *w)

            order = [i for i, t in enumerate(slabs) if not t[4]]
            place = {i: n for n, i in enumerate(order)}

            def split_slab(i):
                n = slabs[i][3][0] * slabs[i][3][1]
                c = place[i]
                r, h, l = raw[i % NRAW], whi[c % NHL], wlo[c % NHL]
                w = [pe_tok[order[c - NHL]]] if c >= NHL else []
                hi_tok[i] = cp(A, h[:, 0:n], r[:, 0:n], dma_tok[i], *w)
                lo_tok[i] = tt(G, l[:, 0:n], r[:, 0:n], h[:, 0:n], ALU.subtract, hi_tok[i])

            fetched = done = 0

            def prefetch():
                nonlocal fetched
                while fetched < len(slabs) and (fetched < NRAW or release(fetched - NRAW)):
                    fetch(fetched)
                    fetched += 1

            i = 0
            for t in tasks:
                if t[0] == "do":
                    t[1]()
                    continue
                prefetch()
                while done < min(i + 3, len(slabs)):
                    if not slabs[done][4]:
                        c = place[done]
                        if done >= fetched or (c >= NHL and pe_tok[order[c - NHL]] is None):
                            break
                        split_slab(done)
                        prefetch()
                    done += 1
                sh = t[3]
                if t[4]:
                    T.wait(dma_tok[i])
                    r = t[2](view(raw[i % NRAW], sh))
                else:
                    c = place[i]
                    T.wait(hi_tok[i], lo_tok[i])
                    r = t[2](view(whi[c % NHL], sh), view(wlo[c % NHL], sh))
                for _ in r or ():
                    if side[0] is not None:
                        next(side[0], None)
                pe_tok[i] = T.last()
                i += 1

        def rms_rows(src, n, col, junk, *w, eps=0):
            for t in range(2):
                act(junk, src[:, t, :], ACT.Square, *w, accum_out=st[:, col + t:col + t + 1])
            r = st[:, col:col + 2]
            a = act(r, r, ACT.Sqrt, scale=1.0 / n, bias=C("eps", eps, 1))
            return V(lambda e: e.reciprocal(r, r), a)

        class Ready:

            def __init__(self, hi, lo):
                self.p, self.tok = (hi, lo), [[] for _ in range(hi.shape[1])]

        h_ = Ready(*hT)

        def norm(xn, tmp, src, g, *w, dst=h_, bias=None, scale=None, scaled=True):
            scale = scale or (lambda f: vcol(g, f))

            def rstd(t, junk):
                r = st[:, t:t + 1]
                act(junk, src[:, t, :], ACT.Square, *w, accum_out=r)
                a = act(r, r, ACT.Sqrt, scale=1.0 / 1024, bias=C("eps", 0, 1))
                return V(lambda e: e.reciprocal(r, r), a)
            v = list(w)
            if scaled:
                for t in range(2):
                    rstd(t, xn[:, t, :])
                    v = ts(V, xn[:, t, :], src[:, t, :], st[:, t:t + 1], None, ALU.mult, None)
                    yield
                src_, v = xn, [v]
            else:
                src_ = src
            for f0 in range(0, 8, 2):
                b = bank("side")
                for t in range(2):
                    for f in (f0, f0 + 1):
                        k = tr(PS[b][:, (f - f0) * 256 + t * 128:(f - f0) * 256 + t * 128 + 128],
                               src_[:, t, f * 128:f * 128 + 128], free[b], v, inc=True)
                if bias is None:
                    for f in (f0, f0 + 1):
                        a = act(dst.p[0][:, f, :], PS[b][:, (f - f0) * 256:(f - f0) * 256 + 256], ACT.Copy, k, scale=scale(f))
                for f in (f0, f0 + 1):
                    i = PS[b][:, (f - f0) * 256:(f - f0) * 256 + 256]
                    hi, lo = dst.p[0][:, f, :], dst.p[1][:, f, :]
                    if bias is None:
                        q = stt(lo, i, scale(f), hi, ALU.mult, ALU.subtract, a)
                    else:
                        o = tmp[:, f - f0, :]
                        q = ts(V, o, i, scale(f), bias(f), ALU.mult, ALU.add, k)
                        a = cp(A, hi, o, q)
                        q = tt(V, lo, o, hi, ALU.subtract, a)
                    dst.tok[f] = [a, q]
                free[b] = [q]
                yield
            if not scaled:
                for t in range(2):
                    rstd(t, xn[:, t, :])

        def run(gen):
            for _ in gen:
                pass

        row_free = [[]]

        def load_row(name):
            a = I[name]
            if len(a.shape) == 2:
                a = a.rearrange("a n -> (a n)")
            row_tok[0] = load(row[:, :], a.rearrange("(a n) -> a n", a=1).broadcast_to([P, 1024]), s_row, *row_free[0])

        row_tok = [None]

        def post_evac(y, yg, t, n, p, m):
            c = slice(n * 512, n * 512 + 512)
            v = cp(V, y[:, t, c], p, m)
            tt(G, yg[:, t, c], y[:, t, c], row[:, c], ALU.mult, row_tok[0], v)
            return act(p, p, ACT.Square, v, accum_out=st[:, 8 + 2 * t + n:9 + 2 * t + n])

        def post(yg, t, half):
            a, g = A.last(), G.last()
            r = st[:, 12 + t:13 + t]
            v = tt(V, r, st[:, 8 + 2 * t:9 + 2 * t], st[:, 9 + 2 * t:10 + 2 * t], ALU.add, a)
            q = 4.0 if half else 1.0
            a = act(r, r, ACT.Sqrt, v, scale=q / 1024, bias=C("eps", 2 if half else 0, 1))
            V(lambda e: e.reciprocal(r, r), a)
            row_free[0] = [g]
            return stt(x[:, t, :], yg[:, t, :], r, x[:, t, :], ALU.mult, ALU.add, g)

        def early_sqrt():
            act(st[:, 15:16], C("eps", 0, 1), ACT.Sqrt)

        tm_banks = {}

        def tm_out(key, lhs, kt0, nk, last, hi, lo, evac, kind="main"):
            lhs, tok = lhs.p, lhs.tok
            yield from tm_out_(key, lhs, tok, kt0, nk, last, hi, lo, evac, kind)

        def tm_out_(key, lhs, tok, kt0, nk, last, hi, lo, evac, kind):
            if kt0 == 0:
                tm_banks[key] = [bank(kind), bank(kind)]
            bs = tm_banks[key]
            n = hi.shape[2]
            for t in range(2):
                for k in range(nk):
                    l = [z[:, kt0 + k, t * 128:t * 128 + 128] for z in lhs]
                    end = last and k == nk - 1
                    m = mm3(PS[bs[t]][:, 0:n], l, (hi[:, k, :], lo[:, k, :]), kt0 + k == 0, end,
                            *(free[bs[t]] if kt0 + k == 0 else []), tok[kt0 + k], inc=(k == nk - 1))
                if last:
                    free[bs[t]] = [evac(t, PS[bs[t]][:, 0:n], m)]
                yield

        def fm_tiles(hi, lo, cols, rhs, evac, nk=8, kind="main"):
            for j0 in range(0, len(cols), 2):
                b = bank(kind)
                part = cols[j0:j0 + 2]
                for j, c0 in enumerate(part):
                    for k in range(nk):
                        m = mm3(PS[b][:, j * 256:j * 256 + 256], (hi[:, k, c0:c0 + 128], lo[:, k, c0:c0 + 128]),
                                (rhs.p[0][:, k, :], rhs.p[1][:, k, :]), k == 0, k == nk - 1, free[b], rhs.tok[k],
                                inc=(k == nk - 1))
                        if k == 3 or (k == 7 and j + 1 < len(part)):
                            yield
                free[b] = [evac(j0, PS[b][:, 0:256 * len(part)].rearrange("p (j t) -> p j t", t=256), m)]
                yield

        def attention(S, tag, heads, logits, mask, vt, nkt, outp, pt=None):
            z = [S(f"z{t}{tag}", [P, 4, 128 * nkt[t]]) for t in range(2)]
            if pt is None:
                pt = S(f"pt{tag}", [P, 4, 2, 256])
            red = S(f"red{tag}", [P, 2, 3, 4])
            pt_free = []
            for g in range(0, len(heads), 4):
                for t in range(2):
                    n = 128 * nkt[t]
                    for h0 in range(0, 4, 2):
                        b = bank("side")
                        T.wait(free[b])
                        for j in range(2):
                            k = logits(heads[g + h0 + j], t, PS[b][:, j * n:(j + 1) * n])
                        i = PS[b][:, 0:2 * n].rearrange("p (j k) -> p j k", j=2)
                        m = mask(t)
                        if m is None:
                            v = cp(V, z[t][:, h0:h0 + 2, :], i, k, pt_free)
                        else:
                            v = tt(V, z[t][:, h0:h0 + 2, :], i, m.unsqueeze(1).broadcast_to([P, 2, n]), ALU.add, k, pt_free)
                        free[b] = [v]
                        yield
                    mx, sm, rc = (red[:, t, q, :] for q in range(3))
                    zt = z[t]
                    v = V(lambda e, mx=mx, zt=zt: e.tensor_reduce(mx, zt[:, :, :], AX.X, ALU.max, negate=True))
                    for h in range(4):
                        a = act(zt[:, h, :], zt[:, h, :], ACT.Exp, v, bias=red[:, t, 0, h:h + 1],
                                accum_out=red[:, t, 1, h:h + 1])
                    V(lambda e, rc=rc, sm=sm: e.reciprocal(rc, sm), a)
                    v = tt(V, zt[:, :, :], zt[:, :, :], rc.unsqueeze(2).broadcast_to([P, 4, n]), ALU.mult)
                    yield
                    for h0 in range(0, 4, 4 // nkt[t]):
                        b = bank("side")
                        nh = 4 // nkt[t]
                        for j in range(nh):
                            for k in range(nkt[t]):
                                m = tr(PS[b][:, (j * nkt[t] + k) * 128:(j * nkt[t] + k) * 128 + 128],
                                       zt[:, h0 + j, k * 128:k * 128 + 128], v, free[b], inc=True)
                        o = pt[:, h0:h0 + nh, 0:nkt[t], t * 128:t * 128 + 128]
                        i = PS[b][:, :].rearrange("p (j k q) -> p j k q", j=nh, k=nkt[t])
                        c = cp(V, o, i, m, pt_free)
                        free[b] = [c]
                    yield
                for j in range(4):
                    h = heads[g + j]
                    b = bank("side")
                    if nkt[0] == 2:
                        mm(PS[b][:, 0:256], vt(h, 0), pt[:, j, 0, :], True, False, c, free[b])
                        m = mm(PS[b][:, 0:256], vt(h, 1), pt[:, j, 1, :], False, True, inc=True)
                    else:
                        mm(PS[b][:, 0:256], vt(h, 0), pt[:, j, 0, :], True, False, c, free[b])
                        m = mm(PS[b][:, 128:256], vt(h, 1), pt[:, j, 1, 128:256], False, True, inc=True)
                    free[b] = [outp(h, PS[b][:, 0:256], m)]
                    yield
                pt_free = [m]

        t_con = [load(con[:, :], consts, s_const), load(vec[:, :], vecs, s_const),
                 load(x[:, :, :], I["x"].rearrange("a (t p) d -> p (a t) d", p=P), s_const)][-1]
        for e in (V, A, G, T):
            e.wait(t_con)

        B1 = Scope()
        za = B1("za", [P, 4, 256])
        zb = B1("zb", [P, 4, 256])
        qq = B1("qq", [P, 8, 256])
        qT, qiT = qq[:, 0:4, :], qq[:, 4:8, :]
        kiT = B1("kiT", [P, 256])
        lat = B1("lat", [P, 2, 128])
        latT = B1("latT", [P, 256])
        wi = B1("wi", [P, 2, 8])
        gab = B1("gab", [P, 16, 256])
        gate = B1("gate", [P, 8])
        w2a2 = B1("w2a2", [P, 512])
        wukT = B1("wukT", [P, 4, 128])
        wuv = B1("wuv", [P, 512])
        kvg = B1("kvg", [P, 128])
        relb = B1("relb", [32, 8])
        biasv = B1("biasv", [8, 384])
        t_small = [load(w2a2[0:64, :], I["w2"].rearrange("a r n -> (a r) n"), s_misc),
                   load(w2a2[64:128, :], I["a2"].rearrange("a r n -> (a r) n"), s_misc),
                   load(wukT[:, :, :], I["w_uk"], s_misc),
                   load(wuv[:, :], I["w_uv"].rearrange("a c h d -> (a c) (h d)"), s_misc),
                   load(kvg[:, :], I["kv_norm_g"].broadcast_to([P, 128]), s_misc),
                   load(relb[:, :], I["rel_bias"], s_misc)][-1]

        M1 = Scope()
        cs = M1("cs", [P, 8])
        mod = M1("mod", [P, 16])
        xn0 = M1("xn0", [P, 2, 1024])
        tmp0 = M1("tmp0", [P, 2, 256])
        hsc = M1("hsc", [P, 8])
        S = M1
        a = act(cs[:, :], vcol("c", 0, 8), ACT.Sigmoid)
        v = tt(V, cs[:, :], cs[:, :], vcol("c", 0, 8), ALU.mult, a)
        t_c = [v]
        bmod = 7
        ada = I["ada_w"].rearrange("a r n -> (a r) n")

        def ada_cols(j, w):
            T.wait(t_c)
            if j == 8:
                T.wait(free[bmod])
            for f in range(2):
                for k in range(8):
                    m = mm(PS[bmod][:, 2 * j + f:2 * j + f + 1], w[:, k, f * 128:f * 128 + 128], cs[:, k:k + 1],
                           k == 0, k == 7, inc=(k == 7))
            if j == 7:
                v = tt(V, mod[:, 0:16], PS[bmod][:, 0:16], vcol("ada_b", 0, 16), ALU.add, m)
                stt(hsc[:, :], mod[:, 8:16], 1.0, vcol("norm_g", 0, 8), ALU.add, ALU.mult)
                free[bmod] = [v]
            if j == 11:
                free[bmod] = [tt(V, gate[:, :], PS[bmod][:, 16:24], vcol("ada_b", 16, 8), ALU.add, m)]

        for j in range(8):
            fmslab(ada, 256 * j, 256, lambda w, j=j: ada_cols(j, w), True)
        g_n = norm(xn0, tmp0, x, "norm_g", t_con, bias=lambda f: mod[:, f:f + 1], scale=lambda f: hsc[:, f:f + 1])
        finish(g_n)
        for j in range(8, 12):
            fmslab(ada, 256 * j, 256, lambda w, j=j: ada_cols(j, w), True)

        w_in = I["w_in"].rearrange("a r n -> (a r) n")
        RW = [None]
        SC = [None]
        R = {}

        def open_rwkv():
            M1.close()
            f = enter()
            RW[0] = Scope()
            SC[0] = Scope()
            for n in ("AR",):
                R[n] = RW[0](n, [P, 4, 2, 2, 128])
            for n in ("bt", "kt", "bonus"):
                R[n] = RW[0](n, [P, 4, 256])
            R["VT"] = RW[0]("VT", [P, 2, 512])
            R["Y"] = gab[:, 12:16, :].rearrange("p f t -> p (f t)").rearrange("p (c h v) -> p c h v", c=2, v=64)
            R["esc"] = RW[0]("esc", [P, 4])
            R["rkv"] = SC[0]("rkv", [P, 13, 256])
            for n in ("c", "lw", "a", "kkn"):
                R[n] = SC[0](n, [P, 4, 256])
            R["mid"] = SC[0]("mid", [P, 8])
            R["u"] = R["AR"][:, 0:2, :, :, :].rearrange("p a b c d -> p (a b c d)").rearrange("p (z j t) -> p z j t", z=2, j=2)
            R["d"] = R["AR"][:, 2:4, :, :, :].rearrange("p a b c d -> p (a b c d)").rearrange("p (z j t) -> p z j t", z=2, j=2)
        do(open_rwkv)

        def shifted(t0):
            def evac(j0, p, m):
                n = p.shape[1]
                z = ((t0 + j0) // 2) % 2
                u, d = R["u"][:, z, 0:n, :], R["d"][:, z, 0:n, :]
                a = cp(A, u, p, m, V.last())
                tt(V, d[:, :, 1:256], u[:, :, 0:255], u[:, :, 1:256], ALU.subtract, a)
                v = ts(V, d[:, :, 0:1], u[:, :, 0:1], -1.0, None, ALU.mult, None)
                for j in range(n):
                    f = t0 + j0 + j
                    v = stt(R["rkv"][:, f, :], d[:, j, :], vcol("shift_mu", f), u[:, j, :], ALU.mult, ALU.add)
                return a
            return evac

        for j in range(6):
            fmslab(w_in, 256 * j, 256, lambda hi, lo, j=j: fm_tiles(hi, lo, [0, 128], h_, shifted(2 * j)))
        fmslab(w_in, 1536, 128, lambda hi, lo: fm_tiles(hi, lo, [0], h_, shifted(12)))

        def rwkv():
            r, k, v_, wa = R["rkv"][:, 0:4, :], R["rkv"][:, 4:8, :], R["rkv"][:, 8:12, :], R["rkv"][:, 12, :]
            AR, bt, kt, c, lw, a, kkn = (R[n] for n in ("AR", "bt", "kt", "c", "lw", "a", "kkn"))
            sq = kt
            t = act(wa[0:64, :], wa[0:64, :], ACT.Tanh, V.last())
            for dst, p0, cb in ((lw, 0, "w0"), (a, 64, "a0")):
                for f in range(0, 4, 2):
                    b = bank("side")
                    for j in range(2):
                        m = mm(PS[b][:, j * 256:j * 256 + 256], w2a2[p0:p0 + 64, (f + j) * 128:(f + j) * 128 + 128],
                               wa[p0:p0 + 64, :], True, True, t, t_small, free[b], inc=True)
                    for j in range(2):
                        q = act(dst[:, f + j, :], PS[b][:, j * 256:j * 256 + 256], ACT.Sigmoid, m, bias=vcol(cb, f + j))
                    free[b] = [q]
            yield
            for f in range(4):
                s = act(sq[:, f, :], k[:, f, :], ACT.Square, scale=vcol("k_k", f))
            for f in range(4):
                ts(V, kkn[:, f, :], k[:, f, :], vcol("k_k", f), None, ALU.mult, None)
            ts(V, lw[:, :, :], lw[:, :, :], -math.exp(-0.5), None, ALU.mult, None, q)
            for f in range(4):
                V(lambda e, f=f: e.tensor_tensor_scan(c[:, f, :], C("reset"), lw[:, f, :], 0.0, ALU.mult, ALU.add))
            for f in range(0, 4, 2):
                b = bank("side")
                for j in range(2):
                    m = mm(PS[b][:, j * 256:j * 256 + 256], C("ones64"), sq[:, f + j, :], True, True, s, free[b], inc=True)
                q = act(bt[:, f:f + 2, :], PS[b][:, :].rearrange("p (j t) -> p j t", j=2), ACT.Sqrt, m)
                free[b] = [q]
            yield
            ts(V, bt[:, :, :], bt[:, :, :], 1e-12, None, ALU.max, None, q)
            V(lambda e: e.reciprocal(bt[:, :, :], bt[:, :, :]))
            tt(V, kkn[:, :, :], kkn[:, :, :], bt[:, :, :], ALU.mult)
            for f in range(4):
                ts(V, bt[:, f, :], a[:, f, :], -1.0, vcol("k_a", f), ALU.add, ALU.mult)
            stt(k, bt[:, :, :], 1.0, k, ALU.add, ALU.mult)
            yield
            for f in range(4):
                v = stt(sq[:, f, :], r[:, f, :], vcol("r_k", f), k[:, f, :], ALU.mult, ALU.mult, T.last())
            for f in range(0, 4, 2):
                b = bank("side")
                for j in range(2):
                    m = mm(PS[b][:, j * 256:j * 256 + 256], C("ones64"), sq[:, f + j, :], True, True, v, free[b], inc=True)
                free[b] = [tt(V, R["bonus"][:, f:f + 2, :], PS[b][:, :].rearrange("p (j t) -> p j t", j=2),
                              v_[:, f:f + 2, :], ALU.mult, m)]
            for t in range(2):
                b = bank("side")
                for f in range(4):
                    m2 = tr(PS[b][:, f * 128:f * 128 + 128], v_[:, f, t * 128:t * 128 + 128], free[b], inc=True)
                free[b] = [cp(A, R["VT"][:, t, :], PS[b][:, :], m2)]
            yield
            cv = c[:, :, :].rearrange("p f (c t) -> p (f c) t", c=2)
            cp(V, R["mid"][:, :], cv[:, :, 63])
            tt(V, cv, cv, R["mid"][:, :].unsqueeze(2).broadcast_to([P, 8, 128]), ALU.subtract)
            v = tt(V, lw[:, :, :], c[:, :, :], lw[:, :, :], ALU.subtract)
            mid = R["mid"][:, :].rearrange("p (f c) -> p f c", c=2)
            v = tt(V, R["esc"][:, :], c[:, :, 127], mid[:, :, 1], ALU.add)
            ARv = AR[:, :, :, :, :].rearrange("p f c a t -> p (f c) a t")
            act(R["esc"][:, :], R["esc"][:, :], ACT.Exp, v)
            a0 = act(ARv[:, :, 0, :], lw[:, :, :].rearrange("p f (c t) -> p (f c) t", c=2), ACT.Exp)
            a1 = act(ARv[:, :, 1, :], cv, ACT.Exp)
            a2 = act(kt[:, :, :], c[:, :, :], ACT.Exp, m, scale=-1.0)
            tt(V, bt[:, :, :], kkn[:, :, :], a[:, :, :], ALU.mult)
            stt(ARv[:, :, 0, :], ARv[:, :, 0, :], -1.0, kkn[:, :, :].rearrange("p f (c t) -> p (f c) t", c=2),
                ALU.mult, ALU.mult, a0)
            tt(V, ARv[:, :, 1, :], ARv[:, :, 1, :], r.rearrange("p f (c t) -> p (f c) t", c=2), ALU.mult, a1)
            tt(V, bt[:, :, :], bt[:, :, :], kt[:, :, :], ALU.mult, a2)
            v = tt(V, kt[:, :, :], kt[:, :, :], k, ALU.mult)
            yield
            SC[0].close()
            enter()
            SC[0] = Scope()
            NM = 8
            TB = SC[0]("TB", [P, NM, 2, 128])
            TK = SC[0]("TK", [P, NM, 2, 128])
            W = SC[0]("W", [P, NM, 128])
            WT = SC[0]("WT", [P, NM, 128])
            X1 = gab[:, 8:12, :].rearrange("p f t -> p (f t)").rearrange("p (n t) -> p n t", t=128)
            OF = gab[:, 4:8, :].rearrange("p f t -> p (f t)").rearrange("p (n t) -> p n t", t=128)
            XU = SC[0]("XU", [P, 2, 4, 64])
            S0 = SC[0]("S0", [P, 2, 64])
            btT = SC[0]("btT", [P, 2, 2, 128])
            G(lambda e: e.memset(TB[:, :, :, :], 0.0))
            zt = G(lambda e: e.memset(TK[:, :, :, :], 0.0))
            tri = con[:, CON["strict"][0]:CON["strict"][0] + 256].bitcast(U32)
            VT, Y = R["VT"], R["Y"]
            for g in range(2):
                war = T.last()
                for src, dst in ((bt, TB), (kt, TK)):
                    for i in range(4):
                        h = 4 * g + i
                        p0, f = (h % 2) * 64, h // 2
                        b = bank("side")
                        for c_ in range(2):
                            m = mm(PS[b][:, c_ * 256:c_ * 256 + 256], src[p0:p0 + 64, f, c_ * 128:c_ * 128 + 128],
                                   AR[p0:p0 + 64, f, c_, :, :].rearrange("p a t -> p (a t)"), True, True, v, free[b], inc=True)
                        o = dst[:, 2 * i:2 * i + 2, :, :].rearrange("p c a t -> p c (a t)")
                        q = V(lambda e, o=o, b=b: e.copy_predicated(
                            o, tri.unsqueeze(1).broadcast_to([P, 2, 256]), PS[b][:, :].rearrange("p (c n) -> p c n", c=2)),
                            m, zt, war)
                        free[b] = [q]
                    yield
                off = lambda l: C("off", 128 * l, 128).unsqueeze(1).broadcast_to([P, NM, 128])
                idb = ident.unsqueeze(1).broadcast_to([P, NM, 128])
                TT = TB[:, :, 0, :]
                o_tok = tt(V, OF[:, :, :], TT, off(0), ALU.mult, T.last())
                wt_tok = tt(V, WT[:, :, :], OF[:, :, :], idb, ALU.add)
                w_tok = None
                for q4 in range(2):
                    b = bank("side")
                    for j in range(4):
                        m = mm(PS[b][:, j * 128:j * 128 + 128], OF[:, 4 * q4 + j, :], ident, True, True, o_tok, free[b], inc=True)
                    w_tok = tt(V, W[:, 4 * q4:4 * q4 + 4, :], PS[b][:, :].rearrange("p (j t) -> p j t", j=4),
                               ident.unsqueeze(1).broadcast_to([P, 4, 128]), ALU.add, m)
                    free[b] = [w_tok]
                yield
                for l in range(1, 7):
                    o_tok = tt(V, OF[:, :, :], TT, off(l), ALU.mult, m)
                    xs = []
                    for q4 in range(2):
                        b = bank("side")
                        for j in range(4):
                            n = 4 * q4 + j
                            m = mm(PS[b][:, j * 128:j * 128 + 128], OF[:, n, :], W[:, n, :], True, True, o_tok, w_tok, free[b], inc=True)
                        q = cp(A, X1[:, 4 * q4:4 * q4 + 4, :], PS[b][:, :].rearrange("p (j t) -> p j t", j=4), m)
                        free[b] = [q]
                        xs.append(q)
                    yield
                    for q4 in range(2):
                        if l < 6:
                            b = bank("side")
                            for j in range(4):
                                n = 4 * q4 + j
                                m = mm(PS[b][:, j * 128:j * 128 + 128], WT[:, n, :], X1[:, n, :], True, True, xs[q4], wt_tok, free[b], inc=True)
                            ws = W[:, 4 * q4:4 * q4 + 4, :]
                            w_tok = tt(V, ws, ws, PS[b][:, :].rearrange("p (j t) -> p j t", j=4), ALU.add, m)
                            free[b] = [w_tok]
                        b = bank("side")
                        for j in range(4):
                            n = 4 * q4 + j
                            m = mm(PS[b][:, j * 128:j * 128 + 128], X1[:, n, :], WT[:, n, :], True, True, xs[q4], wt_tok, free[b], inc=True)
                        ws = WT[:, 4 * q4:4 * q4 + 4, :]
                        wt_new = tt(V, ws, ws, PS[b][:, :].rearrange("p (j t) -> p j t", j=4), ALU.add, m)
                        free[b] = [wt_new]
                    wt_tok = wt_new
                    yield
                b = bank("side")
                for j in range(2):
                    for s_, src in enumerate((bt, kt)):
                        m = tr(PS[b][:, (2 * s_ + j) * 128:(2 * s_ + j) * 128 + 128], src[:, 2 * g + j, 0:128], free[b], inc=True)
                bt_tok = cp(A, btT[:, :, :, :].rearrange("p s j k -> p (s j k)"), PS[b][:, :], m)
                free[b] = [bt_tok]
                s_tok = []
                for c_ in range(2):
                    bb = [bank("side"), bank("side")]
                    for i in range(4):
                        h = 4 * g + i
                        p0, f = (h % 2) * 64, h // 2
                        b = bb[i % 2]
                        o = PS[b][:, (i // 2) * 64:(i // 2) * 64 + 64]
                        m = mm(o, TK[:, 2 * i + c_, 0, :], VT[:, c_, h * 64:h * 64 + 64], True, c_ == 0, free[b], V.last(), A.last(), inc=True)
                        if c_ == 1:
                            m = mm(o, AR[p0:p0 + 64, f, 1, 0, :], S0[p0:p0 + 64, f - 2 * g, :], False, True, s_tok, inc=True)
                    for z, b in enumerate(bb):
                        q = cp(V, XU[:, 0, z:4:2, :], PS[b][:, 0:128].rearrange("p (i v) -> p i v", i=2), m)
                        free[b] = [q]
                    yield
                    b = bank("side")
                    for i in range(4):
                        m = mm(PS[b][:, i * 64:i * 64 + 64], WT[:, 2 * i + c_, :], XU[:, 0, i, :], True, True, q, wt_tok, free[b], inc=True)
                    q = cp(V, XU[:, 1, :, :], PS[b][:, 0:256].rearrange("p (i v) -> p i v", i=4), m)
                    free[b] = [q]
                    yield
                    bb = [bank("side"), bank("side")]
                    for i in range(4):
                        h = 4 * g + i
                        p0, f = (h % 2) * 64, h // 2
                        b = bb[i % 2]
                        o = PS[b][:, (i // 2) * 64:(i // 2) * 64 + 64]
                        mm(o, TB[:, 2 * i + c_, 1, :], XU[:, 1, i, :], True, False, q, free[b])
                        m = mm(o, TK[:, 2 * i + c_, 1, :], VT[:, c_, h * 64:h * 64 + 64], False, c_ == 0, inc=True)
                        if c_ == 1:
                            m = mm(o, AR[p0:p0 + 64, f, 1, 1, :], S0[p0:p0 + 64, f - 2 * g, :], False, True, inc=True)
                    for z, b in enumerate(bb):
                        y_tok = cp(A, Y[:, c_, 4 * g + z:4 * g + 4:2, :], PS[b][:, 0:128].rearrange("p (i v) -> p i v", i=2), m)
                        free[b] = [y_tok]
                    if c_ == 0:
                        b = bank("side")
                        for j in range(2):
                            o = PS[b][:, j * 128:j * 128 + 128]
                            mm(o, btT[:, 0, j, :], XU[:, 1, 2 * j:2 * j + 2, :].rearrange("p i v -> p (i v)"), True, False, bt_tok, free[b])
                            m = mm(o, btT[:, 1, j, :], VT[:, 0, (4 * g + 2 * j) * 64:(4 * g + 2 * j + 2) * 64], False, True, inc=True)
                        for j in range(2):
                            for p0 in (0, 64):
                                q = ts(V, S0[p0:p0 + 64, j, :], PS[b][p0:p0 + 64, j * 128 + p0:j * 128 + p0 + 64],
                                       R["esc"][p0:p0 + 64, 2 * g + j:2 * g + j + 1], None, ALU.mult, None, m)
                        free[b] = [q]
                        s_tok = [q]
                    yield
            yv = Y[:, :, :, :].rearrange("p c h v -> p (c h) v")
            mu = SC[0]("mu", [P, 2, 16])
            ysq = W[:, :, :].rearrange("p n t -> p (n t)").rearrange("p (g v) -> p g v", v=64)
            V(lambda e: e.tensor_reduce(mu[:, 0, :], yv, AX.X, ALU.add), y_tok)
            ts(V, mu[:, 0, :], mu[:, 0, :], 1.0 / 64, None, ALU.mult, None)
            v = tt(V, yv, yv, mu[:, 0, :].unsqueeze(2).broadcast_to([P, 16, 64]), ALU.subtract)
            q = act(ysq, yv, ACT.Square, v, T.last())
            v = V(lambda e: e.tensor_reduce(mu[:, 1, :], ysq, AX.X, ALU.add), q)
            q = act(mu[:, 1, :], mu[:, 1, :], ACT.Sqrt, v, scale=1.0 / 64, bias=C("eps", 1, 1))
            V(lambda e: e.reciprocal(mu[:, 1, :], mu[:, 1, :]), q)
            v = tt(V, yv, yv, mu[:, 1, :].unsqueeze(2).broadcast_to([P, 16, 64]), ALU.mult)
            yield
            yT = R["bonus"]
            tmp = WT[:, :, :].rearrange("p n t -> p (n t)").rearrange("p (f t) -> p f t", t=256)
            for f in range(0, 4, 2):
                b = bank("side")
                for j in range(2):
                    for t in range(2):
                        m = tr(PS[b][:, j * 256 + t * 128:j * 256 + t * 128 + 128],
                               Y[:, t, 2 * (f + j):2 * (f + j) + 2, :].rearrange("p h v -> p (h v)"), v, free[b], inc=True)
                for j in range(2):
                    q = act(tmp[:, f + j, :], PS[b][:, j * 256:j * 256 + 256], ACT.Identity, m,
                            scale=vcol("lnx_g", f + j), bias=vcol("lnx_b", f + j))
                free[b] = [q]
            v = tt(V, yT[:, :, :], yT[:, :, :], tmp, ALU.add, q)
            R["yT"] = v
            yield

        def silu_fm(dst, t0):
            def evac(j0, p, m):
                a = act(dst[:, t0 + j0:t0 + j0 + 2, :], p, ACT.Sigmoid, m)
                return tt(V, dst[:, t0 + j0:t0 + j0 + 2, :], dst[:, t0 + j0:t0 + j0 + 2, :], p, ALU.mult, a)
            return evac

        def copy_fm(dst, t0):
            return lambda j0, p, m: cp(V, dst[:, t0 + j0:t0 + j0 + p.shape[1], :], p, m)

        def sig_fm(dst, t0, bias=None):
            def evac(j0, p, m):
                if bias is None:
                    return act(dst[:, t0 + j0:t0 + j0 + 2, :], p, ACT.Sigmoid, m)
                for j in range(2):
                    a = act(dst[:, t0 + j0 + j, :], p[:, j, :], ACT.Sigmoid, m, bias=vcol(bias, t0 + j0 + j))
                return a
            return evac

        def ki_cols(hi, lo):
            def evac(j0, p, m):
                cp(V, kiT[64:128, :], p[64:128, 0, :], m)
                return cp(V, kiT[0:64, :], p[0:64, 1, :])
            yield from fm_tiles(hi, lo, [0, 64], h_, evac)
            b = bank("main")
            for t in range(2):
                for k in range(8):
                    m = mm3(PS[b][:, t * 8:t * 8 + 8], [z[:, k, t * 128:t * 128 + 128] for z in hT],
                            (hi[:, k, 128:136], lo[:, k, 128:136]), k == 0, k == 7, free[b], inc=(k == 7))
            free[b] = [cp(V, wi[:, :, :], PS[b][:, 0:16].rearrange("p (t h) -> p t h", t=2), m)]

        def ckv_cols(hi, lo):
            b = bank("main")
            for t in range(2):
                for k in range(8):
                    m = mm3(PS[b][:, t * 128:t * 128 + 128], [z[:, k, t * 128:t * 128 + 128] for z in hT],
                            (hi[:, k, :], lo[:, k, :]), k == 0, k == 7, free[b], inc=(k == 7))
            free[b] = [cp(V, lat[:, :, :], PS[b][:, 0:256].rearrange("p (t c) -> p t c", t=2), m)]

        DS = [None]

        def dsa():
            RW_done = R["yT"]
            DS[0] = Scope()
            S = DS[0]
            qabs = S("qabs", [P, 8, 256])
            hk = [S("hk0", [P, 8, 128]), S("hk1", [P, 8, 256])]
            sc = [S("sc0", [P, 128]), S("sc1", [P, 256])]
            wk = [S("wk0", [P, 128]), S("wk1", [P, 256])]
            rl = S("rl", [P, 2, 2, 256])
            top = S("top", [P, 8])
            olT = S("olT", [P, 2, 256])
            b = bank("side")
            m = mm(PS[b][0:8, 0:384], relb[:, :], C("hot", rows=32), True, True, t_small, free[b], inc=True)
            q = cp(V, biasv[:, :], PS[b][0:8, 0:384], m)
            free[b] = [q]
            t_b = load(bias_dram, biasv[:, :], s_misc, q)
            for t in range(2):
                n = 128 * (t + 1)
                t_hk = load(hk[t][:, :, :], bass.AP(bias_dram.tensor, 128 * (1 - t), [[1, 128], [384, 8], [1, n]]),
                            s_misc, t_b)
            v = rms_rows(lat, 128, 4, rl[:, 0, 0, 0:128], V.last())
            for t in range(2):
                v = stt(lat[:, t, :], lat[:, t, :], st[:, 4 + t:5 + t], kvg[:, :], ALU.mult, ALU.mult, t_small)
            b = bank("side")
            for t in range(2):
                m = tr(PS[b][:, t * 128:t * 128 + 128], lat[:, t, :], v, free[b], inc=True)
            free[b] = [cp(V, latT[:, :], PS[b][:, 0:256], m)]
            yield
            for h in (0, 1, 4, 5):
                b = bank("side")
                for j in range(2):
                    p0 = (h % 2) * 64
                    m = mm(PS[b][:, j * 256:j * 256 + 256], wukT[p0:p0 + 64, h // 2 + j, :], qT[p0:p0 + 64, h // 2 + j, :],
                           True, True, V.last(), free[b], inc=True)
                free[b] = [act(qabs[:, h:h + 3:2, :], PS[b][:, :].rearrange("p (j t) -> p j t", j=2), ACT.Copy, m, scale=0.125)]
            yield
            rl_free = [[], []]
            for t in range(2):
                n = 128 * (t + 1)
                for h in (0, 1, 4, 5):
                    b = bank("side")
                    z = h % 2
                    for j in range(2):
                        p0 = z * 64
                        m = mm(PS[b][:, j * n:j * n + n], qiT[p0:p0 + 64, h // 2 + j, t * 128:t * 128 + 128],
                               kiT[p0:p0 + 64, 0:n], True, True, free[b], inc=True)
                    r = rl[:, z, :, 0:n]
                    a = act(r, PS[b][:, 0:2 * n].rearrange("p (j k) -> p j k", j=2), ACT.Relu, m, rl_free[z])
                    free[b] = [a]
                    for j in range(2):
                        if h + j == 0:
                            v = ts(V, sc[t][:, :], r[:, 0, :], wi[:, t, 0:1], None, ALU.mult, None, a)
                        else:
                            v = stt(sc[t][:, :], r[:, j, :], wi[:, t, h + 2 * j:h + 2 * j + 1], sc[t][:, :], ALU.mult, ALU.add, a)
                    rl_free[z] = [v]
                    yield
                s, w = sc[t], wk[t]
                tt(V, s[:, n - 128:n], s[:, n - 128:n], C("causal"), ALU.add)
                for i in range(8):
                    src = s if i == 0 else w
                    V(lambda e, src=src: e.max(top[:, :], src[:, :]))
                    V(lambda e, src=src, w=w: e.match_replace(w[:, :], top[:, :], src[:, :], GONE))
                    if i % 4 == 3:
                        yield
                ts(V, w[:, :], w[:, :], -2.0e38, NEG, ALU.is_ge, ALU.mult)
                tt(V, w[:, n - 128:n], w[:, n - 128:n], C("causal"), ALU.add)
            yb = R["yb"]

            def logits(h, t, o):
                n = 128 * (t + 1)
                mm(o, qabs[:, h, t * 128:t * 128 + 128], latT[:, 0:n], True, False, V.last(), A.last(), t_hk)
                return mm(o, C("flip"), hk[t][:, h, :], False, True, inc=True)

            ob = {}
            ol_free = [[], []]

            def outp(h, p, m):
                a = cp(A, olT[:, h % 2, :], p, m, ol_free[h % 2])
                if h % 2 == 0:
                    ob[0] = bank("side")
                b = ob[0]
                p0 = (h % 2) * 64
                k = mm(PS[b][p0:p0 + 64, 0:256], wuv[:, h * 64:h * 64 + 64], olT[:, h % 2, :], True, True, a, free[b], inc=True)
                ol_free[h % 2] = [k]
                if h % 2 == 1:
                    free[b] = [tt(V, yb[:, h // 2, :], PS[b][:, 0:256], zb[:, h // 2, :], ALU.mult, k)]
                return a
            yield from attention(S, "d", list(range(8)), logits, lambda t: wk[t][:, :],
                                 lambda h, kt_: lat[:, kt_, :], (1, 2), outp,
                                 qq[:, :, :].rearrange("p (j k) t -> p j k t", k=2))

        g_rw = rwkv()
        g_ds = dsa()

        def col(c0, fn, n=256):
            fmslab(w_in, c0, n, fn)

        def gate_col(j):
            col(3912 + 256 * j, lambda hi, lo: fm_tiles(hi, lo, [0, 128], h_, sig_fm(gab, 2 * j)))
        beside(g_rw)
        col(2688, ckv_cols, 128)
        for j in range(2):
            col(1664 + 256 * j, lambda hi, lo, j=j: fm_tiles(hi, lo, [0, 128], h_, silu_fm(za, 2 * j)))
        for j in range(2):
            col(2816 + 256 * j, lambda hi, lo, j=j: fm_tiles(hi, lo, [0, 128], h_, silu_fm(zb, 2 * j)))
        for j in range(2):
            gate_col(j)
        for j in range(4):
            col([2176, 2432, 3328, 3584][j], lambda hi, lo, j=j: fm_tiles(hi, lo, [0, 128], h_, copy_fm(qq, 2 * j)))
        col(3776, ki_cols, 192)
        finish(g_rw)
        YA = {}

        def finish_a():
            SC[0].close()
            v = tt(V, R["bonus"][:, :, :], R["bonus"][:, :, :], za[:, :, :], ALU.mult, R["yT"])
            v = cp(V, za[:, :, :], R["bonus"][:, :, :])
            RW[0].close()
            enter()
            Y_ = Scope()
            YA["scope"] = Y_
            YA["a"] = Ready(Y_("yahi", [P, 4, 256], F32R), Y_("yalo", [P, 4, 256], F32R))
            YA["b"] = Ready(Y_("ybhi", [P, 4, 256], F32R), Y_("yblo", [P, 4, 256], F32R))
            k = split(YA["a"].p[0][:, :, :], YA["a"].p[1][:, :, :], za[:, :, :])
            YA["a"].tok = [[k, A.last()]] * 4
            R["yb"] = za
        do(finish_a)
        beside(g_ds)
        for j in range(2, 8):
            gate_col(j)

        def pa_slabs(w, key, evac):
            wv = w.rearrange("a r n -> (a r) n")
            for n in range(2):
                slab([(None, wv[:, n * 512:n * 512 + 512].rearrange("(k p) n -> p k n", p=P))],
                     lambda hi, lo, n=n: fm_tiles(hi, lo, [0, 128, 256, 384], YA[key], evac(4 * n), nk=4), (4, 512))

        def br_a(t0):
            return lambda j0, p, m: tt(V, gab[:, t0 + j0:t0 + j0 + 2, :], gab[:, t0 + j0:t0 + j0 + 2, :], p, ALU.mult, m)
        pa_slabs(I["w_pa"], "a", br_a)
        finish(g_ds)

        def finish_b():
            DS[0].close()
            k = split(YA["b"].p[0][:, :, :], YA["b"].p[1][:, :, :], za[:, :, :], V.last())
            YA["b"].tok = [[k, A.last()]] * 4
            load_row("final_g")
            early_sqrt()
        do(finish_b)

        def br_b(t0):
            def evac(j0, p, m):
                f = t0 + j0
                o = gab[:, 8 + f:10 + f, :]
                k = tt(V, o, o, p, ALU.mult, m)
                tt(V, o, o, gab[:, f:f + 2, :], ALU.add)
                q = split(hT[0][:, f:f + 2, :], hT[1][:, f:f + 2, :], o, V.last(), T.last())
                h_.tok[f] = h_.tok[f + 1] = [q, A.last()]
                return k
            return evac
        pa_slabs(I["w_pb"], "b", br_b)
        w_o = I["w_o"].rearrange("a r n -> (a r) n")
        def wo_evac(t0):
            def evac(j0, p, m):
                z = (t0 // 2) % 2
                for j in range(2):
                    v = ts(V, YA["m"][:, z, j, :], p[:, j, :], gate[:, t0 + j:t0 + j + 1], None, ALU.mult, None, m,
                           YA.get(z, []))
                b = bank("side")
                for j in range(2):
                    for t in range(2):
                        m = tr(PS[b][:, t * 256 + j * 128:t * 256 + j * 128 + 128], YA["m"][:, z, j, t * 128:t * 128 + 128],
                               v, free[b], inc=True)
                YA[z] = [m]
                o = x[:, :, t0 * 128:t0 * 128 + 256]
                free[b] = [tt(V, o, o, PS[b][:, :].rearrange("p (t n) -> p t n", t=2), ALU.add, m)]
                return v
            return evac

        def wo_cols(j, hi, lo):
            if j == 0:
                YA["m"] = za[:, :, :].rearrange("p (z j) t -> p z j t", z=2)
            return fm_tiles(hi, lo, [0, 128], h_, wo_evac(2 * j))
        for j in range(4):
            fmslab(w_o, 256 * j, 256, lambda hi, lo, j=j: wo_cols(j, hi, lo))

        def after_block1():
            v = V.last()
            for t in range(2):
                r = st[:, t:t + 1]
                act(gab[:, 4 * t:4 * t + 4, :].rearrange("p f t -> p (f t)"), x[:, t, :], ACT.Square, v, accum_out=r)
                a = act(r, r, ACT.Sqrt, scale=1.0 / 1024, bias=C("eps", 0, 1))
                V(lambda e, r=r: e.reciprocal(r, r), a)
                k = stt(x[:, t, :], x[:, t, :], r, row[:, :], ALU.mult, ALU.mult, row_tok[0])
            row_free[0] = [k]
            YA["scope"].close()
            B1.close()
            enter()
        do(after_block1)

        def ffn(tag, w_in_, w_down, pre, post_row):
            wv = w_in_.rearrange("a r n -> (a r) n")
            wd = w_down.rearrange("a r n -> (a r) n")
            L = {}

            def start():
                S = L["S"] = Scope()
                L["aT"] = [S("aThi" + tag, [P, 22, 256], F32R), S("aTlo" + tag, [P, 22, 256], F32R)]
                L["sg"] = S("sg" + tag, [P, 2, 256])
                L["ac"] = S("ac" + tag, [P, 2, 2, 256])
                L["y"] = S("y" + tag, [P, 2, 1024])
                L["yg"] = S("yg" + tag, [P, 2, 1024])
                L["pend"] = None
                load_row(post_row)
                run(norm(L["yg"], None, x, pre, V.last(), scaled=False))
                L["r"] = V.last()
            do(start)

            def turn_over():
                if L["pend"] is None:
                    return
                u, v = L["pend"]
                z = u % 2
                b = bank("side")
                for j in range(2):
                    for t in range(2):
                        m = tr(PS[b][:, j * 256 + t * 128:j * 256 + t * 128 + 128], L["ac"][:, z, t, j * 128:j * 128 + 128],
                               v, free[b], inc=True)
                L["acfree"] = [m]
                p = PS[b][:, :].rearrange("p (j t) -> p j t", j=2)
                hi, lo = (q[:, 2 * u:2 * u + 2, :] for q in L["aT"])
                a = cp(A, hi, p, m)
                free[b] = [tt(V, lo, p, hi, ALU.subtract, a)]
                L["pend"] = None

            for u in range(11):
                def evac(t, p, m, u=u):
                    r = st[:, t:t + 1]
                    a = act(L["sg"][:, t, :], p[:, 0:256], ACT.Silu, m, L["r"], scale=r)
                    v = stt(L["ac"][:, u % 2, t, :], p[:, 256:512], r, L["sg"][:, t, :], ALU.mult, ALU.mult, a,
                            L.get("acfree", []))
                    if t == 1:
                        L["pend2"] = (u, v)
                    return v

                def unit(kh, hi, lo, u=u, ev=evac):
                    run(tm_out(f"f{tag}{u}", h_, kh * 4, 4, kh == 1, hi, lo, ev))
                    if kh == 0:
                        turn_over()
                    else:
                        L["pend"] = L["pend2"]
                tmslabs(wv, [(256 * u, 256), (2816 + 256 * u, 256)], unit)

            def down(i, hi, lo):
                if i == 0:
                    turn_over()
                    L["bk"] = [bank("main") for _ in range(4)]
                    T.wait([V.last(), A.last()])
                    early_sqrt()
                for t in range(2):
                    for n in range(2):
                        b = L["bk"][2 * t + n]
                        for k in range(2):
                            kk = 2 * i + k
                            m = mm3(PS[b][:, :], [z[:, kk, t * 128:t * 128 + 128] for z in L["aT"]],
                                    (hi[:, k, n * 512:n * 512 + 512], lo[:, k, n * 512:n * 512 + 512]), kk == 0, kk == 21,
                                    free[b] if kk == 0 else [], inc=(k == 1))
                        if i == 10:
                            free[b] = [post_evac(L["y"], L["yg"], t, n, PS[b][:, :], m)]
                    if i == 10:
                        post(L["yg"], t, True)
            for i in range(11):
                slab([(None, wd[256 * i:256 * i + 256, :].rearrange("(k p) n -> p k n", p=P))],
                     lambda hi, lo, i=i: down(i, hi, lo), (2, 1024))

            def end():
                L["S"].close()
                enter()
            do(end)

        ffn("1", I["ffn1_w_in_2"], I["ffn1_w_down_2"], "ffn1_pre_g_2", "ffn1_post_g_2")

        w2 = I["w_in_2"].rearrange("a r n -> (a r) n")
        Z = {}

        def mix_start():
            S = Z["S"] = Scope()
            H = Z["H"] = Scope()
            for n in ("qb", "kb"):
                Z[n] = S(n, [P, 8, 256])
            Z["vb"] = S("vb", [P, 2, 1024])
            Z["ga"] = S("ga", [P, 8, 256])
            Z["lf"] = S("lf", [8, 4, 256])
            Z["sel"] = S("sel", [8, 8, 128])
            Z["lb"] = S("lb", [P, 2, 8])
            for n in ("b", "q", "k", "E"):
                Z[n] = H("h" + n, [P, 8, 256])
            Z["i"] = H("hi_", [P, 2, 1024])
            load_row("mix_post_g_2")
            run(norm(Z["i"], None, x, "mix_pre_g_2", V.last()))
            lb = Z["lb"]
            v = tt(V, lb[:, 0, :], vcol("hg_lb_logits_2", 0, 8), vcol("hg_lb_logits_2", 8, 8), ALU.subtract)
            a = act(lb[:, 0, :], lb[:, 0, :], ACT.Sigmoid, v)
            ts(V, lb[:, 1, :], lb[:, 0, :], -1.0, 1.0, ALU.mult, ALU.add, a)
            cp(V, Z["sel"][:, :, :], con[0:8, CON["ident"][0]:CON["ident"][0] + 8].unsqueeze(2).broadcast_to([8, 8, 128]))
        do(mix_start)

        def f_evac(t0):
            def evac(j0, p, m):
                a = act(Z["k"][:, t0:t0 + 2, :], p, ACT.Sigmoid, m)
                for j in range(2):
                    f = t0 + j
                    v = ts(V, Z["E"][:, f, :], Z["k"][:, f, :], Z["lb"][:, 1, f:f + 1], Z["lb"][:, 0, f:f + 1],
                           ALU.mult, ALU.add, a)
                ts(V, Z["k"][:, t0:t0 + 2, :], Z["E"][:, t0:t0 + 2, :], -1.0, 1.0, ALU.mult, ALU.add)
                return a
            return evac
        for j in range(4):
            fmslab(w2, 1024 + 256 * j, 256, lambda hi, lo, j=j: fm_tiles(hi, lo, [0, 128], h_, f_evac(2 * j)))
        for j in range(4):
            fmslab(w2, 256 * j, 256, lambda hi, lo, j=j: fm_tiles(hi, lo, [0, 128], h_, (lambda t0: lambda j0, p, m: silu_fm(Z["q"], t0)(j0, p, m))(2 * j)))

        def tm_copy(key, dst):
            for n in range(2):
                def evac(t, p, m, n=n):
                    return cp(V, dst()[:, t, n * 512:n * 512 + 512], p, m)
                yield n, evac

        for n, ev in tm_copy("i", lambda: Z["i"]):
            tmslabs(w2, [(2048 + 512 * n, 512)], lambda kh, hi, lo, n=n, ev=ev: tm_out(f"i{n}", h_, kh * 4, 4, kh == 1, hi, lo, ev))

        def hgrn():
            b_, q_, k_, E = Z["b"], Z["q"], Z["k"], Z["E"]
            H = Z["H"]
            AD = H("AD", [P, 8, 2, 128])
            AX_ = H("AXc", [P, 8, 128])
            a = act(E[:, :, :], E[:, :, :], ACT.Ln, V.last())
            for f in range(8):
                v = V(lambda e, f=f: e.tensor_tensor_scan(b_[:, f, :], C("reset"), E[:, f, :], 0.0, ALU.mult, ALU.add), a)
            zt = G(lambda e: e.memset(AD[:, :, :, :], 0.0))
            yield
            bv = b_[:, :, :].rearrange("p f t -> p (f t)")
            qv = q_[:, :, :].rearrange("p f t -> p (f t)")
            kv = k_[:, :, :].rearrange("p f t -> p (f t)")
            ev = E[:, :, :].rearrange("p f t -> p (f t)")

            def masked(l, lhs, rhs, tok):
                mask = (ident if l is None else C("off", 128 * l, 128)).bitcast(U32)
                for f in range(0, 8, 2):
                    b = bank("side")
                    for j in range(2):
                        for t in range(2):
                            s = slice(t * 128, t * 128 + 128)
                            m = mm(PS[b][:, (2 * j + t) * 128:(2 * j + t) * 128 + 128], lhs[:, f + j, s], rhs[:, f + j, s],
                                   True, True, tok, free[b], inc=True)
                    o = AD[:, f:f + 2, :, :].rearrange("p j t n -> p (j t) n")
                    c = V(lambda e, o=o, b=b: e.copy_predicated(o, mask.unsqueeze(1).broadcast_to([P, 4, 128]),
                                                                PS[b][:, :].rearrange("p (j n) -> p j n", j=4)), m, zt)
                    free[b] = [c]
                    if f == 2:
                        yield m
                yield m

            for m in masked(None, k_, q_, V.last()):
                yield
            for l in range(8):
                B = 1 << l
                w = T.last()
                if l < 7:
                    pv = bv.rearrange("p (n z) -> p n z", z=2 * B)
                    pe = ev.rearrange("p (n z) -> p n z", z=2 * B)
                    n = 1024 // B
                    ref = pv[:, :, B - 1:B].broadcast_to([P, n, B])
                    tt(V, pe[:, :, 0:B], ref, pv[:, :, 0:B], ALU.subtract, w)
                    v = tt(V, pe[:, :, B:2 * B], pv[:, :, B:2 * B], ref, ALU.subtract)
                    a = act(ev, ev, ACT.Exp, v)
                else:
                    v = tt(V, E[:, :, 0:128], b_[:, :, 127:128].broadcast_to([P, 8, 128]), b_[:, :, 0:128], ALU.subtract, w)
                    pe = E[:, :, :].rearrange("p f (n z) -> p (f n) z", z=256)
                    act(E[:, :, 128:256], b_[:, :, 128:256], ACT.Exp, w)
                    a = act(E[:, :, 0:128], E[:, :, 0:128], ACT.Exp, v)
                    n = 8
                pk = kv.rearrange("p (n z) -> p n z", z=2 * B)
                pq = qv.rearrange("p (n z) -> p n z", z=2 * B)
                tt(V, pe[:, :, 0:B], pe[:, :, 0:B], pk[:, :, 0:B], ALU.mult, a)
                v = tt(V, pe[:, :, B:2 * B], pe[:, :, B:2 * B], pq[:, :, B:2 * B], ALU.mult)
                yield
                if l < 7:
                    for m in masked(l, E, E, v):
                        yield
                else:
                    for f in range(0, 8, 4):
                        b = bank("side")
                        for j in range(4):
                            m = mm(PS[b][:, j * 128:j * 128 + 128], E[:, f + j, 0:128], E[:, f + j, 128:256], True, True,
                                   v, free[b], inc=True)
                        c = cp(V, AX_[:, f:f + 4, :], PS[b][:, :].rearrange("p (j n) -> p j n", j=4), m)
                        free[b] = [c]
                    yield
            o_ = b_[:, :, :].rearrange("p f t -> p (f t)").rearrange("p (t n) -> p t n", t=2)
            i_ = Z["i"]
            for t in range(2):
                for f in range(0, 8, 4):
                    b = bank("side")
                    for j in range(4):
                        h = f + j
                        o = PS[b][:, j * 128:j * 128 + 128]
                        m = mm(o, AD[:, h, t, :], i_[:, t, h * 128:h * 128 + 128], True, t == 0, c, free[b], inc=True)
                        if t == 1:
                            m = mm(o, AX_[:, h, :], i_[:, 0, h * 128:h * 128 + 128], False, True, inc=True)
                    v = cp(V, o_[:, t, f * 128:f * 128 + 512], PS[b][:, :], m)
                    free[b] = [v]
                yield
            junk = E[:, 0:4, :].rearrange("p f t -> p (f t)")
            rms_rows(o_, 1024, 6, junk, v, T.last())
            for t in range(2):
                v = ts(V, o_[:, t, :], o_[:, t, :], st[:, 6 + t:7 + t], None, ALU.mult, None)
            yield
            for f in range(0, 8, 2):
                b = bank("side")
                for j in range(2):
                    for t in range(2):
                        m = tr(PS[b][:, j * 256 + t * 128:j * 256 + t * 128 + 128], o_[:, t, (f + j) * 128:(f + j) * 128 + 128],
                               v, free[b], inc=True)
                for j in range(2):
                    k = stt(Z["ga"][:, f + j, :], PS[b][:, j * 256:j * 256 + 256], vcol("hg_norm_g_2", f + j),
                            Z["ga"][:, f + j, :], ALU.mult, ALU.mult, m)
                free[b] = [k]
            yield

        g_h = hgrn()
        beside(g_h)
        for j in range(4):
            fmslab(w2, 3072 + 256 * j, 256, lambda hi, lo, j=j: fm_tiles(hi, lo, [0, 128], h_, silu_fm(Z["ga"], 2 * j)))

        def scaled(key, t0, s):
            return lambda j0, p, m: act(Z[key][:, t0:t0 + 2, :], p, ACT.Copy, m, scale=s)
        for j in range(4):
            fmslab(w2, 4096 + 256 * j, 256, lambda hi, lo, j=j: fm_tiles(hi, lo, [0, 128], h_,
                                                                         scaled("qb", 2 * j, 1.0 / math.sqrt(128))))
        for j in range(4):
            fmslab(w2, 5120 + 256 * j, 256, lambda hi, lo, j=j: fm_tiles(hi, lo, [0, 128], h_, copy_fm(Z["kb"], 2 * j)))
        for n, ev in tm_copy("v", lambda: Z["vb"]):
            tmslabs(w2, [(6144 + 512 * n, 512)], lambda kh, hi, lo, n=n, ev=ev: tm_out(f"v{n}", h_, kh * 4, 4, kh == 1, hi, lo, ev))

        def fb_cols(hi, lo):
            def evac(j0, p, m):
                lf = Z["lf"]
                xx, t1, nc_ = lf[:, 0, :], lf[:, 1, :], lf[:, 2, :]
                k = act(xx, p[0:8, 0, :], ACT.Identity, m, bias=vec[0:8, VEC["fox_f_bias_2"][0]:VEC["fox_f_bias_2"][0] + 1])
                act(t1, xx, ACT.Abs)
                act(t1, t1, ACT.Exp, scale=-1.0)
                a = act(t1, t1, ACT.Ln, bias=C("one", 0, 1, rows=8))
                stt(xx, xx, 0.0, t1, ALU.min, ALU.subtract, a)
                V(lambda e: e.tensor_tensor_scan(nc_, C("one", rows=8), xx, 0.0, ALU.mult, ALU.add))
                ts(V, lf[:, 3, :], nc_, -1.0, None, ALU.mult, None)
                return k
            return fm_tiles(hi, lo, [0], h_, evac)
        fmslab(w2, 7168, 128, fb_cols)
        finish(g_h)

        def end_hgrn():
            Z["H"].close()
            enter()
            F = Z["F"] = Scope()
            Z["gt"] = F("gt", [P, 16, 256])
            Z["oa"] = Ready(F("oahi", [P, 8, 256], F32R), F("oalo", [P, 8, 256], F32R))
            k = split(Z["oa"].p[0][:, :, :], Z["oa"].p[1][:, :, :], Z["ga"][:, :, :], V.last())
            Z["oa"].tok = [[k, A.last()]] * 8
            Z["A"] = Scope()
        do(end_hgrn)

        def fox():
            def logits(h, t, o):
                n = 128 * (t + 1)
                mm(o, Z["qb"][:, h, t * 128:t * 128 + 128], Z["kb"][:, h, 0:n], True, False, V.last(), A.last())
                return mm(o, Z["sel"][:, h, :], Z["lf"][:, 3, 0:n], False, True, inc=True)

            def mask(t):
                return C("causal") if t == 0 else con[:, CON["zero"][0]:CON["zero"][0] + 256]

            def outp(h, p, m):
                return cp(V, Z["ga"][:, h, :], p, m)
            yield from attention(Z["A"], "f", list(range(8)), logits, mask,
                                 lambda h, kt_: Z["vb"][:, kt_, h * 128:h * 128 + 128], (1, 2), outp)
        g_f = fox()

        def tm_view(key, f0=0):
            return Z[key][:, f0:f0 + 8, :].rearrange("p f t -> p (f t)").rearrange("p (t n) -> p t n", t=2)

        def sig_gate(t0):
            return lambda j0, p, m: sig_fm(Z["gt"], t0, "b_gate_2")(j0, p, m)
        beside(g_f)
        for j in range(8):
            fmslab(w2, 7176 + 256 * j, 256, lambda hi, lo, j=j: fm_tiles(hi, lo, [0, 128], h_, sig_gate(2 * j)))
        wba = I["w_branch_a_2"].rearrange("a r n -> (a r) n")
        wbb = I["w_branch_b_2"].rearrange("a r n -> (a r) n")

        def br2a(t0):
            def evac(j0, p, m):
                o = Z["gt"][:, t0:t0 + 2, :]
                return tt(V, o, o, p, ALU.mult, m)
            return evac
        for j in range(4):
            fmslab(wba, 256 * j, 256, lambda hi, lo, j=j: fm_tiles(hi, lo, [0, 128], Z["oa"], br2a(2 * j)))
        finish(g_f)

        def split_b():
            k = split(Z["oa"].p[0][:, :, :], Z["oa"].p[1][:, :, :], Z["ga"][:, :, :], V.last(), T.last())
            Z["oa"].tok = [[k, A.last()]] * 8
            Z["mem"] = load(tm_view("kb"), I["mem_2"].rearrange("a (t p) d -> p (a t) d", p=P), s_misc, fence())
        do(split_b)

        def br2b(t0):
            def evac(j0, p, m):
                o = Z["gt"][:, 8 + t0:10 + t0, :]
                k = tt(V, o, o, p, ALU.mult, m)
                tt(V, o, o, Z["gt"][:, t0:t0 + 2, :], ALU.add)
                q = split(hT[0][:, t0:t0 + 2, :], hT[1][:, t0:t0 + 2, :], o, V.last())
                h_.tok[t0] = h_.tok[t0 + 1] = [q, A.last()]
                return k
            return evac
        for j in range(4):
            fmslab(wbb, 256 * j, 256, lambda hi, lo, j=j: fm_tiles(hi, lo, [0, 128], Z["oa"], br2b(2 * j)))
        wout = I["w_out_2"].rearrange("a r n -> (a r) n")

        def post_slabs(w, key, lhs, y, yg):
            for n in range(2):
                tmslabs(w, [(512 * n, 512)], lambda kh, hi, lo, n=n: tm_out(
                    f"{key}{n}", lhs(), kh * 4, 4, kh == 1, hi, lo, lambda t, p, m: post_evac(tm_view(y), tm_view(yg), t, n, p, m)))

        wkv = I["w_mkv_2"].rearrange("a r n -> (a r) n")
        wmq = I["w_mq_2"].rearrange("a r n -> (a r) n")
        wmo = I["w_mo_2"].rearrange("a r n -> (a r) n")

        def mem_norm():
            early_sqrt()
            yield
            yield from norm(tm_view("qb"), None, tm_view("kb"), "mem_kv_g_2", Z["mem"], dst=Z["oa"])
        g_m = mem_norm()
        beside(g_m)
        post_slabs(wout, "wout", lambda: h_, "ga", "gt")
        finish(g_m)

        def mix_end():
            for t in range(2):
                post(tm_view("gt"), t, False)
                yield
            load_row("mem_post_g_2")
            yield from norm(tm_view("gt"), None, x, "mem_pre_g_2", V.last())
        g_e = mix_end()
        beside(g_e)
        for j in range(4):
            fmslab(wkv, 256 * j, 256, lambda hi, lo, j=j: fm_tiles(hi, lo, [0, 128], Z["oa"], copy_fm(Z["kb"], 2 * j)))
        finish(g_e)
        for j in range(4):
            fmslab(wmq, 256 * j, 256, lambda hi, lo, j=j: fm_tiles(hi, lo, [0, 128], h_, scaled("qb", 2 * j, 1.0 / 16)))

        def mem_attention():
            z = [Z["gt"][:, 4 * t:4 * t + 4, :] for t in range(2)]
            pt = Z["gt"][:, 8:16, :].rearrange("p (j k) t -> p j k t", k=2)
            red = Z["A"]("mred", [P, 2, 3, 4])
            t0 = [V.last(), A.last()]
            for t in range(2):
                for h0 in (0, 2):
                    b = bank("side")
                    for j in range(2):
                        h = h0 + j
                        for d in range(2):
                            m = mm(PS[b][:, j * 256:j * 256 + 256], Z["qb"][:, 2 * h + d, t * 128:t * 128 + 128],
                                   Z["kb"][:, 2 * h + d, :], d == 0, d == 1, t0, free[b], inc=(d == 1))
                    free[b] = [cp(V, z[t][:, h0:h0 + 2, :], PS[b][:, :].rearrange("p (j k) -> p j k", j=2), m)]
                yield
            for t in range(2):
                mx, sm, rc = (red[:, t, q, :] for q in range(3))
                zt = z[t]
                v = V(lambda e, mx=mx, zt=zt: e.tensor_reduce(mx, zt[:, :, :], AX.X, ALU.max, negate=True))
                for h in range(4):
                    a = act(zt[:, h, :], zt[:, h, :], ACT.Exp, v, bias=red[:, t, 0, h:h + 1], accum_out=red[:, t, 1, h:h + 1])
                V(lambda e, rc=rc, sm=sm: e.reciprocal(rc, sm), a)
                v = tt(V, zt[:, :, :], zt[:, :, :], rc.unsqueeze(2).broadcast_to([P, 4, 256]), ALU.mult)
                yield
                for h0 in (0, 2):
                    b = bank("side")
                    for j in range(2):
                        for k in range(2):
                            m = tr(PS[b][:, (2 * j + k) * 128:(2 * j + k) * 128 + 128], zt[:, h0 + j, k * 128:k * 128 + 128],
                                   v, free[b], inc=True)
                    c = cp(V, pt[:, h0:h0 + 2, :, t * 128:t * 128 + 128],
                           PS[b][:, :].rearrange("p (j k q) -> p j k q", j=2, k=2), m)
                    free[b] = [c]
            yield
            while not Z.get("v done"):
                yield
            for f in range(0, 8, 2):
                b = bank("side")
                for j in range(2):
                    for k in range(2):
                        m = mm(PS[b][:, j * 256:j * 256 + 256], Z["vb"][:, k, (f + j) * 128:(f + j) * 128 + 128],
                               pt[:, (f + j) // 2, k, :], k == 0, k == 1, c, V.last(), free[b], inc=(k == 1))
                i = PS[b][:, :].rearrange("p (j t) -> p j t", j=2)
                hi, lo = (q[:, f:f + 2, :] for q in Z["oa"].p)
                a = cp(A, hi, i, m)
                q = tt(V, lo, i, hi, ALU.subtract, a)
                Z["oa"].tok[f] = Z["oa"].tok[f + 1] = [a, q]
                free[b] = [q]
            early_sqrt()
        g_a = mem_attention()
        beside(g_a)
        for n, ev in tm_copy("mv", lambda: Z["vb"]):
            tmslabs(wkv, [(1024 + 512 * n, 512)], lambda kh, hi, lo, n=n, ev=ev: tm_out(f"mv{n}", Z["oa"], kh * 4, 4, kh == 1, hi, lo, ev))
        do(lambda: Z.update({"v done": True}))
        finish(g_a)
        post_slabs(wmo, "wmo", lambda: Z["oa"], "qb", "kb")

        def mem_end():
            for t in range(2):
                post(tm_view("kb"), t, False)
            Z["A"].close()
            Z["F"].close()
            Z["S"].close()
            enter()
        do(mem_end)

        ffn("2", I["ffn2_w_in_2"], I["ffn2_w_down_2"], "ffn2_pre_g_2", "ffn2_post_g_2")

        bias_dram = nc.dram_tensor("bias_scratch", (8, 384), F32, kind="Internal").ap()
        run_tasks()
        t_out = load(out.rearrange("a (t p) d -> p (a t) d", p=P), x[:, :, :], s_out, V.last())
        load.q.wait(t_out, (s_misc, load.count[s_misc.name]))

        block = ctx.enter_context(nc.Block())

        @block.sync
        def _(e):
            load.q.play(e)

        @block.vector
        def _(e):
            V.play(e)

        @block.scalar
        def _(e):
            A.play(e)

        @block.gpsimd
        def _(e):
            G.play(e)

        @block.tensor
        def _(e):
            T.play(e)


DIRECT = ["x", "ada_w", "ada_b", "w_in", "w2", "a2", "kv_norm_g", "w_uk", "w_uv", "w_pa", "w_pb", "w_o", "rel_bias",
          "final_g", "mem_2", "ffn1_w_in_2", "ffn1_w_down_2", "ffn1_post_g_2", "w_in_2", "w_branch_a_2",
          "w_branch_b_2", "w_out_2", "mix_post_g_2", "w_mq_2", "w_mkv_2", "w_mo_2", "mem_post_g_2",
          "ffn2_w_in_2", "ffn2_w_down_2", "ffn2_post_g_2"]


def kernel(**inputs):
    import concourse.bacc as bacc
    from concourse.bass_utils import run_bass_kernel_spmd

    arrays = {}
    for name in DIRECT:
        a = np.asarray(inputs[name])
        if name == "w_uk":
            a = a.reshape(128, 4, 128).transpose(2, 1, 0)
        arrays[name] = np.ascontiguousarray(a)
    vecs = np.zeros((P, NVEC), np.float32)
    for name, (o, w) in VEC.items():
        a = np.asarray(inputs[name]).reshape(-1)
        if name == "fox_f_bias_2":
            vecs[0:8, o] = a
        elif name == "shift_mu" or a.size == 128 * w:
            vecs[:, o:o + w] = a.reshape(w, 128).T
    arrays["vecs"] = vecs
    arrays["consts"] = constants()
    nc = bacc.Bacc("TRN2", target_bir_lowering=False, num_devices=1)
    aps = {n: nc.dram_tensor(f"in_{n}", a.shape, mybir.dt.from_np(a.dtype), kind="ExternalInput").ap()
           for n, a in arrays.items()}
    out = nc.dram_tensor("out_0", (1, 256, 1024), F32, kind="ExternalOutput").ap()
    program(nc, {n: aps[n] for n in DIRECT}, aps["consts"], aps["vecs"], out)
    r = run_bass_kernel_spmd(nc, [{f"in_{n}": a for n, a in arrays.items()}], core_ids=[0])
    return r.results[0]["out_0"]
```

```python
import math
from contextlib import ExitStack

import numpy as np

import concourse.bass as bass
from concourse import mybir

F32 = mybir.dt.float32
F32R = mybir.dt.float32r
U32 = mybir.dt.uint32
ALU = mybir.AluOpType
ACT = mybir.ActivationFunctionType
AX = mybir.AxisListType
P = 128
NRAW, NHL = 4, 3
NEG = -1.0e30
GONE = -3.0e38

VEC = {}
for _n, _w in [("c", 8), ("norm_g", 8), ("ada_b", 24), ("shift_mu", 13), ("w0", 4), ("a0", 4), ("k_k", 4),
               ("k_a", 4), ("r_k", 4), ("lnx_g", 4), ("lnx_b", 4), ("ffn1_pre_g_2", 8), ("mix_pre_g_2", 8),
               ("hg_lb_logits_2", 16), ("hg_norm_g_2", 8), ("b_gate_2", 16), ("mem_pre_g_2", 8),
               ("mem_kv_g_2", 8), ("ffn2_pre_g_2", 8), ("fox_f_bias_2", 1)]:
    VEC[_n] = (sum(w for _, w in VEC.values()), _w)
NVEC = sum(w for _, w in VEC.values())

CON = {}
for _n, _w in [("ident", 128), ("flip", 128), ("strict", 128), ("incl", 128), ("zero", 128), ("causal", 128),
               ("ones64", 128), ("off", 7 * 128), ("reset", 256), ("one", 256), ("eps", 4), ("hot", 384)]:
    CON[_n] = (sum(w for _, w in CON.values()), _w)
NCON = sum(w for _, w in CON.values())


def constants():
    c = np.zeros((P, NCON), np.float32)

    def put(name, a):
        o, w = CON[name]
        c[:a.shape[0], o:o + w] = a
    s, t = np.arange(P)[:, None], np.arange(P)[None, :]
    put("ident", s == t)
    put("flip", s + t == P - 1)
    put("strict", s < t)
    put("incl", s <= t)
    put("causal", np.where(t > s, NEG, 0.0))
    put("ones64", s // 64 == t // 64)
    put("off", np.concatenate([(s // (2 << l) == t // (2 << l)) & ((s >> l) % 2 == 0) & ((t >> l) % 2 == 1)
                               for l in range(7)], axis=1))
    put("reset", np.broadcast_to(np.arange(256) % P != 0, (P, 256)))
    put("one", np.ones((P, 256)))
    put("eps", np.broadcast_to(np.array([1e-6, 64e-5, 4e-6, 0.0]), (P, 4)))
    dist = np.arange(256)
    d = np.maximum(dist, 1).astype(np.float32)
    large = 16 + (np.log(d / np.float32(16)) / np.float32(math.log(8)) * np.float32(16)).astype(np.int32)
    bucket = np.where(dist < 16, dist, np.minimum(large, 31))
    hot = np.zeros((32, 384), np.float32)
    hot[bucket, 255 - dist] = 1.0
    put("hot", hot)
    return c


def width(ap):
    n = 1
    for d in ap.shape[1:]:
        n *= d
    return n


class Engine:
    when = {}

    def __init__(self, sem, serial):
        self.sem, self.serial, self.n, self.ops, self.seen, self.t = sem, serial, 0, [], {}, 0.0

    def __call__(self, fn, *waits, inc=True, cost=0.1):
        if self.serial and self.n:
            waits += (self.last(),)
        self.wait(*waits)
        self.t += cost
        if inc:
            self.n += 1
            self.when[self.sem.name, self.n] = self.t + 0.15
        self.ops.append((fn, self.sem if inc else None))
        return (self.sem, self.n)

    def wait(self, *waits):
        for w in waits:
            for sem, v in (w if isinstance(w, list) else [w]):
                if v > self.seen.get(sem.name, 0):
                    self.seen[sem.name] = v
                    self.ops.append((None, (sem, v)))
                    self.t = max(self.t, self.when.get((sem.name, v), 0.0))

    def last(self):
        return (self.sem, self.n)

    def play(self, eng):
        for fn, s in self.ops:
            if fn is None:
                eng.wait_ge(*s)
            elif s is None:
                fn(eng)
            elif isinstance(s, tuple):
                fn(eng).then_inc(*s)
            else:
                fn(eng).then_inc(s, 1)


class Loader:

    def __init__(self):
        self.q, self.count = Engine(None, False), {}

    def __call__(self, out, in_, sem, *waits):
        self.q.wait(*waits)
        self.q.ops.append((lambda e: e.dma_start(out, in_), (sem, 16)))
        self.count[sem.name] = self.count.get(sem.name, 0) + 16
        self.q.t += out.shape[0] * width(out) * 4 / 350e3
        self.q.when[sem.name, self.count[sem.name]] = self.q.t + 2.0
        return (sem, self.count[sem.name])


def program(nc, I, consts, vecs, out):
    Engine.when.clear()
    ctx = ExitStack()
    with ctx:
        def sem(name):
            return ctx.enter_context(nc.semaphore(name))

        class Scope:
            def __init__(self):
                self.es = ExitStack()

            def __call__(self, name, shape, dt=F32):
                return self.es.enter_context(nc.sbuf_tensor(name, shape, dt))

            def close(self):
                self.es.close()

        glob = Scope()
        V, A, G, T = (Engine(sem(n), s) for n, s in
                      [("s_vec", True), ("s_act", True), ("s_pool", True), ("s_pe", False)])
        load = Loader()
        s_const = sem("s_const")
        s_vecs = sem("s_vecs")
        s_row = sem("s_row")
        s_raw = [sem(f"s_raw{i}") for i in range(NRAW)]
        s_misc = sem("s_misc")
        s_out = sem("s_out")

        NC = CON["hot"][0]
        con = glob("con", [P, NC])
        vec = glob("vec", [P, NVEC])
        raw = [glob(f"raw{i}", [P, 1024]) for i in range(NRAW)]
        whi = [glob(f"whi{i}", [P, 1024], F32R) for i in range(NHL)]
        wlo = [glob(f"wlo{i}", [P, 1024], F32R) for i in range(NHL)]
        x = glob("x", [P, 2, 1024])
        hT = [glob("hThi", [P, 8, 256], F32R), glob("hTlo", [P, 8, 256], F32R)]
        row = glob("row", [P, 1024])
        st = glob("st", [P, 16])
        PS = [ctx.enter_context(nc.psum_tensor(f"ps{i}", [P, 512], F32)) for i in range(8)]
        free = [[] for _ in range(8)]
        turn = {"main": 0, "side": 0}
        BANKS = {"main": [0, 1, 2], "side": [3, 4, 5, 6, 7]}

        def bank(kind):
            b = BANKS[kind][turn[kind] % len(BANKS[kind])]
            turn[kind] += 1
            return b

        def C(name, i=0, w=None, rows=P):
            o, n = CON[name]
            return con[0:rows, o + i:o + (i + w if w else n)]

        def vcol(name, j=0, w=1):
            o = VEC[name][0] + j
            return vec[:, o:o + w]

        ident = C("ident")

        def fence():
            return [e.last() for e in (V, A, G, T)]

        def enter():
            f = fence()
            for e in (V, A, G):
                e.wait(f)
            return f

        def elementwise(E, o):
            n = width(o)
            return 0.1 + n * (0.0021 if E is G else 0.0009 if E is A else 0.00105)

        def tt(E, o, a, b, op, *w):
            return E(lambda e: e.tensor_tensor(o, a, b, op), *w, cost=elementwise(E, o))

        def ts(E, o, a, s1, s2, op0, op1, *w):
            if op1 is None:
                return E(lambda e: e.tensor_scalar(o, a, s1, None, op0), *w, cost=elementwise(E, o))
            return E(lambda e: e.tensor_scalar(o, a, s1, s2, op0, op1), *w, cost=elementwise(E, o))

        def stt(o, a, s, b, op0, op1, *w):
            return V(lambda e: e.scalar_tensor_tensor(out=o, in0=a, scalar=s, in1=b, op0=op0, op1=op1), *w,
                     cost=elementwise(V, o))

        def act(o, a, f, *w, **kw):
            return A(lambda e: e.activation(o, a, f, **kw), *w, cost=elementwise(A, o))

        def recip(o, a, *w):
            return V(lambda e: e.reciprocal(o, a), *w, cost=0.1 + 0.0064 * width(o))

        def cp(E, o, a, *w):
            if E is A:
                return act(o, a, ACT.Copy, *w)
            return E(lambda e: e.tensor_copy(o, a), *w, cost=elementwise(E, o))

        def mm(o, l, r, start, stop, *w, inc=False, skip=False):
            return T(lambda e: e.matmul(o, l, r, start=start, stop=stop, skip_group_check=skip), *w, inc=inc,
                     cost=max(width(r), 64) * (1 if r.dtype == F32R else 4) / 2400)

        def mm3(o, l, r, start, stop, *w, inc=False):
            mm(o, l[0], r[0], start, False, *w)
            mm(o, l[0], r[1], False, False)
            return mm(o, l[1], r[0], False, stop, inc=inc)

        def tr(o, a, *w, inc=False):
            return T(lambda e: e.transpose(o, a, ident), *w, inc=inc, cost=0.11)

        def split_tiles(dst, src, *w):
            for f in range(src.shape[1]):
                hi, lo = (q[:, f, :] for q in dst.p)
                a = cp(A, hi, src[:, f, :], *w)
                dst.tok[f] = [a, tt(G if f % 3 == 2 else V, lo, src[:, f, :], hi, ALU.subtract, a, *w)]

        tasks, slabs = [], []

        def slab(parts, shape, plain=False):
            slabs.append((parts, shape, plain))

        WAIT = "wait"
        side = []

        class Chain:

            def __init__(self, gen):
                self.gen, self.ready, self.done, self.part = gen, 0.0, False, 0

            def step(self):
                n = [e.n for e in (V, A, G)]
                r = next(self.gen, None)
                self.ready = max([e.t + 0.15 for e, k in zip((V, A, G), n) if e.n > k], default=0.0)
                if isinstance(r, tuple):
                    self.ready = Engine.when[r[0].name, r[1]]
                return r != WAIT

        def advance():
            going = list(side)
            while going:
                for c in list(going):
                    if c.done or c.ready > T.t + 0.4 or not c.step():
                        going.remove(c)

        def chain(fn):
            c = Chain(None)

            def gen():
                yield from fn()
                c.done = True
                while True:
                    yield WAIT
            c.gen = gen()
            return c

        def beside(*chains):
            def go():
                side[:] = chains
            tasks.append(go)

        def finish(*chains, beside_=()):
            def go():
                while not all(c.done for c in chains):
                    for c in sorted((c for c in [*chains, *beside_] if not c.done), key=lambda c: c.ready):
                        if c.step():
                            break
            tasks.append(go)

        def advance_past(c, n):
            while c.part < n:
                c.step()

        def do(fn):
            tasks.append(fn)

        def fmslab(w, c0, n, fn):
            for c in range(c0, c0 + n, 128):
                slab([(None, w[:, c:c + 128].rearrange("(k p) n -> p k n", p=P))], (8, 128))
            tasks.append(fn)

        def tmslabs(w, cols, fn, half=None):
            for kh in range(w.shape[0] // 256):
                parts, o = [], 0
                for c0, n in cols:
                    parts.append(((o, n), w[kh * 256:(kh + 1) * 256, c0:c0 + n].rearrange("(k p) n -> p k n", p=P)))
                    o += n
                slab(parts, (2, o))
                if half is not None and kh == 2:
                    finish(half)
                tasks.append(lambda kh=kh: fn([kh]))

        ring = {"fetched": 0, "split": 0, "taken": 0}
        dma_tok, lo_tok, hi_tok, use_tok = {}, {}, {}, {}
        place = {}

        def view(buf, shape):
            k, n = shape
            return buf[:, 0:k * n].rearrange("p (k n) -> p k n", k=k)

        def prefetch():
            while ring["fetched"] < len(slabs):
                i = ring["fetched"]
                parts, shape, _ = slabs[i]
                old, w = i - NRAW, []
                if old >= 0:
                    if (use_tok if slabs[old][2] else lo_tok).get(old) is None:
                        return
                    w = [use_tok[old]] if slabs[old][2] else [lo_tok[old], hi_tok[old]]
                dst = view(raw[i % NRAW], shape)
                for sel, src in parts:
                    d = dst if sel is None else dst[:, :, sel[0]:sel[0] + sel[1]]
                    dma_tok[i] = load(d, src, s_raw[i % NRAW], *w)
                ring["fetched"] += 1

        def split_ahead(upto):
            while ring["split"] < min(upto, len(slabs)):
                i = ring["split"]
                if not slabs[i][2]:
                    c = len(place)
                    before = [j for j in place if place[j] == c - NHL]
                    if i >= ring["fetched"] or (before and before[0] not in use_tok):
                        return
                    place[i] = c
                    n = slabs[i][1][0] * slabs[i][1][1]
                    r, h, l = raw[i % NRAW], whi[c % NHL], wlo[c % NHL]
                    hi_tok[i] = cp(A, h[:, 0:n], r[:, 0:n], dma_tok[i], *[use_tok[j] for j in before])
                    lo_tok[i] = tt(G, l[:, 0:n], r[:, 0:n], h[:, 0:n], ALU.subtract, hi_tok[i])
                    prefetch()
                ring["split"] += 1

        def take(E=None):
            i = ring["taken"]
            ring["taken"] += 1
            prefetch()
            split_ahead(i + NHL)
            if slabs[i][2]:
                E.wait(dma_tok[i])
                return view(raw[i % NRAW], slabs[i][1])
            T.wait(hi_tok[i], lo_tok[i])
            c = place[i] % NHL
            return view(whi[c], slabs[i][1]), view(wlo[c], slabs[i][1])

        def give(E=T, n=1):
            for i in range(ring["taken"] - n, ring["taken"]):
                use_tok[i] = E.last()

        def run_tasks():
            prefetch()
            for t in tasks:
                for _ in t() or ():
                    advance()

        def rms_rows(src, n, col, junk, *w, eps=0):
            for t in range(2):
                act(junk, src[:, t, :], ACT.Square, *w, accum_out=st[:, col + t:col + t + 1])
            r = st[:, col:col + 2]
            a = act(r, r, ACT.Sqrt, scale=1.0 / n, bias=C("eps", eps, 1))
            return recip(r, r, a)

        class Ready:

            def __init__(self, hi, lo):
                self.p, self.tok = (hi, lo), [[] for _ in range(hi.shape[1])]

        h_ = Ready(*hT)

        def norm(xn, tmp, src, g, *w, dst=h_, bias=None, scale=None, scaled=True):
            scale = scale or (lambda f: vcol(g, f))

            def rstd(t, junk):
                r = st[:, t:t + 1]
                act(junk, src[:, t, :], ACT.Square, w[t], accum_out=r)
                a = act(r, r, ACT.Sqrt, scale=1.0 / 1024, bias=C("eps", 0, 1))
                return recip(r, r, a)
            v = list(w)
            if scaled:
                for t in range(2):
                    q = rstd(t, xn[:, t, :])
                    a = act(xn[:, t, 512:1024], src[:, t, 512:1024], ACT.Copy, q, scale=st[:, t:t + 1])
                    q = ts(V, xn[:, t, 0:512], src[:, t, 0:512], st[:, t:t + 1], None, ALU.mult, None)
                    v[t] = [q, a]
                    yield
                src_ = xn
            else:
                src_ = src
            tmp_free = []
            bs = [bank("side") for _ in range(4)]
            for t in range(2):
                for f in range(8):
                    b = bs[f // 2]
                    o = (f % 2) * 256 + t * 128
                    k = tr(PS[b][:, o:o + 128], src_[:, t, f * 128:f * 128 + 128], free[b], v[t], inc=True)
            if bias is not None:
                yield
            for f0 in range(0, 8, 2):
                b = bs[f0 // 2]
                for f in (f0, f0 + 1):
                    i = PS[b][:, (f - f0) * 256:(f - f0) * 256 + 256]
                    if bias is None:
                        a = act(dst.p[0][:, f, :], i, ACT.Copy, k, scale=scale(f))
                    else:
                        a = act(dst.p[0][:, f, :], i, ACT.Identity, k, scale=scale(f), bias=bias(f))
                        if f % 2 == 1:
                            a = act(tmp[:, f - f0, :], i, ACT.Identity, k, tmp_free, scale=scale(f), bias=bias(f))
                for f in (f0, f0 + 1):
                    i = PS[b][:, (f - f0) * 256:(f - f0) * 256 + 256]
                    hi, lo = dst.p[0][:, f, :], dst.p[1][:, f, :]
                    if bias is None:
                        q = stt(lo, i, scale(f), hi, ALU.mult, ALU.subtract, a)
                    else:
                        o = tmp[:, f - f0, :]
                        if f % 2 == 0:
                            ts(V, o, i, scale(f), bias(f), ALU.mult, ALU.add, k, a)
                        q = tt(V, lo, o, hi, ALU.subtract, a)
                    dst.tok[f] = [a, q]
                tmp_free = [q]
                free[b] = [q]
                yield
            if not scaled:
                for t in range(2):
                    rstd(t, xn[:, t, :])

        def run(gen):
            for _ in gen:
                pass

        row_free = [[]]
        x_tok, t_out = [None, None], [None]

        def load_row(name, c0=0):
            a = I[name]
            if len(a.shape) == 2:
                a = a.rearrange("a n -> (a n)")
            row_tok[0] = load(row[:, :], a[c0:c0 + 1024].rearrange("(a n) -> a n", a=1).broadcast_to([P, 1024]), s_row,
                              *row_free[0])

        row_tok = [None]

        def post_evac(yg, t, n, p, m):
            c = slice(n * 512, n * 512 + 512)
            v = tt(V, yg[:, t, c], p, row[:, c], ALU.mult, m, row_tok[0])
            row_free[0] = [v]
            return act(p, p, ACT.Square, v, accum_out=st[:, 8 + 2 * t + n:9 + 2 * t + n])

        def post(yg, t, half):
            a = A.last()
            r = st[:, 12 + t:13 + t]
            v = tt(V, r, st[:, 8 + 2 * t:9 + 2 * t], st[:, 9 + 2 * t:10 + 2 * t], ALU.add, a)
            q = 4.0 if half else 1.0
            a = act(r, r, ACT.Sqrt, v, scale=q / 1024, bias=C("eps", 2 if half else 0, 1))
            recip(r, r, a)
            return stt(x[:, t, :], yg[:, t, :], r, x[:, t, :], ALU.mult, ALU.add)

        def early_sqrt():
            act(st[:, 15:16], C("eps", 0, 1), ACT.Sqrt)

        tm_banks = {}

        def tm_out(key, lhs, khs, evac, kind="main", nk=8):
            if khs[0] == 0:
                tm_banks[key] = [bank(kind), bank(kind)]
            bs = tm_banks[key]
            w = []
            for t in range(2):
                for i, kh in enumerate(khs):
                    if t == 0:
                        w.append(take())
                    hi, lo = w[i]
                    for k in range(2):
                        kk = 2 * kh + k
                        l = [z[:, kk, t * 128:t * 128 + 128] for z in lhs.p]
                        m = mm3(PS[bs[t]][:, :], l, (hi[:, k, :], lo[:, k, :]), kk == 0, kk == nk - 1,
                                *(free[bs[t]] if kk == 0 else []), lhs.tok[kk], inc=(k == 1))
                        if k == 0:
                            yield
                    if i < len(khs) - 1:
                        yield
                if t == 1:
                    give(n=len(khs))
                if 2 * khs[-1] + 2 == nk:
                    free[bs[t]] = [evac(t, PS[bs[t]][:, :], m)]
                yield

        held = [None]

        def fm_tiles(n, rhs, evac, nk=8, kind="main", hold=False):
            per = 8 // nk
            for j0 in range(0, n, 2):
                b = bank(kind)
                w = min(2, n - j0)
                for j in range(j0, j0 + w):
                    if j % per == 0:
                        held[0] = take()
                    hi, lo = held[0]
                    c0 = (j % per) * 128
                    for k in range(nk):
                        m = mm3(PS[b][:, (j - j0) * 256:(j - j0) * 256 + 256], (hi[:, k, c0:c0 + 128], lo[:, k, c0:c0 + 128]),
                                (rhs.p[0][:, k, :], rhs.p[1][:, k, :]), k == 0, k == nk - 1, free[b], rhs.tok[k],
                                inc=(k == nk - 1))
                        if k % 2 == 1 and not (k == nk - 1 and (j == j0 + w - 1 or (j + 1) % per == 0)):
                            yield
                    if ((j + 1) % per == 0 or j == n - 1) and not (hold and j == n - 1):
                        give()
                        if j < j0 + w - 1:
                            yield
                free[b] = [evac(j0, PS[b][:, 0:256 * w].rearrange("p (j t) -> p j t", t=256), m)]
                yield

        def attention(bufs, heads, logits, mask, vt, nkt, outp):
            z, pt, red = bufs
            pt_free = []
            for g in range(0, len(heads), 4):
                for t in range(2):
                    n = 128 * nkt[t]
                    for h0 in range(0, 4, 2):
                        b = bank("side")
                        T.wait(free[b])
                        for j in range(2):
                            k = logits(heads[g + h0 + j], t, PS[b][:, j * n:(j + 1) * n])
                        i = PS[b][:, 0:2 * n].rearrange("p (j k) -> p j k", j=2)
                        m = mask(t)
                        if m is None:
                            v = cp(V, z[t][:, h0:h0 + 2, :], i, k, pt_free)
                        else:
                            v = tt(V, z[t][:, h0:h0 + 2, :], i, m.unsqueeze(1).broadcast_to([P, 2, n]), ALU.add, k, pt_free)
                        free[b] = [v]
                        yield
                    mx, sm, rc = (red[:, t, q, :] for q in range(3))
                    zt = z[t]
                    v = V(lambda e, mx=mx, zt=zt: e.tensor_reduce(mx, zt[:, :, :], AX.X, ALU.max, negate=True), cost=0.8)
                    for h in range(4):
                        a = act(zt[:, h, :], zt[:, h, :], ACT.Exp, v, bias=red[:, t, 0, h:h + 1],
                                accum_out=red[:, t, 1, h:h + 1])
                    recip(rc, sm, a)
                    v = tt(V, zt[:, :, :], zt[:, :, :], rc.unsqueeze(2).broadcast_to([P, 4, n]), ALU.mult)
                    yield
                    for h0 in range(0, 4, 4 // nkt[t]):
                        b = bank("side")
                        nh = 4 // nkt[t]
                        for j in range(nh):
                            for k in range(nkt[t]):
                                m = tr(PS[b][:, (j * nkt[t] + k) * 128:(j * nkt[t] + k) * 128 + 128],
                                       zt[:, h0 + j, k * 128:k * 128 + 128], v, free[b], inc=True)
                        o = pt[:, h0:h0 + nh, 0:nkt[t], t * 128:t * 128 + 128]
                        i = PS[b][:, :].rearrange("p (j k q) -> p j k q", j=nh, k=nkt[t])
                        c = cp(V, o, i, m, pt_free)
                        free[b] = [c]
                    yield
                for j in range(4):
                    h = heads[g + j]
                    b = bank("side")
                    if nkt[0] == 2:
                        mm(PS[b][:, 0:256], vt(h, 0), pt[:, j, 0, :], True, False, c, free[b])
                        m = mm(PS[b][:, 0:256], vt(h, 1), pt[:, j, 1, :], False, True, inc=True)
                    else:
                        mm(PS[b][:, 0:256], vt(h, 0), pt[:, j, 0, :], True, False, c, free[b])
                        m = mm(PS[b][:, 128:256], vt(h, 1), pt[:, j, 1, 128:256], False, True, inc=True)
                    free[b] = [outp(h, PS[b][:, 0:256], m)]
                    yield
                pt_free = [m]

        t_vec = load(vec[:, :], vecs, s_vecs)
        for e in (V, A):
            e.wait(t_vec)
        first = {}

        def load_first():
            first["x"] = load(x[:, :, :], I["x"].rearrange("a (t p) d -> p (a t) d", p=P), s_const)
            first["con"] = load(con[:, :], consts[:, 0:NC], s_const)

        B1 = Scope()
        za = B1("za", [P, 4, 256])
        zb = B1("zb", [P, 4, 256])
        qq = B1("qq", [P, 8, 256])
        qT, qiT = qq[:, 0:4, :], qq[:, 4:8, :]
        kiT = B1("kiT", [P, 256])
        lat = B1("lat", [P, 2, 128])
        latT = B1("latT", [P, 256])
        wi = B1("wi", [P, 2, 8])
        gab = B1("gab", [P, 16, 256])
        w2a2 = B1("w2a2", [P, 512])
        wukT = B1("wukT", [P, 4, 128])
        wuv = B1("wuv", [P, 512])
        kvg = B1("kvg", [P, 128])
        relb = B1("relb", [32, 8])
        DSA = {}
        for n, sh in [("qabs", [P, 8, 256]), ("hk0", [P, 8, 128]), ("hk1", [P, 8, 256]), ("sc0", [P, 128]),
                      ("sc1", [P, 256]), ("wk0", [P, 128]), ("wk1", [P, 256]), ("rl", [P, 2, 2, 256]),
                      ("top", [P, 8]), ("olT", [P, 2, 256]), ("z0", [P, 4, 128]), ("red", [P, 2, 3, 4])]:
            DSA[n] = B1(n, sh)
        small = {}

        def load_small():
            load(w2a2[0:64, :], I["w2"].rearrange("a r n -> (a r) n"), s_misc)
            load(w2a2[64:128, :], I["a2"].rearrange("a r n -> (a r) n"), s_misc)
            load(wukT[:, :, :], I["w_uk"], s_misc)
            load(wuv[:, :], I["w_uv"].rearrange("a c h d -> (a c) (h d)"), s_misc)
            load(kvg[:, :], I["kv_norm_g"].broadcast_to([P, 128]), s_misc)
            load(hot, consts[0:32, NC:NC + 384], s_misc, *row_free[0])
            small["t"] = load(relb[:, :], I["rel_bias"], s_misc)

        def distance_bias():
            b = bank("side")
            m = mm(PS[b][0:8, 0:384], relb[:, :], hot, True, True, small["t"], free[b], inc=True)
            q = cp(V, biasv, PS[b][0:8, 0:384], m)
            free[b] = [q]
            DSA["t_bias"] = q
            row_free[0] = [m]

        def store_bias():
            DSA["t_b"] = load(bias_dram, biasv, s_misc, DSA["t_bias"])

        def load_bias():
            for t in range(2):
                n = 128 * (t + 1)
                DSA["t_hk"] = load(DSA[f"hk{t}"][:, :, :], bass.AP(bias_dram.tensor, 128 * (1 - t), [[1, 128], [384, 8], [1, n]]),
                                   s_misc, DSA["t_b"])

        M1 = Scope()
        cs = B1("cs", [P, 8])
        ones1 = B1("ones1", [P, 1])
        acc = row[:, :].rearrange("p (z n) -> p z n", z=4)
        mod = M1("mod", [P, 16])
        xn0 = M1("xn0", [P, 2, 1024])
        tmp0 = M1("tmp0", [P, 2, 256])
        hot = row[0:32, 0:384]
        biasv = row[0:8, 512:896]
        hsc = M1("hsc", [P, 8])
        S = M1
        a = act(cs[:, :], vcol("c", 0, 8), ACT.Sigmoid)
        V(lambda e: e.memset(ones1[:, :], 1.0))
        v = tt(V, cs[:, :], cs[:, :], vcol("c", 0, 8), ALU.mult, a)
        cs_tok = v
        acc_free, acc_tok = [[], [], [], []], {}
        V_COLS = [1, 2, 4, 5, 7]
        ada = I["ada_w"].rearrange("a r n -> (a r) n")

        def ada_cols(j):
            pe = j % 3 == 0
            z = V_COLS.index(j) % 4 if not pe else 0
            o = acc[:, z, :]
            for kh in range(2):
                w = take(T if pe else V)
                for k in range(4):
                    kk = 4 * kh + k
                    if pe:
                        for f in range(2):
                            m = mm(PS[2 + 5 * f][:, j:j + 1], w[:, k, f * 128:f * 128 + 128], cs[:, kk:kk + 1], kk == 0, kk == 7,
                                   cs_tok, inc=True)
                    elif kk == 0:
                        v = ts(V, o, w[:, 0, :], cs[:, 0:1], None, ALU.mult, None, acc_free[z])
                    else:
                        v = stt(o, w[:, k, :], cs[:, kk:kk + 1], o, ALU.mult, ALU.add)
                give(T if pe else V)
            if not pe:
                acc_tok[j] = v

        def ada_sum(j):
            z = V_COLS.index(j) % 4
            for f in range(2):
                m = mm(PS[2 + 5 * f][:, j:j + 1], acc[:, z, f * 128:f * 128 + 128], ones1[:, :], True, True, acc_tok[j], inc=True)
            acc_free[z] = row_free[0] = [m]
            if j == 7:
                mv, bv = (q.rearrange("p (j f) -> p j f", f=2) for q in (mod[:, 0:16], vcol("ada_b", 0, 16)))
                for f in range(2):
                    free[2 + 5 * f] = [tt(V, mv[:, :, f], PS[2 + 5 * f][:, 0:8], bv[:, :, f], ALU.add, m)]
                stt(hsc[:, :], mod[:, 8:16], 1.0, vcol("norm_g", 0, 8), ALU.add, ALU.mult)

        def ada_slabs(j):
            for kh in range(2):
                slab([(None, ada[512 * kh:512 * kh + 512, 256 * j:256 * j + 256].rearrange("(k p) n -> p k n", p=P))], (4, 256), True)
            tasks.append((lambda: ada_cols(j)) if j < 8 else lambda: gate_rows(j))
        def gate_rows(j):
            b = bank("main")
            for kh in range(2):
                w = take(T)
                for k in range(4):
                    kk = 4 * kh + k
                    m = mm(PS[b][:, 0:256], cs[:, kk:kk + 1].broadcast_to([P, 128]), w[:, k, :], kk == 0, kk == 7, free[b],
                           inc=(k == 3))
                    if k % 2 == 1:
                        yield
                give(T)
            o = row[:, 256 * j - 2048:256 * j - 1792]
            free[b] = [tt(V, o, PS[b][:, 0:256], o, ALU.add, m, row_tok[0])]
            row_free[0] = free[b]
            yield

        for j in range(8):
            ada_slabs(j)
            if j == 1:
                do(load_first)
            for i in {3: [1], 5: [2], 6: [4]}.get(j, []):
                do(lambda i=i: ada_sum(i))
            if j == 4:
                do(lambda: [e.wait(first["con"]) for e in (V, A, G, T)])
                do(lambda: first.update(n=norm(xn0, tmp0, x, "norm_g", first["x"], first["x"], bias=lambda f: mod[:, f:f + 1],
                                               scale=lambda f: hsc[:, f:f + 1])))
            if j in (4, 6):
                do(lambda: next(first["n"]))
        do(lambda: (next(first["n"]), ada_sum(5), ada_sum(7), A.wait(V.last())))

        def first_norm():
            run(first["n"])
            load_small()
        do(first_norm)

        w_in = I["w_in"].rearrange("a r n -> (a r) n")
        RW = [None]
        SC = [None]
        R = {}

        def open_rwkv():
            M1.close()
            enter()
            RW[0] = Scope()
            SC[0] = Scope()
            for n in ("AR",):
                R[n] = RW[0](n, [P, 4, 2, 2, 128])
            for n in ("bt", "kt", "bonus"):
                R[n] = RW[0](n, [P, 4, 256])
            R["VT"] = RW[0]("VT", [P, 2, 512])
            R["Y"] = x[:, 1, :].rearrange("p (c h v) -> p c h v", c=2, v=64)
            R["esc"] = RW[0]("esc", [P, 4])
            R["rkv"] = SC[0]("rkv", [P, 13, 256])
            for n in ("c", "lw", "a", "kkn"):
                R[n] = SC[0](n, [P, 4, 256])
            R["mid"] = SC[0]("mid", [P, 8])
            R["u"] = x[:, 0, :].rearrange("p (z j t) -> p z j t", z=2, j=2)
            R["d"] = x[:, 1, :].rearrange("p (z j t) -> p z j t", z=2, j=2)
        do(open_rwkv)

        def shifted(t0):
            def evac(j0, p, m):
                n = p.shape[1]
                z = ((t0 + j0) // 2) % 2
                u, d = R["u"][:, z, 0:n, :], R["d"][:, z, 0:n, :]
                a = cp(A, u, p, m, R.get(("u", z), []))
                tt(V, d[:, :, 1:256], u[:, :, 0:255], u[:, :, 1:256], ALU.subtract, a)
                v = ts(V, d[:, :, 0:1], u[:, :, 0:1], -1.0, None, ALU.mult, None)
                for j in range(n):
                    f = t0 + j0 + j
                    v = stt(R["rkv"][:, f, :], d[:, j, :], vcol("shift_mu", f), u[:, j, :], ALU.mult, ALU.add)
                R["u", z] = [v]
                R["tok"] = v
                return a
            return evac

        def rkv_cols(j):
            fmslab(w_in, 256 * j, 256, lambda: fm_tiles(2, h_, shifted(2 * j)))
        rkv_cols(2)
        rkv_cols(3)
        do(distance_bias)
        fmslab(w_in, 1536, 128, lambda: fm_tiles(1, h_, shifted(12)))
        do(store_bias)

        def rwkv():
            r, k, v_, wa = R["rkv"][:, 0:4, :], R["rkv"][:, 4:8, :], R["rkv"][:, 8:12, :], R["rkv"][:, 12, :]
            AR, bt, kt, c, lw, a, kkn = (R[n] for n in ("AR", "bt", "kt", "c", "lw", "a", "kkn"))
            sq = kt
            t = act(wa[0:64, :], wa[0:64, :], ACT.Tanh, R["tok"])
            yield
            for dst, p0, cb in ((lw, 0, "w0"), (a, 64, "a0")):
                for f in range(0, 4, 2):
                    b = bank("side")
                    for j in range(2):
                        m = mm(PS[b][:, j * 256:j * 256 + 256], w2a2[p0:p0 + 64, (f + j) * 128:(f + j) * 128 + 128],
                               wa[p0:p0 + 64, :], True, True, t, small["t"], free[b], inc=True)
                    for j in range(2):
                        q = act(dst[:, f + j, :], PS[b][:, j * 256:j * 256 + 256], ACT.Sigmoid, m, bias=vcol(cb, f + j))
                    free[b] = [q]
                yield
            for f in range(4):
                s = act(sq[:, f, :], k[:, f, :], ACT.Square, scale=vcol("k_k", f))
            for f in range(4):
                ts(V, kkn[:, f, :], k[:, f, :], vcol("k_k", f), None, ALU.mult, None)
            yield s
            for f in range(0, 4, 2):
                b = bank("side")
                for j in range(2):
                    m = mm(PS[b][:, j * 256:j * 256 + 256], C("ones64"), sq[:, f + j, :], True, True, s, free[b], inc=True)
                n = act(bt[:, f:f + 2, :], PS[b][:, :].rearrange("p (j t) -> p j t", j=2), ACT.Sqrt, m)
                free[b] = [n]
            ts(V, lw[:, :, :], lw[:, :, :], -math.exp(-0.5), None, ALU.mult, None, q)
            for f in range(4):
                V(lambda e, f=f: e.tensor_tensor_scan(c[:, f, :], C("reset"), lw[:, f, :], 0.0, ALU.mult, ALU.add), cost=0.35)
            yield
            for f in range(4):
                ts(V, bt[:, f, :], bt[:, f, :], 1e-12, None, ALU.max, None, n)
                recip(bt[:, f, :], bt[:, f, :])
                tt(V, kkn[:, f, :], kkn[:, f, :], bt[:, f, :], ALU.mult)
                yield
            for f in range(4):
                ts(V, bt[:, f, :], a[:, f, :], -1.0, vcol("k_a", f), ALU.add, ALU.mult)
            stt(k, bt[:, :, :], 1.0, k, ALU.add, ALU.mult)
            yield
            cv = c[:, :, :].rearrange("p f (c t) -> p (f c) t", c=2)
            cp(V, R["mid"][:, :], cv[:, :, 63])
            tt(V, cv, cv, R["mid"][:, :].unsqueeze(2).broadcast_to([P, 8, 128]), ALU.subtract)
            v = tt(V, lw[:, :, :], c[:, :, :], lw[:, :, :], ALU.subtract)
            mid = R["mid"][:, :].rearrange("p (f c) -> p f c", c=2)
            v = tt(V, R["esc"][:, :], c[:, :, 127], mid[:, :, 1], ALU.add)
            ARv = AR[:, :, :, :, :].rearrange("p f c a t -> p (f c) a t")
            act(R["esc"][:, :], R["esc"][:, :], ACT.Exp, v)
            yield
            a0 = act(ARv[:, :, 0, :], lw[:, :, :].rearrange("p f (c t) -> p (f c) t", c=2), ACT.Exp)
            a1 = act(ARv[:, :, 1, :], cv, ACT.Exp)
            a2 = act(kt[:, :, :], c[:, :, :], ACT.Exp, scale=-1.0)
            tt(V, bt[:, :, :], kkn[:, :, :], a[:, :, :], ALU.mult)
            stt(ARv[:, :, 0, :], ARv[:, :, 0, :], -1.0, kkn[:, :, :].rearrange("p f (c t) -> p (f c) t", c=2),
                ALU.mult, ALU.mult, a0)
            yield
            tt(V, bt[:, :, :], bt[:, :, :], kt[:, :, :], ALU.mult, a2)
            tt(V, kt[:, :, :], kt[:, :, :], k, ALU.mult)
            while not R.get("r and v"):
                yield WAIT
            sq = kkn
            for f in range(4):
                v = stt(sq[:, f, :], r[:, f, :], vcol("r_k", f), k[:, f, :], ALU.mult, ALU.mult, R["tok"])
            yield
            for f in range(0, 4, 2):
                b = bank("side")
                for j in range(2):
                    m = mm(PS[b][:, j * 256:j * 256 + 256], C("ones64"), sq[:, f + j, :], True, True, v, free[b], inc=True)
                free[b] = [tt(V, R["bonus"][:, f:f + 2, :], PS[b][:, :].rearrange("p (j t) -> p j t", j=2),
                              v_[:, f:f + 2, :], ALU.mult, m)]
            v = tt(V, ARv[:, :, 1, :], ARv[:, :, 1, :], r.rearrange("p f (c t) -> p (f c) t", c=2), ALU.mult, a1)
            yield
            for t in range(2):
                b = bank("side")
                for f in range(4):
                    m2 = tr(PS[b][:, f * 128:f * 128 + 128], v_[:, f, t * 128:t * 128 + 128], v, free[b], inc=True)
                vt_tok = cp(A, R["VT"][:, t, :], PS[b][:, :], m2)
                free[b] = [vt_tok]
            yield
            SC[0].close()
            for e in (V, A, G):
                e.wait(m2, V.last(), A.last(), G.last())
            SC[0] = Scope()
            M = {"vt": vt_tok, "v": v}
            for n, sh in [("TB", [P, 8, 2, 128]), ("TK", [P, 8, 2, 128]), ("W", [P, 8, 128]), ("WT", [P, 8, 128]),
                          ("OF", [P, 8, 128]), ("XU", [P, 2, 4, 64]), ("S0", [P, 2, 64]), ("btT", [P, 2, 2, 128])]:
                M[n] = SC[0](n, sh)
            M["mu"] = SC[0]("mu", [P, 2, 2, 2, 2])
            M["X1"] = x[:, 0, :].rearrange("p (n t) -> p n t", t=128)
            R["M"] = M
            while "y0" not in R or "y1" not in R:
                yield WAIT
            R["ya"] = [R["y0"], R["y1"]]

        def rwkv_heads(z):
            while "M" not in R:
                yield WAIT
            M = R["M"]
            AR, bt, kt, VT, Y = (R[n] for n in ("AR", "bt", "kt", "VT", "Y"))
            NM = 4
            TB, TK, W, WT, OF, X1 = (M[n][:, NM * z:NM * z + NM] for n in ("TB", "TK", "W", "WT", "OF", "X1"))
            XU = M["XU"][:, :, 2 * z:2 * z + 2, :]
            S0 = M["S0"][:, z, :]
            btT = M["btT"][:, :, z, :]
            G(lambda e: e.memset(TB, 0.0), cost=2.2)
            zt = G(lambda e: e.memset(TK, 0.0), cost=2.2)
            tri = con[:, CON["strict"][0]:CON["strict"][0] + 256].bitcast(U32)
            off = lambda l: C("off", 128 * l, 128).unsqueeze(1).broadcast_to([P, NM, 128])
            idb = ident.unsqueeze(1).broadcast_to([P, NM, 128])
            TT = TB[:, :, 0, :]
            war, x_free = [], []

            def halves(buf, l, c):
                return buf.rearrange("p n (a c b) -> p (n a) c b", c=2, b=1 << l)[:, :, c, :]

            def half(buf, n, l, c):
                return buf[:, n, :].rearrange("p (a c b) -> p a c b", c=2, b=1 << l)[:, :, c, :]

            def out(b, n, l):
                return PS[b][:, n * 64:n * 64 + 64].rearrange("p (a b) -> p a b", b=1 << l)

            def all_out(b, l):
                return PS[b][:, 0:64 * NM].rearrange("p (a b) -> p a b", b=1 << l)
            for f in (z, z + 2):
                for src, dst in ((bt, TB), (kt, TK)):
                    for i in range(2):
                        p0 = i * 64
                        b = bank("side")
                        for c_ in range(2):
                            m = mm(PS[b][:, c_ * 256:c_ * 256 + 256], src[p0:p0 + 64, f, c_ * 128:c_ * 128 + 128],
                                   AR[p0:p0 + 64, f, c_, :, :].rearrange("p a t -> p (a t)"), True, True, M["v"], free[b], inc=True)
                        o = dst[:, 2 * i:2 * i + 2, :, :].rearrange("p c a t -> p c (a t)")
                        q = V(lambda e, o=o, b=b: e.copy_predicated(
                            o, tri.unsqueeze(1).broadcast_to([P, 2, 256]), PS[b][:, :].rearrange("p (c n) -> p c n", c=2)),
                            m, zt, war, cost=0.6)
                        free[b] = [q]
                    if src is bt:
                        yield
                z_tok = G(lambda e: e.memset(X1, 0.0), x_free, cost=1.0)
                o_tok = tt(V, OF, TT, off(0), ALU.mult, x_free)
                wt_tok = tt(V, WT, OF, idb, ALU.add)
                yield o_tok
                b = bank("side")
                for n in range(NM):
                    m = mm(PS[b][:, n * 128:n * 128 + 128], OF[:, n, :], ident, True, True, o_tok, free[b], inc=True)
                w_tok = tt(V, W, PS[b][:, :].rearrange("p (j t) -> p j t", j=NM), idb, ALU.add, m)
                free[b] = [w_tok]
                o_tok = tt(V, OF, TT, off(1), ALU.mult, m)
                yield
                for l in range(1, 7):
                    b = bank("side")
                    for n in range(NM):
                        m = mm(out(b, n, l), OF[:, n, :], half(W, n, l, 0), True, True, o_tok, w_tok, free[b], inc=True)
                    x_tok = cp(A, halves(X1, l, 0), all_out(b, l), m, z_tok)
                    free[b] = [x_tok]
                    if l < 6:
                        o_tok = tt(V, OF, TT, off(l + 1), ALU.mult, m)
                    yield x_tok
                    if l < 6:
                        b2 = bank("side")
                        for n in range(NM):
                            m2 = mm(out(b2, n, l), WT[:, n, :], half(X1, n, l, 0), True, True, x_tok, wt_tok, free[b2], inc=True)
                    b = bank("side")
                    for n in range(NM):
                        m = mm(out(b, n, l), X1[:, n, :], half(WT, n, l, 1), True, True, x_tok, wt_tok, free[b], inc=True)
                    if l < 6:
                        zc = X1.rearrange("p n (a c d b) -> p (n a) c d b", c=2, d=2, b=1 << l)[:, :, 1, 0, :]
                        z_tok = G(lambda e, zc=zc: e.memset(zc, 0.0), m, cost=0.4)
                        ws = halves(W, l, 0)
                        w_tok = tt(V, ws, ws, all_out(b2, l), ALU.add, m2)
                        free[b2] = [w_tok]
                    ws = halves(WT, l, 1)
                    wt_tok = tt(V, ws, ws, all_out(b, l), ALU.add, m)
                    free[b] = [wt_tok]
                    yield w_tok if l < 6 else wt_tok
                x_free = [m]
                b = bank("side")
                for s_, src in enumerate((bt, kt)):
                    m = tr(PS[b][:, s_ * 128:s_ * 128 + 128], src[:, f, 0:128], free[b], inc=True)
                bt_tok = cp(A, btT, PS[b][:, 0:256].rearrange("p (s k) -> p s k", s=2), m)
                free[b] = [bt_tok]
                s_tok = []
                for c_ in range(2):
                    for i in range(2):
                        h, p0 = 2 * f + i, i * 64
                        b = bank("side")
                        m = mm(PS[b][:, 0:64], TK[:, 2 * i + c_, 0, :], VT[:, c_, h * 64:h * 64 + 64], True, c_ == 0, free[b],
                               M["vt"], wt_tok, inc=True)
                        if c_ == 1:
                            m = mm(PS[b][:, 0:64], AR[p0:p0 + 64, f, 1, 0, :], S0[p0:p0 + 64, :], False, True, s_tok, inc=True)
                        q = cp(V, XU[:, 0, i, :], PS[b][:, 0:64], m)
                        free[b] = [q]
                    yield
                    b = bank("side")
                    for i in range(2):
                        m = mm(PS[b][:, i * 64:i * 64 + 64], WT[:, 2 * i + c_, :], XU[:, 0, i, :], True, True, q, wt_tok, free[b], inc=True)
                    q = cp(V, XU[:, 1, :, :], PS[b][:, 0:128].rearrange("p (i v) -> p i v", i=2), m)
                    free[b] = [q]
                    yield
                    if c_ == 0:
                        b = bank("side")
                        o = PS[b][:, 0:128]
                        mm(o, btT[:, 0, :], XU[:, 1, :, :].rearrange("p i v -> p (i v)"), True, False, q, bt_tok, free[b])
                        m = mm(o, btT[:, 1, :], VT[:, 0, 2 * f * 64:(2 * f + 2) * 64], False, True, inc=True)
                        for p0 in (0, 64):
                            s_tok = [ts(V, S0[p0:p0 + 64, :], PS[b][p0:p0 + 64, p0:p0 + 64], R["esc"][p0:p0 + 64, f:f + 1],
                                        None, ALU.mult, None, m)]
                        free[b] = s_tok
                    for i in range(2):
                        h, p0 = 2 * f + i, i * 64
                        b = bank("side")
                        o = PS[b][:, 0:64]
                        mm(o, TB[:, 2 * i + c_, 1, :], XU[:, 1, i, :], True, False, q, free[b])
                        m = mm(o, TK[:, 2 * i + c_, 1, :], VT[:, c_, h * 64:h * 64 + 64], False, c_ == 0, inc=True)
                        if c_ == 1:
                            m = mm(o, AR[p0:p0 + 64, f, 1, 1, :], S0[p0:p0 + 64, :], False, True, inc=True)
                        y_tok = cp(A, Y[:, c_, h, :], o, m)
                        free[b] = [y_tok]
                    war = [m]
                    yield s_tok[0] if c_ == 0 else y_tok
                yv = Y[:, :, 2 * f:2 * f + 2, :]
                mu, var = M["mu"][:, z, 0, :, :], M["mu"][:, z, 1, :, :]
                wide = lambda q: q.unsqueeze(3).broadcast_to([P, 2, 2, 64])
                ysq = W[:, 0:2, :].rearrange("p c (h v) -> p c h v", h=2)
                tmp = W[:, 2:4, :].rearrange("p c n -> p (c n)")
                V(lambda e, yv=yv, mu=mu: e.tensor_reduce(mu, yv, AX.X, ALU.add), y_tok, cost=0.35)
                ts(V, mu, mu, 1.0 / 64, None, ALU.mult, None)
                v = tt(V, yv, yv, wide(mu), ALU.subtract)
                q = act(ysq, yv, ACT.Square, v)
                yield q
                v = V(lambda e, var=var, ysq=ysq: e.tensor_reduce(var, ysq, AX.X, ALU.add), q, cost=0.35)
                q = act(var, var, ACT.Sqrt, v, scale=1.0 / 64, bias=C("eps", 1, 1))
                recip(var, var, q)
                v = tt(V, yv, yv, wide(var), ALU.mult)
                while not R.get("za zb"):
                    yield WAIT
                yield v
                b = bank("side")
                for t in range(2):
                    m = tr(PS[b][:, t * 128:t * 128 + 128], Y[:, t, 2 * f:2 * f + 2, :].rearrange("p h v -> p (h v)"),
                           v, free[b], inc=True)
                q = act(tmp, PS[b][:, 0:256], ACT.Identity, m, scale=vcol("lnx_g", f), bias=vcol("lnx_b", f))
                free[b] = [q]
                tt(V, tmp, tmp, R["bonus"][:, f, :], ALU.add, q)
                y_tok = tt(V, za[:, f, :], tmp, za[:, f, :], ALU.mult)
            R[f"y{z}"] = y_tok

        def silu_fm(dst, t0):
            def evac(j0, p, m):
                a = act(dst[:, t0 + j0:t0 + j0 + 2, :], p, ACT.Sigmoid, m)
                return tt(V, dst[:, t0 + j0:t0 + j0 + 2, :], dst[:, t0 + j0:t0 + j0 + 2, :], p, ALU.mult, a)
            return evac

        def copy_fm(dst, t0):
            return lambda j0, p, m: cp(V, dst[:, t0 + j0:t0 + j0 + p.shape[1], :], p, m)

        def sig_fm(dst, t0, bias=None):
            def evac(j0, p, m):
                if bias is None:
                    return act(dst[:, t0 + j0:t0 + j0 + 2, :], p, ACT.Sigmoid, m)
                for j in range(2):
                    a = act(dst[:, t0 + j0 + j, :], p[:, j, :], ACT.Sigmoid, m, bias=vcol(bias, t0 + j0 + j))
                return a
            return evac

        def ki_cols():
            def evac(j0, p, m):
                cp(V, kiT[64:128, :], p[64:128, 0, :], m)
                return cp(V, kiT[0:64, :], p[0:64, 1, :])
            yield from fm_tiles(2, h_, evac, hold=True)
            hi, lo = held[0]
            b = bank("main")
            for t in range(2):
                for k in range(8):
                    m = mm3(PS[b][:, t * 8:t * 8 + 8], [z[:, k, t * 128:t * 128 + 128] for z in hT],
                            (hi[:, k, 64:72], lo[:, k, 64:72]), k == 0, k == 7, free[b], inc=(k == 7))
            give()
            free[b] = [cp(V, wi[:, :, :], PS[b][:, 0:16].rearrange("p (t h) -> p t h", t=2), m)]

        def ckv_cols():
            hi, lo = take()
            b = bank("main")
            for t in range(2):
                for k in range(8):
                    m = mm3(PS[b][:, t * 128:t * 128 + 128], [z[:, k, t * 128:t * 128 + 128] for z in hT],
                            (hi[:, k, :], lo[:, k, :]), k == 0, k == 7, free[b], inc=(k == 7))
                    if k % 4 == 3 and k + t < 8:
                        yield
            give()
            free[b] = [cp(V, lat[:, :, :], PS[b][:, 0:256].rearrange("p (t c) -> p t c", t=2), m)]
            yield

        def dsa():
            A.wait(DSA["t_hk"])
            qabs, rl, top = DSA["qabs"], DSA["rl"], DSA["top"]
            hk, sc, wk = ([DSA[f"{n}{t}"] for t in range(2)] for n in ("hk", "sc", "wk"))
            olT = DSA["olT"]
            v = rms_rows(lat, 128, 4, rl[:, 0, 0, 0:128], R["dsa in"])
            for t in range(2):
                v = stt(lat[:, t, :], lat[:, t, :], st[:, 4 + t:5 + t], kvg[:, :], ALU.mult, ALU.mult, small["t"])
            yield
            b = bank("side")
            for t in range(2):
                m = tr(PS[b][:, t * 128:t * 128 + 128], lat[:, t, :], v, free[b], inc=True)
            lat_tok = cp(V, latT[:, :], PS[b][:, 0:256], m)
            free[b] = [lat_tok]
            yield
            for h in (0, 1, 4, 5):
                b = bank("side")
                for j in range(2):
                    p0 = (h % 2) * 64
                    m = mm(PS[b][:, j * 256:j * 256 + 256], wukT[p0:p0 + 64, h // 2 + j, :], qT[p0:p0 + 64, h // 2 + j, :],
                           True, True, R["dsa in"], free[b], inc=True)
                qa_tok = act(qabs[:, h:h + 3:2, :], PS[b][:, :].rearrange("p (j t) -> p j t", j=2), ACT.Copy, m, scale=0.125)
                free[b] = [qa_tok]
            yield
            rl_free = [[], []]
            for t in range(2):
                n = 128 * (t + 1)
                for h in (0, 1, 4, 5):
                    b = bank("side")
                    z = h % 2
                    for j in range(2):
                        p0 = z * 64
                        m = mm(PS[b][:, j * n:j * n + n], qiT[p0:p0 + 64, h // 2 + j, t * 128:t * 128 + 128],
                               kiT[p0:p0 + 64, 0:n], True, True, free[b], inc=True)
                    r = rl[:, z, :, 0:n]
                    a = act(r, PS[b][:, 0:2 * n].rearrange("p (j k) -> p j k", j=2), ACT.Relu, m, rl_free[z])
                    free[b] = [a]
                    for j in range(2):
                        if h + j == 0:
                            v = ts(V, sc[t][:, :], r[:, 0, :], wi[:, t, 0:1], None, ALU.mult, None, a)
                        else:
                            v = stt(sc[t][:, :], r[:, j, :], wi[:, t, h + 2 * j:h + 2 * j + 1], sc[t][:, :], ALU.mult, ALU.add, a)
                    rl_free[z] = [v]
                    yield
                s, w = sc[t], wk[t]
                tt(V, s[:, n - 128:n], s[:, n - 128:n], C("causal"), ALU.add)
                for i in range(8):
                    src = s if i == 0 else w
                    V(lambda e, src=src: e.max(top[:, :], src[:, :]), cost=0.3)
                    V(lambda e, src=src, w=w: e.match_replace(w[:, :], top[:, :], src[:, :], GONE), cost=0.3)
                    if i % 2 == 1:
                        yield
                ts(V, w[:, :], w[:, :], -2.0e38, NEG, ALU.is_ge, ALU.mult)
                tt(V, w[:, n - 128:n], w[:, n - 128:n], C("causal"), ALU.add)
            while not R.get("za zb"):
                yield WAIT

            def logits(h, t, o):
                n = 128 * (t + 1)
                mm(o, qabs[:, h, t * 128:t * 128 + 128], latT[:, 0:n], True, False, lat_tok, qa_tok, DSA["t_hk"])
                return mm(o, C("flip"), hk[t][:, h, :], False, True, inc=True)

            ol_free = [[], []]

            last = []

            def values(h, a):
                b = bank("side")
                p0 = (h % 2) * 64
                k = mm(PS[b][p0:p0 + 64, 0:256], wuv[:, h * 64:h * 64 + 64], olT[:, h % 2, :], True, True, a, free[b], inc=True)
                ol_free[h % 2] = [k]
                y = zb[p0:p0 + 64, h // 2, :]
                free[b] = [tt(V, y, PS[b][p0:p0 + 64, 0:256], y, ALU.mult, k)]

            def outp(h, p, m):
                a = cp(A, olT[:, h % 2, :], p, m, ol_free[h % 2])
                if last:
                    values(*last.pop())
                last.append((h, a))
                return a
            yield from attention(([DSA["z0"], rl[:, :, :, :].rearrange("p a b k -> p (a b) k")],
                                  qq[:, :, :].rearrange("p (j k) t -> p j k t", k=2), DSA["red"]),
                                 list(range(8)), logits, lambda t: wk[t][:, :], lambda h, kt_: lat[:, kt_, :], (1, 2), outp)
            values(*last.pop())

        g_rw = chain(rwkv)
        g_r = [chain(lambda z=z: rwkv_heads(z)) for z in range(2)]
        g_ds = chain(dsa)

        def col(c0, fn, n=256):
            fmslab(w_in, c0, n, fn)

        gtm = gab[:, :, :].rearrange("p f t -> p (f t)").rearrange("p (t n) -> p t n", t=2)

        def gate_cols(n):
            def evac(t, p, m):
                return act(gtm[:, t, 512 * n:512 * n + 512], p, ACT.Sigmoid, m)
            tmslabs(w_in, [(3912 + 512 * n, 512)], lambda kh: tm_out(f"g{n}", h_, kh, evac))
        beside(*g_r, g_rw)
        for j in (4, 5, 0, 1):
            rkv_cols(j)
        do(lambda: R.update({"r and v": True}))
        do(load_bias)
        col(2688, ckv_cols, 128)
        for j in range(4):
            col([2176, 2432, 3328, 3584][j], lambda j=j: fm_tiles(2, h_, copy_fm(qq, 2 * j)))
        fmslab(w_in, 3776, 128, lambda: None)
        fmslab(w_in, 3840, 128, ki_cols)
        do(lambda: R.update({"dsa in": V.last()}))
        beside(*g_r, g_rw, g_ds)
        for j in range(2):
            col(1664 + 256 * j, lambda j=j: fm_tiles(2, h_, silu_fm(za, 2 * j)))
        for j in range(2):
            col(2816 + 256 * j, lambda j=j: fm_tiles(2, h_, silu_fm(zb, 2 * j)))
        do(lambda: R.update({"za zb": True}))
        do(lambda: (row_free[0].append(DSA["t_hk"]), load_row("ada_b", 2048)))
        for n in range(4):
            gate_cols(n)
            ada_slabs(8 + n)
        finish(g_rw, *g_r, beside_=[g_ds])
        YA = {}

        def finish_a():
            v = V.last()
            SC[0].close()
            RW[0].close()
            for e in (A, G):
                e.wait(v)
            Y_ = YA["scope"] = Scope()
            YA["a"] = Ready(Y_("yahi", [P, 4, 256], F32R), Y_("yalo", [P, 4, 256], F32R))
            YA["b"] = Ready(Y_("ybhi", [P, 4, 256], F32R), Y_("yblo", [P, 4, 256], F32R))
            split_tiles(YA["a"], za[:, :, :])
            R["final_g"] = load(za[:, :, :].rearrange("p f t -> p (f t)"),
                                I["final_g"].rearrange("(a n) -> a n", a=1).broadcast_to([P, 1024]), s_misc,
                                V.last(), A.last(), G.last())
            first["x"] = load(x[:, :, :], I["x"].rearrange("a (t p) d -> p (a t) d", p=P), s_const, R["ya"])
        do(finish_a)
        beside(g_ds)

        def branch(tag, w, lhs, evac, half=None):
            wv = w.rearrange("a r n -> (a r) n")
            nk = wv.shape[0] // 128
            for n in range(2):
                tmslabs(wv, [(512 * n, 512)],
                        lambda kh, n=n: tm_out(f"{tag}{n}", lhs(), kh, lambda t, p, m: evac(n, t, p, m), nk=nk),
                        half if n == 0 else None)
        def first_branch(g):
            def evac(n, t, p, m):
                o = g()[:, t, 512 * n:512 * n + 512]
                return tt(V, o, o, p, ALU.mult, m)
            return evac

        def second_branch(g, ready):
            def evac(n, t, p, m):
                o = g()[:, t, 1024 + 512 * n:1536 + 512 * n]
                k = tt(V, o, o, p, ALU.mult, m)
                ready[n, t] = tt(V, o, o, g()[:, t, 512 * n:512 * n + 512], ALU.add)
                return k
            return evac

        def to_h(g, ready, me):
            g = g()
            for n in range(2):
                for t in range(2):
                    while (n, t) not in ready:
                        yield WAIT
                    yield ready[n, t]
                    b = bank("side")
                    for j in range(4):
                        m = tr(PS[b][:, j * 128:j * 128 + 128], g[:, t, 1024 + 512 * n + 128 * j:1152 + 512 * n + 128 * j],
                               ready[n, t], free[b], inc=True)
                    p = PS[b][:, :].rearrange("p (j q) -> p j q", j=4)
                    hi, lo = (q[:, 4 * n:4 * n + 4, t * 128:t * 128 + 128] for q in hT)
                    a = cp(A, hi, p, m)
                    free[b] = [tt(V, lo, p, hi, ALU.subtract, a)]
                    for f in range(4 * n, 4 * n + 4):
                        h_.tok[f] = (h_.tok[f] if t else []) + [a, V.last()]
                    me().part += 1
                    yield
        branch("pa", I["w_pa"], lambda: YA["a"], first_branch(lambda: gtm))
        finish(g_ds)
        def finish_b():
            split_tiles(YA["b"], zb[:, :, :], V.last())
            early_sqrt()
        do(finish_b)

        ready_1 = {}
        g_t = chain(lambda: to_h(lambda: gtm, ready_1, lambda: g_t))
        beside(g_t)
        branch("pb", I["w_pb"], lambda: YA["b"], second_branch(lambda: gtm, ready_1))
        do(lambda: advance_past(g_t, 2))

        def wo_evac(n, t, p, m):
            gate = row[:, 512 * n:512 * n + 512]
            y = gtm[:, t, 512 * n:512 * n + 512]
            k = tt(V, y, p, gate, ALU.mult, m)
            row_free[0] = [k]
            o = x[:, t, 512 * n:512 * n + 512]
            x_tok[t] = tt(V, o, o, y, ALU.add, first["x"])
            return k
        branch("wo", I["w_o"], lambda: h_, wo_evac, half=g_t)

        def after_block1():
            for t in range(2):
                v = x_tok[t]
                r = st[:, t:t + 1]
                act(gab[:, 4 * t:4 * t + 4, :].rearrange("p f t -> p (f t)"), x[:, t, :], ACT.Square, v, accum_out=r)
                a = act(r, r, ACT.Sqrt, scale=1.0 / 1024, bias=C("eps", 0, 1))
                recip(r, r, a)
                x_tok[t] = stt(x[:, t, :], x[:, t, :], r, za[:, :, :].rearrange("p f t -> p (f t)"), ALU.mult, ALU.mult,
                               R["final_g"])
            YA["scope"].close()
            B1.close()
            enter()
        do(after_block1)

        def ffn(tag, w_in_, w_down, pre, post_row):
            wv = w_in_.rearrange("a r n -> (a r) n")
            wd = w_down.rearrange("a r n -> (a r) n")
            L = {}

            def start():
                S = L["S"] = Scope()
                L["aT"] = [S("aThi" + tag, [P, 22, 256], F32R), S("aTlo" + tag, [P, 22, 256], F32R)]
                L["sg"] = S("sg" + tag, [P, 2, 256])
                L["ac"] = S("ac" + tag, [P, 2, 2, 256])
                L["yg"] = S("yg" + tag, [P, 2, 1024])
                L["pend"] = None
                load_row(post_row)
                L["norm"] = norm(L["yg"], None, x, pre, *x_tok, scaled=False)
                for _ in range(4):
                    next(L["norm"])
            do(start)

            def turn_over():
                if L["pend"] is None:
                    return
                u, v = L["pend"]
                z = u % 2
                b = bank("side")
                for j in range(2):
                    for t in range(2):
                        m = tr(PS[b][:, j * 256 + t * 128:j * 256 + t * 128 + 128], L["ac"][:, z, t, j * 128:j * 128 + 128],
                               v, free[b], inc=True)
                L["acfree"] = [m]
                p = PS[b][:, :].rearrange("p (j t) -> p j t", j=2)
                hi, lo = (q[:, 2 * u:2 * u + 2, :] for q in L["aT"])
                a = cp(A, hi, p, m)
                free[b] = [tt(V, lo, p, hi, ALU.subtract, a)]
                L["pend"] = None

            for u in range(11):
                def evac(t, p, m, u=u):
                    r = st[:, t:t + 1]
                    a = act(L["sg"][:, t, :], p[:, 0:256], ACT.Silu, m, L["r"], scale=r)
                    v = stt(L["ac"][:, u % 2, t, :], p[:, 256:512], r, L["sg"][:, t, :], ALU.mult, ALU.mult, a,
                            L.get("acfree", []))
                    if t == 1:
                        L["pend2"] = (u, v)
                    return v

                def unit(khs, u=u, ev=evac):
                    run(tm_out(f"f{tag}{u}", h_, khs, ev))
                    kh = khs[0]
                    if u + kh == 0:
                        run(L["norm"])
                        L["r"] = V.last()
                    if kh == 1:
                        turn_over()
                    elif kh == 3:
                        L["pend"] = L["pend2"]
                tmslabs(wv, [(256 * u, 256), (2816 + 256 * u, 256)], unit)

            def down(kk):
                if kk == 0:
                    turn_over()
                    L["bk"] = [bank(k) for k in ("main", "main", "main", "side")]
                    T.wait([V.last(), A.last()])
                    early_sqrt()
                kks = [kk] if tag == "1" or kk < 19 else [19, 20, 21]
                w = []
                for t in range(2):
                    for n in range(2):
                        b = L["bk"][2 * t + n]
                        for i, q in enumerate(kks):
                            if t + n == 0:
                                w.append(take())
                            hi, lo = w[i]
                            m = mm3(PS[b][:, :], [z[:, q, t * 128:t * 128 + 128] for z in L["aT"]],
                                    (hi[:, 0, n * 512:n * 512 + 512], lo[:, 0, n * 512:n * 512 + 512]), q == 0, q == 21,
                                    free[b] if q == 0 else [], inc=(q == 21 or t + n == 2))
                        if kks[-1] == 21:
                            free[b] = [post_evac(L["yg"], t, n, PS[b][:, :], m)]
                    if kks[-1] == 21:
                        x_tok[t] = post(L["yg"], t, True)
                        if tag == "2":
                            t_out[0] = load(out[0, t * 128:t * 128 + 128, :], x[:, t, :], s_out, x_tok[t])
                give(n=len(kks))
            for kk in range(22):
                slab([(None, wd[128 * kk:128 * kk + 128, :].rearrange("(k p) n -> p k n", p=P))], (1, 1024))
                if tag == "1" or kk < 20:
                    tasks.append(lambda kk=kk: down(kk))

            def end():
                L["S"].close()
                enter()
            do(end)

        ffn("1", I["ffn1_w_in_2"], I["ffn1_w_down_2"], "ffn1_pre_g_2", "ffn1_post_g_2")

        w2 = I["w_in_2"].rearrange("a r n -> (a r) n")
        Z = {}

        def mix_start():
            S = Z["S"] = Scope()
            for n in ("qb", "kb"):
                Z[n] = S(n, [P, 8, 256])
            Z["vb"] = S("vb", [P, 2, 1024])
            Z["ga"] = S("ga", [P, 8, 256])
            Z["lf"] = S("lf", [8, 4, 256])
            Z["sel"] = S("sel", [8, 8, 128])
            Z["lb"] = S("lb", [P, 2, 8])
            Z["gt"] = S("gt", [P, 16, 256])
            Z["fox"] = ([S("z0f", [P, 4, 128]), S("z1f", [P, 4, 256])], S("ptf", [P, 4, 2, 256]), S("redf", [P, 2, 3, 4]))
            H = Z["H"] = Scope()
            for n in ("b", "q", "k", "E"):
                Z[n] = H("h" + n, [P, 8, 256])
            Z["i"] = H("hi_", [P, 2, 1024])
            load_row("b_gate_2", 0)
            run(norm(Z["i"], None, x, "mix_pre_g_2", *x_tok))
            lb = Z["lb"]
            v = tt(V, lb[:, 0, :], vcol("hg_lb_logits_2", 0, 8), vcol("hg_lb_logits_2", 8, 8), ALU.subtract)
            a = act(lb[:, 0, :], lb[:, 0, :], ACT.Sigmoid, v)
            ts(V, lb[:, 1, :], lb[:, 0, :], -1.0, 1.0, ALU.mult, ALU.add, a)
            cp(V, Z["sel"][:, :, :], con[0:8, CON["ident"][0]:CON["ident"][0] + 8].unsqueeze(2).broadcast_to([8, 8, 128]))
        do(mix_start)

        def f_evac(t0):
            def evac(j0, p, m):
                a = act(Z["k"][:, t0:t0 + 2, :], p, ACT.Sigmoid, m)
                for j in range(2):
                    f = t0 + j
                    v = ts(V, Z["E"][:, f, :], Z["k"][:, f, :], Z["lb"][:, 1, f:f + 1], Z["lb"][:, 0, f:f + 1],
                           ALU.mult, ALU.add, a)
                ts(V, Z["k"][:, t0:t0 + 2, :], Z["E"][:, t0:t0 + 2, :], -1.0, 1.0, ALU.mult, ALU.add)
                return a
            return evac
        for j in range(4):
            fmslab(w2, 1024 + 256 * j, 256, lambda j=j: fm_tiles(2, h_, f_evac(2 * j)))
        for j in range(4):
            fmslab(w2, 256 * j, 256, lambda j=j: fm_tiles(2, h_, (lambda t0: lambda j0, p, m: silu_fm(Z["q"], t0)(j0, p, m))(2 * j)))

        def tm_copy(key, dst):
            for n in range(2):
                def evac(t, p, m, n=n):
                    return cp(V, dst()[:, t, n * 512:n * 512 + 512], p, m)
                yield n, evac

        def hgrn():
            b_, q_, k_, E = Z["b"], Z["q"], Z["k"], Z["E"]
            H = Z["H"]
            AD = H("AD", [P, 8, 2, 128])
            AX_ = H("AXc", [P, 8, 128])
            a = act(E[:, :, :], E[:, :, :], ACT.Ln, V.last())
            for f in range(8):
                v = V(lambda e, f=f: e.tensor_tensor_scan(b_[:, f, :], C("reset"), E[:, f, :], 0.0, ALU.mult, ALU.add), a, cost=0.35)
            zt = G(lambda e: e.memset(AD[:, :, :, :], 0.0))
            yield

            def masked(l, lhs, rhs, tok, part=range(8)):
                B = 64 if l is None else 1 << l
                mask = (ident if l is None else C("off", 128 * l, 128)).bitcast(U32)

                def odd(ap):
                    if l is None:
                        return ap
                    return ap.rearrange("p (a c b) -> p a c b", c=2, b=B)[:, :, 1, :]
                per = 4 if l is None else 8
                n = 512 // per
                for f in range(part[0], part[0] + len(part), per // 2):
                    b = bank("side")
                    for j in range(per // 2):
                        for t in range(2):
                            s = slice(t * 128, t * 128 + 128)
                            o = PS[b][:, (2 * j + t) * n:(2 * j + t) * n + n]
                            if l is not None:
                                o = o.rearrange("p (a b) -> p a b", b=B)
                            m = mm(o, lhs[:, f + j, s], odd(rhs[:, f + j, s]), True, True, tok, free[b], inc=True)
                    o = AD[:, f:f + per // 2, :, :].rearrange("p j t n -> p (j t) n")
                    d = PS[b][:, :].rearrange("p (j n) -> p j n", j=per)
                    k = mask.unsqueeze(1).broadcast_to([P, per, 128])
                    if l is not None:
                        o = o.rearrange("p j (a c b) -> p j a c b", c=2, b=B)[:, :, :, 1, :]
                        d = d.rearrange("p j (a b) -> p j a b", b=B)
                        k = odd(mask).unsqueeze(1).broadcast_to([P, per, 64 // B, B])
                    c = V(lambda e, o=o, d=d, k=k: e.copy_predicated(o, k, d), m, zt, cost=0.6)
                    free[b] = [c]
                    yield m

            for m in masked(None, k_, q_, V.last()):
                yield
            e_free = [m, m]
            for l in range(8):
                B = 1 << l
                for g in range(2):
                    f0 = 4 * g
                    part = lambda z: z[:, f0:f0 + 4, :].rearrange("p f t -> p (f t)")
                    ev = part(E)
                    if l < 7:
                        pv, pe, pk, pq = (part(z).rearrange("p (n z) -> p n z", z=2 * B) for z in (b_, E, k_, q_))
                        ref = pv[:, :, B - 1:B].broadcast_to([P, 512 // B, B])
                        tt(V, pe[:, :, 0:B], ref, pv[:, :, 0:B], ALU.subtract, e_free[g])
                        v = tt(V, pe[:, :, B:2 * B], pv[:, :, B:2 * B], ref, ALU.subtract)
                        a = act(ev, ev, ACT.Exp, v)
                    else:
                        pe, pk, pq = (part(z).rearrange("p (n z) -> p n z", z=256) for z in (E, k_, q_))
                        e_, bb = E[:, f0:f0 + 4, :], b_[:, f0:f0 + 4, :]
                        v = tt(V, e_[:, :, 0:128], bb[:, :, 127:128].broadcast_to([P, 4, 128]), bb[:, :, 0:128], ALU.subtract,
                               e_free[g])
                        act(e_[:, :, 128:256], bb[:, :, 128:256], ACT.Exp, e_free[g])
                        a = act(e_[:, :, 0:128], e_[:, :, 0:128], ACT.Exp, v)
                    yield
                    tt(V, pe[:, :, 0:B], pe[:, :, 0:B], pk[:, :, 0:B], ALU.mult, a)
                    v = tt(V, pe[:, :, B:2 * B], pe[:, :, B:2 * B], pq[:, :, B:2 * B], ALU.mult)
                    yield
                    if l < 7:
                        for m in masked(l, E, E, v, range(f0, f0 + 4)):
                            e_free[g] = m
                            yield
                    else:
                        b = bank("side")
                        for j in range(4):
                            m = mm(PS[b][:, j * 128:j * 128 + 128], E[:, f0 + j, 0:128], E[:, f0 + j, 128:256], True, True,
                                   v, free[b], inc=True)
                        c = cp(V, AX_[:, f0:f0 + 4, :], PS[b][:, :].rearrange("p (j n) -> p j n", j=4), m)
                        free[b] = [c]
                        yield
            o_ = b_[:, :, :].rearrange("p f t -> p (f t)").rearrange("p (t n) -> p t n", t=2)
            i_ = Z["i"]
            while not Z.get("i done"):
                yield WAIT
            for t in range(2):
                for f in range(0, 8, 4):
                    b = bank("side")
                    for j in range(4):
                        h = f + j
                        o = PS[b][:, j * 128:j * 128 + 128]
                        m = mm(o, AD[:, h, t, :], i_[:, t, h * 128:h * 128 + 128], True, t == 0, c, Z["i done"], free[b], inc=True)
                        if t == 1:
                            m = mm(o, AX_[:, h, :], i_[:, 0, h * 128:h * 128 + 128], False, True, inc=True)
                    v = cp(V, o_[:, t, f * 128:f * 128 + 512], PS[b][:, :], m)
                    free[b] = [v]
                yield
            junk = E[:, 0:4, :].rearrange("p f t -> p (f t)")
            rms_rows(o_, 1024, 6, junk, v)
            while not Z.get("ga done"):
                yield WAIT
            for t in range(2):
                v = stt(o_[:, t, :], o_[:, t, :], st[:, 6 + t:7 + t], tm_view("ga")[:, t, :], ALU.mult, ALU.mult)
                yield
            for f in range(0, 8, 2):
                b = bank("side")
                for j in range(2):
                    for t in range(2):
                        m = tr(PS[b][:, j * 256 + t * 128:j * 256 + t * 128 + 128], o_[:, t, (f + j) * 128:(f + j) * 128 + 128],
                               v, free[b], inc=True)
                for j in range(2):
                    k = act(Z["ga"][:, f + j, :], PS[b][:, j * 256:j * 256 + 256], ACT.Copy, m, scale=vcol("hg_norm_g_2", f + j))
                free[b] = [k]
                Z["ga tok"] = k
            yield

        g_h = chain(hgrn)
        beside(g_h)
        for n, ev in tm_copy("i", lambda: Z["i"]):
            tmslabs(w2, [(2048 + 512 * n, 512)], lambda kh, n=n, ev=ev: tm_out(f"i{n}", h_, kh, ev))
        do(lambda: Z.update({"i done": [V.last()]}))

        def scaled(key, t0, s):
            return lambda j0, p, m: act(Z[key][:, t0:t0 + 2, :], p, ACT.Copy, m, scale=s)
        for j in range(4):
            fmslab(w2, 4096 + 256 * j, 256, lambda j=j: fm_tiles(2, h_,
                                                                         scaled("qb", 2 * j, 1.0 / math.sqrt(128))))
        for j in range(4):
            fmslab(w2, 5120 + 256 * j, 256, lambda j=j: fm_tiles(2, h_, copy_fm(Z["kb"], 2 * j)))
        for n, ev in tm_copy("v", lambda: Z["vb"]):
            tmslabs(w2, [(6144 + 512 * n, 512)], lambda kh, n=n, ev=ev: tm_out(f"v{n}", h_, kh, ev))

        def fb_cols():
            def evac(j0, p, m):
                lf = Z["lf"]
                xx, t1, nc_ = lf[:, 0, :], lf[:, 1, :], lf[:, 2, :]
                k = act(xx, p[0:8, 0, :], ACT.Identity, m, bias=vec[0:8, VEC["fox_f_bias_2"][0]:VEC["fox_f_bias_2"][0] + 1])
                act(t1, xx, ACT.Abs)
                act(t1, t1, ACT.Exp, scale=-1.0)
                a = act(t1, t1, ACT.Ln, bias=C("one", 0, 1, rows=8))
                stt(xx, xx, 0.0, t1, ALU.min, ALU.subtract, a)
                V(lambda e: e.tensor_tensor_scan(nc_, C("one", rows=8), xx, 0.0, ALU.mult, ALU.add))
                ts(V, lf[:, 3, :], nc_, -1.0, None, ALU.mult, None)
                return k
            return fm_tiles(1, h_, evac)
        fmslab(w2, 7168, 128, fb_cols)
        def fox():
            def logits(h, t, o):
                n = 128 * (t + 1)
                mm(o, Z["qb"][:, h, t * 128:t * 128 + 128], Z["kb"][:, h, 0:n], True, False, Z["fox in"])
                return mm(o, Z["sel"][:, h, :], Z["lf"][:, 3, 0:n], False, True, inc=True)

            def mask(t):
                return C("causal") if t == 0 else con[:, CON["zero"][0]:CON["zero"][0] + 256]

            def outp(h, p, m):
                return cp(V, Z["qb"][:, h, :], p, m)
            yield Z["fox in"][0]
            yield from attention(Z["fox"], list(range(8)), logits, mask,
                                 lambda h, kt_: Z["vb"][:, kt_, h * 128:h * 128 + 128], (1, 2), outp)
        g_f = chain(fox)

        def tm_view(key, f0=0):
            return Z[key][:, f0:f0 + 8, :].rearrange("p f t -> p (f t)").rearrange("p (t n) -> p t n", t=2)

        def gate2(n):
            def evac(t, p, m):
                o = tm_gt()[:, t, 512 * n:512 * n + 512]
                v = tt(V, o, p, row[:, 512 * (n % 2):512 * (n % 2) + 512], ALU.add, m, row_tok[0])
                row_free[0] = [v]
                act(o, o, ACT.Sigmoid, v)
                return v
            tmslabs(w2, [(7176 + 512 * n, 512)], lambda kh: tm_out(f"gt{n}", h_, kh, evac))

        def tm_gt():
            return Z["gt"][:, :, :].rearrange("p f t -> p (f t)").rearrange("p (t n) -> p t n", t=2)
        do(lambda: Z.update({"fox in": [V.last(), A.last()]}))
        beside(g_h, g_f)
        for n in (0, 1):
            gate2(n)
        do(lambda: load_row("b_gate_2", 1024))
        def tm_silu(key, dst):
            for n in range(2):
                def evac(t, p, m, n=n):
                    o = dst()[:, t, n * 512:n * 512 + 512]
                    a = act(o, p, ACT.Sigmoid, m)
                    return tt(V, o, o, p, ALU.mult, a)
                yield n, evac
        for n, ev in tm_silu("ga", lambda: tm_view("ga")):
            tmslabs(w2, [(3072 + 512 * n, 512)], lambda kh, n=n, ev=ev: tm_out(f"ga{n}", h_, kh, ev))
        do(lambda: Z.update({"ga done": [V.last()]}))
        for n in (2, 3):
            gate2(n)
        do(lambda: load_row("mix_post_g_2"))
        finish(g_h)

        def end_hgrn():
            Z["H"].close()
            enter()
            F = Z["F"] = Scope()
            Z["oa"] = Ready(F("oahi", [P, 8, 256], F32R), F("oalo", [P, 8, 256], F32R))
            split_tiles(Z["oa"], Z["ga"], Z["ga tok"])
        do(end_hgrn)
        beside(g_f)
        branch("ba", I["w_branch_a_2"], lambda: Z["oa"], first_branch(tm_gt))
        finish(g_f)

        def split_b():
            split_tiles(Z["oa"], Z["qb"], V.last(), T.last())
            Z["mem"] = load(tm_view("kb"), I["mem_2"].rearrange("a (t p) d -> p (a t) d", p=P), s_misc, fence())
        do(split_b)

        ready_2 = {}
        g_t2 = chain(lambda: to_h(tm_gt, ready_2, lambda: g_t2))
        beside(g_t2)
        branch("bb", I["w_branch_b_2"], lambda: Z["oa"], second_branch(tm_gt, ready_2))
        do(lambda: advance_past(g_t2, 2))
        wout = I["w_out_2"].rearrange("a r n -> (a r) n")

        def post_slabs(w, key, lhs, yg, half=None):
            for n in range(2):
                tmslabs(w, [(512 * n, 512)], lambda kh, n=n: tm_out(
                    f"{key}{n}", lhs(), kh, lambda t, p, m: post_evac(tm_view(yg), t, n, p, m)), half if n == 0 else None)

        wkv = I["w_mkv_2"].rearrange("a r n -> (a r) n")
        wmq = I["w_mq_2"].rearrange("a r n -> (a r) n")
        wmo = I["w_mo_2"].rearrange("a r n -> (a r) n")

        def mem_norm():
            early_sqrt()
            yield
            yield from norm(tm_view("qb"), None, tm_view("kb"), "mem_kv_g_2", Z["mem"], Z["mem"], dst=Z["oa"])
        g_m = chain(mem_norm)
        beside(g_t2, g_m)
        post_slabs(wout, "wout", lambda: h_, "gt", half=g_t2)
        finish(g_m)

        def mix_end():
            for t in range(2):
                x_tok[t] = post(tm_view("gt"), t, False)
            yield
            load_row("mem_post_g_2")
            yield from norm(tm_view("gt"), None, x, "mem_pre_g_2", *x_tok)
        g_e = chain(mix_end)
        beside(g_e)
        for j in range(4):
            fmslab(wkv, 256 * j, 256, lambda j=j: fm_tiles(2, Z["oa"], copy_fm(Z["kb"], 2 * j)))
        finish(g_e)
        for j in range(4):
            fmslab(wmq, 256 * j, 256, lambda j=j: fm_tiles(2, h_, scaled("qb", 2 * j, 1.0 / 16)))

        def mem_attention():
            z = [Z["gt"][:, 4 * t:4 * t + 4, :] for t in range(2)]
            pt = Z["gt"][:, 8:16, :].rearrange("p (j k) t -> p j k t", k=2)
            red = Z["fox"][2]
            t0 = [V.last(), A.last()]
            for t in range(2):
                for h0 in (0, 2):
                    b = bank("side")
                    for j in range(2):
                        h = h0 + j
                        for d in range(2):
                            m = mm(PS[b][:, j * 256:j * 256 + 256], Z["qb"][:, 2 * h + d, t * 128:t * 128 + 128],
                                   Z["kb"][:, 2 * h + d, :], d == 0, d == 1, t0, free[b], inc=(d == 1))
                    free[b] = [cp(V, z[t][:, h0:h0 + 2, :], PS[b][:, :].rearrange("p (j k) -> p j k", j=2), m)]
                yield
            for t in range(2):
                mx, sm, rc = (red[:, t, q, :] for q in range(3))
                zt = z[t]
                v = V(lambda e, mx=mx, zt=zt: e.tensor_reduce(mx, zt[:, :, :], AX.X, ALU.max, negate=True), cost=0.8)
                for h in range(4):
                    a = act(zt[:, h, :], zt[:, h, :], ACT.Exp, v, bias=red[:, t, 0, h:h + 1], accum_out=red[:, t, 1, h:h + 1])
                recip(rc, sm, a)
                v = tt(V, zt[:, :, :], zt[:, :, :], rc.unsqueeze(2).broadcast_to([P, 4, 256]), ALU.mult)
                yield
                for h0 in (0, 2):
                    b = bank("side")
                    for j in range(2):
                        for k in range(2):
                            m = tr(PS[b][:, (2 * j + k) * 128:(2 * j + k) * 128 + 128], zt[:, h0 + j, k * 128:k * 128 + 128],
                                   v, free[b], inc=True)
                    c = cp(V, pt[:, h0:h0 + 2, :, t * 128:t * 128 + 128],
                           PS[b][:, :].rearrange("p (j k q) -> p j k q", j=2, k=2), m)
                    free[b] = [c]
            yield
            while not Z.get("v done"):
                yield WAIT
            for f in range(0, 8, 2):
                b = bank("side")
                for j in range(2):
                    for k in range(2):
                        m = mm(PS[b][:, j * 256:j * 256 + 256], Z["vb"][:, k, (f + j) * 128:(f + j) * 128 + 128],
                               pt[:, (f + j) // 2, k, :], k == 0, k == 1, c, Z["v done"], free[b], inc=(k == 1))
                i = PS[b][:, :].rearrange("p (j t) -> p j t", j=2)
                hi, lo = (q[:, f:f + 2, :] for q in Z["oa"].p)
                a = cp(A, hi, i, m)
                q = tt(V, lo, i, hi, ALU.subtract, a)
                Z["oa"].tok[f] = Z["oa"].tok[f + 1] = [a, q]
                free[b] = [q]
            early_sqrt()
        g_a = chain(mem_attention)
        beside(g_a)
        for n, ev in tm_copy("mv", lambda: Z["vb"]):
            tmslabs(wkv, [(1024 + 512 * n, 512)], lambda kh, n=n, ev=ev: tm_out(f"mv{n}", Z["oa"], kh, ev))
        do(lambda: Z.update({"v done": [V.last()]}))
        finish(g_a)
        post_slabs(wmo, "wmo", lambda: Z["oa"], "kb")

        def mem_end():
            for t in range(2):
                x_tok[t] = post(tm_view("kb"), t, False)
            Z["F"].close()
            Z["S"].close()
            enter()
        do(mem_end)

        ffn("2", I["ffn2_w_in_2"], I["ffn2_w_down_2"], "ffn2_pre_g_2", "ffn2_post_g_2")

        bias_dram = nc.dram_tensor("bias_scratch", (8, 384), F32, kind="Internal").ap()
        run_tasks()
        load.q.wait(t_out[0], (s_misc, load.count[s_misc.name]))

        block = ctx.enter_context(nc.Block())

        @block.sync
        def _(e):
            load.q.play(e)

        @block.vector
        def _(e):
            V.play(e)

        @block.scalar
        def _(e):
            A.play(e)

        @block.gpsimd
        def _(e):
            G.play(e)

        @block.tensor
        def _(e):
            T.play(e)


DIRECT = ["x", "ada_w", "ada_b", "b_gate_2", "w_in", "w2", "a2", "kv_norm_g", "w_uk", "w_uv", "w_pa", "w_pb", "w_o", "rel_bias",
          "final_g", "mem_2", "ffn1_w_in_2", "ffn1_w_down_2", "ffn1_post_g_2", "w_in_2", "w_branch_a_2",
          "w_branch_b_2", "w_out_2", "mix_post_g_2", "w_mq_2", "w_mkv_2", "w_mo_2", "mem_post_g_2",
          "ffn2_w_in_2", "ffn2_w_down_2", "ffn2_post_g_2"]


def kernel(**inputs):
    import concourse.bacc as bacc
    from concourse.bass_utils import run_bass_kernel_spmd

    arrays = {}
    for name in DIRECT:
        a = np.asarray(inputs[name])
        if name == "w_uk":
            a = a.reshape(128, 4, 128).transpose(2, 1, 0)
        arrays[name] = np.ascontiguousarray(a)
    vecs = np.zeros((P, NVEC), np.float32)
    for name, (o, w) in VEC.items():
        a = np.asarray(inputs[name]).reshape(-1)
        if name == "fox_f_bias_2":
            vecs[0:8, o] = a
        elif name == "shift_mu" or a.size == 128 * w:
            vecs[:, o:o + w] = a.reshape(w, 128).T
    arrays["vecs"] = vecs
    arrays["consts"] = constants()
    nc = bacc.Bacc("TRN2", target_bir_lowering=False, num_devices=1)
    aps = {n: nc.dram_tensor(f"in_{n}", a.shape, mybir.dt.from_np(a.dtype), kind="ExternalInput").ap()
           for n, a in arrays.items()}
    out = nc.dram_tensor("out_0", (1, 256, 1024), F32, kind="ExternalOutput").ap()
    program(nc, {n: aps[n] for n in DIRECT}, aps["consts"], aps["vecs"], out)
    r = run_bass_kernel_spmd(nc, [{f"in_{n}": a for n, a in arrays.items()}], core_ids=[0])
    return r.results[0]["out_0"]
```
